# Optimizing a Trainium2 kernel written in Bass

```python
import jax, jax.numpy as jnp
from jax import lax
import numpy as np

"""Hybrid decoder trunk: DEPTH pre-norm residual layers. Each layer runs three causal token mixers in parallel on the same RMS-normalised input: (A) an xLSTM mLSTM matrix memory in chunkwise-parallel form, (B) LongNet-style dilated sliding-window attention with three (window, dilation) head groups merged by their softmax denominators, and (C) cross-attention into fixed memory tokens. All three take their columns from ONE combined input projection; each branch is projected to D_MODEL and the branches are merged by per-channel sigmoid gates (from the same projection), then ONE output projection. The channel mixer alternates dense SwiGLU (even layers) and a top-2-of-8 expert SwiGLU (odd layers). One final RMSNorm.
Inputs: x (BATCH, SEQ, D_MODEL), mem (BATCH, N_MEM, D_MODEL), per-layer parameters. Output: (BATCH, SEQ, D_MODEL).
"""

D_MODEL = 1024
BATCH = 1
SEQ = 256
DEPTH = 2

EPS = 1e-6
N_MEM = 256
MLSTM_HEADS = 4
MLSTM_DH = 128
MLSTM_W = MLSTM_HEADS * MLSTM_DH
MLSTM_CHUNK = 128
CONV_W = 4
M_INIT = -1e30
DIL_PATTERNS = ((128, 1), (512, 4), (2048, 16))
DIL_HEADS_PER_GROUP = 4
DIL_DH = 64
DIL_W = 3 * DIL_HEADS_PER_GROUP * DIL_DH
DIL_OUT_W = DIL_HEADS_PER_GROUP * DIL_DH
Q_BLOCK = 128
MEM_HEADS = 4
MEM_DH = 128
MEM_W = MEM_HEADS * MEM_DH
N_BRANCH = 3
IN_SPLITS = (MLSTM_W, MLSTM_W, MLSTM_W, MLSTM_W, 2 * MLSTM_HEADS, DIL_W, DIL_W, DIL_W, MEM_W, N_BRANCH * D_MODEL)
IN_COLS = 4 * MLSTM_W + 2 * MLSTM_HEADS + 3 * DIL_W + MEM_W + N_BRANCH * D_MODEL
D_FF = 11 * D_MODEL // 4
N_EXPERTS = 8
TOP_K = 2
D_FF_EXPERT = 7 * D_MODEL // 2
MOE_TOKEN_BLOCK = 128
N_DENSE = (DEPTH + 1) // 2
N_MOE = DEPTH // 2

kernel_name = 'hybrid_mlstm_dilated_memory_moe'

def _rmsnorm(x, g):
    xf = x.astype(jnp.float32)
    y = xf * lax.rsqrt(jnp.mean(xf * xf, axis=-1, keepdims=True) + EPS)
    return (y * g.astype(jnp.float32)).astype(x.dtype)

def _headwise_layernorm(h, g):
    mu = jnp.mean(h, axis=-1, keepdims=True)
    var = jnp.mean(jnp.square(h - mu), axis=-1, keepdims=True)
    return (h - mu) * lax.rsqrt(var + EPS) * g.astype(jnp.float32).reshape(h.shape[-2], h.shape[-1])

def _causal_depthwise_conv(x, w):
    c = x.shape[-1]
    return lax.conv_general_dilated(x, w[:, None, :].astype(x.dtype), window_strides=(1,), padding=((CONV_W - 1, 0),), dimension_numbers=('NWC', 'WIO', 'NWC'), feature_group_count=c)

def _mlstm_chunkwise(q, k, v, i_pre, f_pre):
    b, s, h, dh = q.shape
    L = MLSTM_CHUNK
    nc = s // L
    k = k * (dh ** -0.5)
    log_f = jax.nn.log_sigmoid(f_pre)

    def seq_chunks(a):
        return a.reshape(b, nc, L, h, dh).transpose(1, 0, 3, 2, 4)

    def gate_chunks(a):
        return a.reshape(b, nc, L, h).transpose(1, 0, 3, 2)

    causal = jnp.tril(jnp.ones((L, L), dtype=bool))

    def step(carry, xs):
        c_state, n_state, m_state = carry
        qc, kc, vc, ic, lfc = xs
        cum = jnp.cumsum(lfc, axis=-1)
        d_mat = cum[..., :, None] - cum[..., None, :] + ic[..., None, :]
        d_mat = jnp.where(causal, d_mat, -jnp.inf)
        inter = cum + m_state[..., None]
        m_row = jnp.maximum(jnp.max(d_mat, axis=-1), inter)
        w_intra = jnp.exp(d_mat - m_row[..., None])
        w_inter = jnp.exp(inter - m_row)
        s_mat = jnp.einsum('bhld,bhjd->bhlj', qc, kc) * w_intra
        num = jnp.einsum('bhlj,bhjd->bhld', s_mat, vc) + w_inter[..., None] * jnp.einsum('bhvd,bhld->bhlv', c_state, qc)
        den = jnp.sum(s_mat, axis=-1) + w_inter * jnp.einsum('bhd,bhld->bhl', n_state, qc)
        h_out = num / jnp.maximum(jnp.abs(den), jnp.exp(-m_row))[..., None]
        total = cum[..., -1]
        g_end = total[..., None] - cum + ic
        m_new = jnp.maximum(total + m_state, jnp.max(g_end, axis=-1))
        w_end = jnp.exp(g_end - m_new[..., None])
        decay = jnp.exp(total + m_state - m_new)
        c_new = decay[..., None, None] * c_state + jnp.einsum('bhlv,bhld->bhvd', vc * w_end[..., None], kc)
        n_new = decay[..., None] * n_state + jnp.einsum('bhl,bhld->bhd', w_end, kc)
        return (c_new, n_new, m_new), h_out

    init = (jnp.zeros((b, h, dh, dh), jnp.float32), jnp.zeros((b, h, dh), jnp.float32), jnp.full((b, h), M_INIT, jnp.float32))
    _, hs = lax.scan(step, init, (seq_chunks(q), seq_chunks(k), seq_chunks(v), gate_chunks(i_pre), gate_chunks(log_f)))
    return hs.transpose(1, 0, 3, 2, 4).reshape(b, s, h, dh)

def _dilated_attention(q, k, v):
    b, s, _ = q.shape
    g_n = len(DIL_PATTERNS)
    hg, dh = DIL_HEADS_PER_GROUP, DIL_DH
    q = q.reshape(b, s, g_n, hg, dh)
    k = k.reshape(b, s, g_n, hg, dh)
    v = v.reshape(b, s, g_n, hg, dh)
    nb = s // Q_BLOCK
    q_blocks = q.reshape(b, nb, Q_BLOCK, g_n, hg, dh).transpose(1, 0, 2, 3, 4, 5)
    scale = dh ** -0.5

    def block(args):
        q_blk, start = args
        pos = start + jnp.arange(Q_BLOCK)
        outs, lses = [], []
        for g, (window, dil) in enumerate(DIL_PATTERNS):
            offs = jnp.arange(window // dil + 1) * dil
            idx = pos[:, None] - offs[None, :]
            valid = idx >= 0
            idx = jnp.maximum(idx, 0)
            kg = jnp.take(k[:, :, g], idx, axis=1)
            vg = jnp.take(v[:, :, g], idx, axis=1)
            sc = jnp.einsum('bqhd,bqjhd->bhqj', q_blk[:, :, g], kg) * scale
            sc = jnp.where(valid[None, None], sc, -jnp.inf)
            mx = jnp.max(sc, axis=-1, keepdims=True)
            p = jnp.exp(sc - mx)
            den = jnp.sum(p, axis=-1)
            o = jnp.einsum('bhqj,bqjhd->bqhd', p, vg) / den.transpose(0, 2, 1)[..., None]
            lse = (mx[..., 0] + jnp.log(den)).transpose(0, 2, 1)
            outs.append(o)
            lses.append(lse)
        o_all = jnp.stack(outs, axis=2)
        w = jax.nn.softmax(jnp.stack(lses, axis=2), axis=2)
        return jnp.einsum('bqgh,bqghd->bqhd', w, o_all)

    out = lax.map(block, (q_blocks, jnp.arange(nb) * Q_BLOCK))
    return out.transpose(1, 0, 2, 3, 4).reshape(b, s, hg * dh)

def _memory_attention(q, mem_n, w_kv):
    b, s, _ = q.shape
    kv = (mem_n @ w_kv).astype(jnp.float32)
    km, vm = jnp.split(kv, 2, axis=-1)
    km = km.reshape(b, -1, MEM_HEADS, MEM_DH)
    vm = vm.reshape(b, -1, MEM_HEADS, MEM_DH)
    qh = q.reshape(b, s, MEM_HEADS, MEM_DH)
    sc = jnp.einsum('bshd,bnhd->bhsn', qh, km) * (MEM_DH ** -0.5)
    p = jax.nn.softmax(sc, axis=-1)
    return jnp.einsum('bhsn,bnhd->bshd', p, vm).reshape(b, s, MEM_W)

def _swiglu(u, wg, wu, wd):
    return (jax.nn.silu(u @ wg) * (u @ wu)) @ wd

def _moe_swiglu(u, w_router, wg, wu, wd):
    b, s, d = u.shape
    ut = u.reshape(-1, d)
    t = ut.shape[0]
    probs = jax.nn.softmax((ut @ w_router).astype(jnp.float32), axis=-1)
    top_p, top_i = lax.top_k(probs, TOP_K)
    top_p = top_p / jnp.sum(top_p, axis=-1, keepdims=True)
    gates = jnp.sum(jax.nn.one_hot(top_i, N_EXPERTS, dtype=jnp.float32) * top_p[..., None], axis=1).astype(u.dtype)
    nblk = t // MOE_TOKEN_BLOCK

    def block(args):
        xb, gb = args
        h = jax.nn.silu(jnp.einsum('td,edf->tef', xb, wg)) * jnp.einsum('td,edf->tef', xb, wu)
        return jnp.einsum('tef,efd->td', h * gb[..., None], wd)

    y = lax.map(block, (ut.reshape(nblk, MOE_TOKEN_BLOCK, d), gates.reshape(nblk, MOE_TOKEN_BLOCK, N_EXPERTS)))
    return y.reshape(b, s, d)

def setup_inputs(seed: int = 0) -> dict:
    key = jax.random.key(seed)
    ks = jax.random.split(key, 24)

    def nrm(k, shape, scale):
        return jax.random.normal(k, shape, jnp.float32) * scale

    def gain(k, shape):
        return 1.0 + 0.02 * jax.random.normal(k, shape, jnp.float32)

    b_i = nrm(ks[4], (DEPTH, MLSTM_HEADS), 0.1)
    b_f = 3.0 + nrm(ks[5], (DEPTH, MLSTM_HEADS), 0.5)
    return {
        'x': nrm(ks[0], (BATCH, SEQ, D_MODEL), 1.0),
        'mem': nrm(ks[1], (BATCH, N_MEM, D_MODEL), 1.0),
        'norm_mix': gain(ks[2], (DEPTH, D_MODEL)),
        'w_in': nrm(ks[3], (DEPTH, D_MODEL, IN_COLS), D_MODEL ** -0.5),
        'conv_qk': nrm(ks[6], (DEPTH, CONV_W, 2 * MLSTM_W), CONV_W ** -0.5),
        'b_gate_if': jnp.concatenate([b_i, b_f], axis=-1),
        'mlstm_norm': gain(ks[7], (DEPTH, MLSTM_W)),
        'norm_mem': gain(ks[8], (DEPTH, D_MODEL)),
        'w_mem_kv': nrm(ks[9], (DEPTH, D_MODEL, 2 * MEM_W), D_MODEL ** -0.5),
        'w_br_m': nrm(ks[10], (DEPTH, MLSTM_W, D_MODEL), MLSTM_W ** -0.5),
        'w_br_d': nrm(ks[11], (DEPTH, DIL_OUT_W, D_MODEL), DIL_OUT_W ** -0.5),
        'w_br_x': nrm(ks[12], (DEPTH, MEM_W, D_MODEL), MEM_W ** -0.5),
        'w_out': nrm(ks[13], (DEPTH, D_MODEL, D_MODEL), D_MODEL ** -0.5),
        'norm_ffn': gain(ks[14], (DEPTH, D_MODEL)),
        'ffn_w_gate': nrm(ks[15], (N_DENSE, D_MODEL, D_FF), D_MODEL ** -0.5),
        'ffn_w_up': nrm(ks[16], (N_DENSE, D_MODEL, D_FF), D_MODEL ** -0.5),
        'ffn_w_down': nrm(ks[17], (N_DENSE, D_FF, D_MODEL), D_FF ** -0.5),
        'moe_router': nrm(ks[18], (N_MOE, D_MODEL, N_EXPERTS), D_MODEL ** -0.5),
        'moe_w_gate': nrm(ks[19], (N_MOE, N_EXPERTS, D_MODEL, D_FF_EXPERT), D_MODEL ** -0.5),
        'moe_w_up': nrm(ks[20], (N_MOE, N_EXPERTS, D_MODEL, D_FF_EXPERT), D_MODEL ** -0.5),
        'moe_w_down': nrm(ks[21], (N_MOE, N_EXPERTS, D_FF_EXPERT, D_MODEL), D_FF_EXPERT ** -0.5),
        'norm_final': gain(ks[22], (D_MODEL,)),
    }

def reference(x, mem, norm_mix, w_in, conv_qk, b_gate_if, mlstm_norm, norm_mem, w_mem_kv, w_br_m, w_br_d, w_br_x, w_out, norm_ffn, ffn_w_gate, ffn_w_up, ffn_w_down, moe_router, moe_w_gate, moe_w_up, moe_w_down, norm_final):
    b, s, _ = x.shape
    split_points = [int(p) for p in np.cumsum(IN_SPLITS)[:-1]]
    for layer in range(DEPTH):
        u = _rmsnorm(x, norm_mix[layer])
        proj = u @ w_in[layer]
        q_m, k_m, v_m, o_m, if_m, q_d, k_d, v_d, q_x, gate_pre = jnp.split(proj, split_points, axis=-1)
        qk = jax.nn.silu(_causal_depthwise_conv(jnp.concatenate([q_m, k_m], axis=-1), conv_qk[layer]))
        q_m, k_m = jnp.split(qk, 2, axis=-1)
        if_pre = (if_m + b_gate_if[layer]).astype(jnp.float32)
        h_m = _mlstm_chunkwise(q_m.astype(jnp.float32).reshape(b, s, MLSTM_HEADS, MLSTM_DH), k_m.astype(jnp.float32).reshape(b, s, MLSTM_HEADS, MLSTM_DH), v_m.astype(jnp.float32).reshape(b, s, MLSTM_HEADS, MLSTM_DH), if_pre[..., :MLSTM_HEADS], if_pre[..., MLSTM_HEADS:])
        h_m = (_headwise_layernorm(h_m, mlstm_norm[layer]).reshape(b, s, MLSTM_W) * jax.nn.sigmoid(o_m.astype(jnp.float32))).astype(x.dtype)
        h_d = _dilated_attention(q_d.astype(jnp.float32), k_d.astype(jnp.float32), v_d.astype(jnp.float32)).astype(x.dtype)
        mem_n = _rmsnorm(mem, norm_mem[layer])
        h_x = _memory_attention(q_x.astype(jnp.float32), mem_n, w_mem_kv[layer]).astype(x.dtype)
        g_m, g_d, g_x = jnp.split(jax.nn.sigmoid(gate_pre), N_BRANCH, axis=-1)
        merged = g_m * (h_m @ w_br_m[layer]) + g_d * (h_d @ w_br_d[layer]) + g_x * (h_x @ w_br_x[layer])
        x = x + merged @ w_out[layer]
        u = _rmsnorm(x, norm_ffn[layer])
        if layer % 2 == 0:
            x = x + _swiglu(u, ffn_w_gate[layer // 2], ffn_w_up[layer // 2], ffn_w_down[layer // 2])
        else:
            x = x + _moe_swiglu(u, moe_router[layer // 2], moe_w_gate[layer // 2], moe_w_up[layer // 2], moe_w_down[layer // 2])
    return _rmsnorm(x, norm_final)


_drawn_inputs = setup_inputs


def setup_inputs(seed=0):
    import zlib

    import numpy as np

    out = dict(_drawn_inputs(seed))
    spreads = {}
    factors = {'mlstm_norm': 14.449, 'norm_mem': 8.0, 'norm_final': 7.981, 'norm_ffn': 4.315}
    for name, (base, spread) in spreads.items():
        noise = np.random.default_rng([zlib.crc32(name.encode()), seed]).standard_normal(out[name].shape)
        drawn = base * np.exp(spread * noise) if base else spread * noise
        out[name] = __import__('jax').numpy.asarray(drawn.astype(out[name].dtype))
    for name, factor in factors.items():
        out[name] = (out[name] * factor).astype(out[name].dtype)
    return out
```

```python
import concourse.bass as bass
from concourse import mybir
from contextlib import ExitStack


def hybrid_trunk(nc: bass.Bass, x_in, mem_in, norm_mix, w_in, conv_qk, b_gate_if, mlstm_norm, norm_mem,
                 w_mem_kv, w_br_m, w_br_d, w_br_x, w_out, norm_ffn, ffn_w_gate, ffn_w_up, ffn_w_down,
                 moe_router, moe_w_gate, moe_w_up, moe_w_down, norm_final, out):
    f32, f32r, i32 = mybir.dt.float32, mybir.dt.float32r, mybir.dt.int32
    ALU, ACT, AX = mybir.AluOpType, mybir.ActivationFunctionType, mybir.AxisListType

    P = 128
    S, D = x_in.shape[1], x_in.shape[2]
    L = w_in.shape[0]
    TT, KT = S // P, D // P
    NM = mem_in.shape[1]
    MH, MD = 4, 128
    MW = MH * MD
    XH, XD = 4, 128
    XW = XH * XD
    DG, DHG, DD = 3, 4, 64
    DW = DG * DHG * DD
    E = moe_router.shape[2]
    FF = ffn_w_gate.shape[2]
    FE = moe_w_gate.shape[3]
    EPS, NEG = 1e-6, -1e30
    assert TT == 2 and NM == S and MD == P and XD == P and E == 8

    C_QM, C_KM, C_VM, C_OM = 0, MW, 2 * MW, 3 * MW
    C_IF = 4 * MW
    C_QD = C_IF + 2 * MH
    C_VD = C_QD + 2 * DW
    C_QX = C_VD + DW
    C_G = C_QX + XW

    CH = 2048
    UC = CH // KT
    RAW, SPL = 3, 3
    MRAW = 6
    HC = 512

    def rows(w, k0, nk, c0, nc_):
        return w[k0 * P:(k0 + nk) * P, c0:c0 + nc_].rearrange("(t p) n -> p t n", p=P)

    chunks = []

    def chunk(w, k0, nk, c0, n):
        chunks.append((rows(w, k0, nk, c0, n), nk, n))
        return len(chunks) - 1

    plan = []

    def mixer_plan(l):
        mem = w_mem_kv[l]
        plan.append(("norm", dict(n=3 * l, src="mem")))
        for i in range(XW // UC):
            plan.append(("unit", dict(c=chunk(mem, 0, KT, i * UC, UC), form="F", to=("km", i), l=l, ex=[])))
        for i in range(XW // UC):
            plan.append(("unit", dict(c=chunk(mem, 0, KT, XW + i * UC, UC), form="T", to=("vm", i), l=l, ex=[])))
        plan.append(("norm", dict(n=3 * l + 1, src="x")))
        w = w_in[l]
        units = []

        def add(kind, c0, width, form):
            for i in range(width // UC):
                units.append((c0 + i * UC, UC, form, (kind, i)))

        add("qx", C_QX, XW, "F")
        units.append((C_IF, 2 * MH, "T", ("if", 0)))
        add("qm", C_QM, MW, "F")
        add("km2", C_KM, MW, "F")
        add("vml", C_VM, MW, "T")
        add("qd", C_QD, DW, "F")
        add("kd", C_QD + DW, DW, "F")
        add("vd", C_VD, DW, "T")
        add("om", C_OM, MW, "T")
        add("g", C_G, 3 * D, "T")
        extras = {
            2: [("memA", 0)], 3: [("memC", 0), ("memA", 1)],
            4: [("conv", 0), ("memE", 0), ("memC", 1), ("memA", 2)],
            5: [("conv", 1), ("memE", 1), ("memC", 2), ("memA", 3)],
            6: [("conv", 2), ("memE", 2), ("memC", 3)],
            7: [("conv", 3), ("memE", 3)],
            8: [("cum", 0)], 9: [("brow", 0)], 10: [("mrow", 0)],
            12: [("mlA", 0)], 13: [("mlA", 1), ("mlE", 0)], 14: [("mlA", 2), ("mlE", 1)],
            15: [("mlA", 3), ("mlE", 2)], 16: [("mlE", 3)],
            18: [("dS", 0)], 19: [("dR", 0)],
            20: [("mlF", 0), ("dT", 0), ("dS", 1)], 21: [("dE", 0), ("dR", 1)],
            22: [("dT", 1), ("dS", 2)], 23: [("dE", 1), ("dR", 2)],
            24: [("dT", 2), ("dS", 3)], 25: [("dE", 2), ("dR", 3)],
            26: [("dT", 3)], 27: [("dE", 3)],
            28: [("ht", 0)], 29: [("ht", 1)], 30: [("ht", 2)], 31: [("ht", 3), ("ht", 4)],
        }
        for s, (c0, n, form, to) in enumerate(units):
            plan.append(("unit", dict(c=chunk(w, 0, KT, c0, n), form=form, to=to, l=l, ex=extras.pop(s, []))))
        assert not extras
        for b, (wb, kt) in enumerate(((w_br_m[l], MW // P), (w_br_d[l], DHG * DD // P), (w_br_x[l], XW // P))):
            if kt * D <= CH:
                c = chunk(wb, 0, kt, 0, D)
                plan.append(("branch", dict(c=c, b=b, kt=kt, halves=(0, 1), l=l)))
            else:
                for h in range(2):
                    plan.append(("branch", dict(c=chunk(wb, 0, kt, h * HC, HC), b=b, kt=kt, halves=(h,), l=l)))
        plan.append(("merged", dict(l=l)))
        for h in range(2):
            for q in range(2):
                plan.append(("outproj", dict(c=chunk(w_out[l], 4 * q, 4, h * HC, HC), h=h, q=q, l=l)))
        plan.append(("norm", dict(n=3 * l + 2, src="x")))

    NP_ = FF // UC

    mixer_plan(0)
    for p in range(NP_ + 1):
        if p < NP_:
            plan.append(("gate", dict(c=chunk(ffn_w_gate[0], 0, KT, p * UC, UC), p=p)))
            plan.append(("up", dict(c=chunk(ffn_w_up[0], 0, KT, p * UC, UC), p=p)))
        if p:
            plan.append(("down", dict(c=chunk(ffn_w_down[0], 2 * (p - 1), 2, 0, D), p=p - 1)))
    plan.append(("ffn_end", {}))
    mixer_plan(1)
    plan.append(("unit", dict(c=chunk(moe_router[0], 0, KT, 0, E), form="T", to=("route", 0), l=1, ex=[])))
    NDC = len(chunks)

    NJ = FE // HC
    moe_chunks = []
    for j in range(NJ):
        moe_chunks += [("g", j, 0), ("g", j, 1), ("u", j, 0), ("u", j, 1)]
        if j:
            moe_chunks += [("d", j - 1, 0), ("d", j - 1, 1)]
    moe_chunks += [("d", NJ - 1, 0), ("d", NJ - 1, 1)]
    EC = len(moe_chunks)
    assert EC % MRAW == 0 and EC % SPL == 0

    ctx = ExitStack()
    with ctx:
        base = (nc.sbuf_base + 31) // 32 * 32
        top = [base]

        def at(name, shape, dt=f32, off=None):
            size = 4
            for n in shape[1:]:
                size *= n
            if off is None:
                off = top[0]
                top[0] += (size + 31) // 32 * 32
            return nc.alloc_sbuf_tensor_at(name, shape, dt, offset=off)

        raw = [at(f"raw{i}", [P, CH]) for i in range(RAW)]
        whi = at("w_hi", [P, SPL, CH], f32r)
        wlo = at("w_lo", [P, SPL, CH], f32r)
        xthi = at("xT_hi", [P, KT, S], f32r)
        xtlo = at("xT_lo", [P, KT, S], f32r)
        o_x = top[0]
        x = at("x", [P, TT, D])
        xn = at("x_normed", [P, TT, D])
        gain = at("gain", [P, D])
        g0 = top[0]
        gates = at("gates", [P, 3, TT, D])
        CW = S + 4
        convx = at("conv_x", [P, 2, 2, CW], off=g0)
        convy = at("conv_y", [P, 2, 2 * S], off=g0 + 4160)
        convt = at("conv_t", [P, 2, 2 * S], off=g0 + 8256)
        diag = at("diag", [P, TT, MH, P], off=g0 + 12352)
        wml = at("mlstm_w", [P, MH, 3 * P], off=g0 + 16448)
        raw_moe = raw + [at(f"raw{i}", [P, CH], off=g0 + (i - RAW) * CH * 4) for i in range(RAW, MRAW)]
        r1 = top[0]
        qk = at("qk_mT", [P, 2 * MH, S])
        hmT = [at("hmT_hi", [P, 4, S], f32r, off=r1), at("hmT_lo", [P, 4, S], f32r, off=r1 + 4 * S * 4)]
        r2 = top[0]
        qd = at("q_dT", [P, DW // P, S])
        kd = at("k_dT", [P, DW // P, S])
        qx = at("q_xT", [P, XH, S], off=r2)
        kmT = at("k_memT", [P, XH, NM], off=r2 + 4096)
        vm = at("v_mem", [P, TT, XW], off=r2 + 8192)
        hxT = [at("hxT_hi", [P, 4, S], f32r, off=r2), at("hxT_lo", [P, 4, S], f32r, off=r2 + 4096)]
        hdT = [at("hdT_hi", [P, 2, S], f32r, off=r2 + 8192), at("hdT_lo", [P, 2, S], f32r, off=r2 + 8192 + 2048)]
        VA = MD + 2
        vaug = at("v_aug", [P, TT, MH, VA])
        so = at("sig_o", [P, TT, MW])
        vd = at("v_d", [P, TT, DW])
        probs = at("probs", [P, 2, 3, 3 * P])
        probsT = at("probsT", [P, 3, 3 * P])
        hraw = at("h_raw", [P, TT, MH, MD])
        o_xn = o_x + TT * D * 4
        hm = at("h_m", [P, TT, MW], off=o_xn)
        hx = at("h_x", [P, TT, XW], off=o_xn + TT * MW * 4)
        hd = at("h_d", [P, TT, DHG * DD], off=o_xn + TT * D * 4)
        merged = at("merged", [P, TT, D], off=o_xn)
        o = r1
        sg = at("silu_g", [P, 2, HC], off=o); o += 4096
        hh = at("hidden", [P, 2, HC], off=o); o += 4096
        hThi = at("hiddenT_hi", [P, 2, 4 * P], f32r, off=o); o += 4096
        hTlo = at("hiddenT_lo", [P, 2, 4 * P], f32r, off=o); o += 4096
        xehi = at("xe_hi", [P, KT, P], f32r, off=o); o += 4096
        xelo = at("xe_lo", [P, KT, P], f32r, off=o); o += 4096
        ye = at("y_e", [P, D], off=o); o += 4096
        pick = at("pick", [P, TT, P], off=o); o += 1024
        pickg = at("pick_gated", [P, TT, P], off=o); o += 1024
        put = at("put", [P, TT, P], off=o); o += 1024
        assert o <= r1 + 52 * 1024
        dmask = at("dil_mask", [P, DG, 3 * P])
        maskT = at("causal_maskT", [P, P])
        ident = at("ident", [P, P])
        ones = at("ones", [P, P])
        upper = at("upper", [P, P])
        upper_s = at("upper_strict", [P, P])
        slots = at("slots", [P, 2, P])
        resid = at("residue", [P, 2, P])
        diff = at("diff", [P, P], i32, off=g0)
        diffm = at("diff_masked", [P, 2, P], i32, off=g0 + 512)
        cwn = at("conv_rows", [L * 4 * 8, P], off=g0 + 2048)
        cw = at("conv_w", [P, L * 4 * 8])
        bif = at("b_if", [P, L, 2 * MH])
        mln = at("mlstm_gain", [P, MW])
        ss = at("sum_sq", [P, TT])
        var = at("var", [P, TT])
        lnv = at("ln_v", [P, TT])
        r0 = at("rstd0", [P, TT])
        nt = at("newton", [P, TT])
        rstd = at("rstd", [P, TT])
        ifr = at("if_raw", [P, TT, 2 * MH])
        ifb = at("if_pre", [P, TT, 2 * MH])
        nab = at("neg_abs_f", [P, TT, MH])
        ef = at("exp_f", [P, TT, MH])
        lf = at("log_f", [P, TT, MH])
        cumf = at("cum_f", [P, TT, MH])
        bb = at("b", [P, TT, MH])
        mm_ = at("m_minus_f", [P, TT, MH])
        m2 = at("m2", [P, 2, MH])
        ngm = at("neg_m", [P, TT, MH])
        fm = at("m_row", [P, TT, MH])
        em = at("exp_neg_m", [P, TT, MH])
        den = at("den", [P, 2, 2])
        dn = at("den_abs", [P, 2])
        rec = at("rec", [P, 2])
        mx = at("row_max", [P, 2, 2])
        nb = at("neg_max", [P, 2, 2])
        st = at("bn", [P, 6])
        mv = at("mean_var", [P, TT * MH, 2])
        lv8 = at("ln_v8", [P, TT * MH])
        r8 = at("rstd8_0", [P, TT * MH])
        v8 = at("var8", [P, TT * MH])
        n8 = at("newton8", [P, TT * MH])
        lg = at("logits", [P, TT, E])
        m1 = at("top1", [P, TT])
        gt = at("greater", [P, E, E])
        eq = at("equal", [P, E, E])
        lt = at("earlier", [P, E, E])
        cnt = at("rank", [P, TT, E])
        sel = at("selected", [P, TT, E])
        eg = at("exp_logits", [P, TT, E])
        dg = at("gate_den", [P, TT])
        posm = at("position", [P, TT, E])
        tot = at("expert_tokens", [P, E])
        tmx = at("most_tokens", [P, 1])
        tab = at("route_table", [P, E + 1, 4])
        cur = at("route_now", [P, 4])
        flag = at("overflow", [P, 1], i32)
        assert top[0] <= nc.sbuf_usable_end, (top[0], nc.sbuf_usable_end)

        ps = nc.alloc_psum_tensor("ps", [P, 8, HC], f32)

        def sem(name):
            return ctx.enter_context(nc.semaphore(name))

        raw_loaded = [sem(f"raw_loaded{i}") for i in range(RAW)]
        moe_loaded = [sem(f"moe_loaded{i}") for i in range(MRAW)]
        hi_done, lo_done, chunk_used = sem("hi_done"), sem("lo_done"), sem("chunk_used")
        consts_loaded, consts_made, masks_made = sem("consts_loaded"), sem("consts_made"), sem("masks_made")
        cw_psum, cw_ready = sem("conv_w_psum"), sem("conv_w_ready")
        x_loaded, mem_loaded, gain_loaded, mln_loaded = sem("x_loaded"), sem("mem_loaded"), sem("gain_loaded"), sem("mlstm_gain_loaded")
        vars_, rstd0, normed = sem("variances"), sem("rstd0_ready"), sem("normed")
        tr_psum, tr_hi, tr_lo = sem("transposed"), sem("transposed_hi"), sem("transposed_lo")
        unit_done, unit_act, unit_dve = sem("unit_done"), sem("unit_read_act"), sem("unit_read_dve")
        conv_acc, conv_tanh, conv_done = sem("conv_acc"), sem("conv_tanh"), sem("conv_done")
        gate_done = sem("gates_done")
        if_neg, if_ln, logf = sem("neg_abs_ready"), sem("softplus_ready"), sem("log_f_ready")
        cum_psum, diag_ready, rows_psum, rows_read = sem("cum_psum"), sem("diag_ready"), sem("rows_psum"), sem("rows_read")
        em_in, em_ready, wml_ready = sem("m_row_ready"), sem("exp_neg_m_ready"), sem("mlstm_w_ready")
        s_mem, s_ml, s_d = sem("mem_scores"), sem("mlstm_scores"), sem("dil_scores")
        max_mem, max_d, d_masked = sem("mem_max"), sem("dil_max"), sem("dil_masked")
        p_mem, p_d, sw_ml = sem("mem_probs"), sem("dil_probs"), sem("mlstm_weighted")
        pt_psum, pt_ready = sem("probsT_psum"), sem("probsT_ready")
        mix_psum, mix_read = sem("mix_psum"), sem("mix_read")
        ml_var, ml_rstd, hm_ready = sem("mlstm_var"), sem("mlstm_rstd"), sem("h_m_ready")
        act_seq, dve_seq, pool_seq = sem("act_seq"), sem("dve_seq"), sem("pool_seq")
        merged_ready = sem("merged_ready")
        m_cur = sem("moe_route_now")
        silu_done, hid_done, hid_hi, hid_lo, y_read = sem("silu_done"), sem("hidden_done"), sem("hidden_hi"), sem("hidden_lo"), sem("y_read")
        route_exp, route_sel, route_pos, flag_ready = (sem(n) for n in ("route_exp", "route_selected", "route_pos", "flag_ready"))
        m_silu, m_hid, m_tp, m_thi, m_tlo = (sem("moe_" + n) for n in ("silu", "hidden", "hiddenT_psum", "hiddenT_hi", "hiddenT_lo"))
        m_pick, m_gath, m_xehi, m_xelo, m_putp, m_put, m_y, m_scat, m_added = (sem("moe_" + n) for n in ("pick", "gathered", "xe_hi", "xe_lo", "put_psum", "put", "y", "scattered", "added"))
        out_stored = sem("out_stored")

        gunits = []
        for kind, a in plan:
            if kind == "unit":
                a["u"] = len(gunits)
                gunits.append("act")
            elif kind == "branch":
                a["u"] = len(gunits)
                gunits += ["dve"] * (TT * len(a["halves"]))
            elif kind == "outproj" and a["q"] == 0:
                a["u"] = len(gunits)
                gunits += ["dve"] * TT
            elif kind == "outproj":
                a["u"] = len(gunits) - TT

        product, n_unit_done = {}, 0
        for kind, a in plan:
            if kind == "unit":
                product[a["u"]] = (chunk_used, a["c"] + 1)
            elif kind == "branch" or (kind == "outproj" and a["q"] == 1):
                m = TT * len(a.get("halves", (0,)))
                for i in range(m - 1):
                    n_unit_done += 1
                    product[a["u"] + i] = (unit_done, n_unit_done)
                product[a["u"] + m - 1] = (chunk_used, a["c"] + 1)

        chunk_of = {(kind, a["p"]): a["c"] for kind, a in plan if kind in ("gate", "up", "down")}

        def read_count(u):
            return sum(g == gunits[u] for g in gunits[:u + 1])

        def wait_bank(eng, u):
            if u >= 2:
                eng.wait_ge(unit_act if gunits[u - 2] == "act" else unit_dve, read_count(u - 2))

        n_tr = 0
        for kind, a in plan:
            if kind == "norm":
                a["tr"] = n_tr
                n_tr += KT // 2
            elif kind == "merged":
                a["tr"] = n_tr
                n_tr += KT // 2
            elif kind == "unit":
                for name, i in a["ex"]:
                    if name == "ht":
                        a.setdefault("tr", {})[i] = n_tr
                        n_tr += 1

        def view(t, n, kt):
            return t[:, 0:n * kt].rearrange("p (k n) -> p k n", k=kt)

        norms = [(3 * l + i, g[l]) for l in range(L) for i, g in enumerate((norm_mem, norm_mix, norm_ffn))] + [(3 * L, norm_final)]

        def ht_src(i):
            if i < 2:
                return hx, [2 * i, 2 * i + 1], hxT, 2 * i
            if i < 4:
                return hm, [2 * i - 4, 2 * i - 3], hmT, 2 * i - 4
            return hd, [0, 1], hdT, 0

        block = ctx.enter_context(nc.Block())

        def evac(l, kind, i=None):
            found = [a["u"] for k_, a in plan if k_ == "unit" and a["l"] == l and a["to"][0] == kind
                     and (i is None or a["to"][1] == i)]
            return read_count(found[-1])

        tr_norm = {a["n"]: a["tr"] for k_, a in plan if k_ == "norm"}
        tr_merged = [a["tr"] for k_, a in plan if k_ == "merged"]
        used_before = {}
        seen = 0
        for k_, a in plan:
            if k_ in ("norm", "merged"):
                used_before[a["tr"]] = seen
            seen += "c" in a

        def bcast(ap, shape):
            return ap.broadcast_to(shape)

        slots_mem = 2 * MH
        mixes = XH + MH + DHG

        @block.sync
        def _(eng):
            for c, (src, kt, n) in enumerate(chunks):
                if c >= RAW:
                    eng.wait_ge(lo_done, c - RAW + 1)
                eng.dma_start(view(raw[c % RAW], n, kt), src).then_inc(raw_loaded[c % RAW], 16)
            eng.wait_ge(lo_done, NDC)
            eng.wait_ge(merged_ready, 4 * L)

            def experts(r):
                with eng.Fori(0, E) as e:
                    for k, (kind, j, part) in enumerate(moe_chunks):
                        eng.wait_ge(lo_done, e * EC + (NDC + r * E * EC + k - MRAW + 1))
                        w = {"g": moe_w_gate, "u": moe_w_up, "d": moe_w_down}[kind][0][bass.ds(e, 1)]
                        if kind == "d":
                            k0 = 4 * j + 2 * part
                            src = w[:, k0 * P:(k0 + 2) * P, 0:D]
                            dst = view(raw_moe[k % MRAW], D, 2)
                        else:
                            src = w[:, 4 * part * P:4 * (part + 1) * P, j * HC:(j + 1) * HC]
                            dst = view(raw_moe[k % MRAW], HC, 4)
                        eng.dma_start(dst, src.rearrange("e (t p) n -> p (e t) n", p=P))\
                           .then_inc(moe_loaded[k % MRAW], 16)

            experts(0)
            eng.wait_ge(flag_ready, 1)
            over = eng.value_load(flag[0:1, 0:1], min_val=0, max_val=1)
            with eng.If(over > 0):
                experts(1)
            eng.wait_ge(normed, TT * (3 * L + 1))
            for t in range(TT):
                eng.dma_start(out[0, t * P:(t + 1) * P, :], xn[:, t, :]).then_inc(out_stored, 16)
            eng.wait_ge(out_stored, 16 * TT)

        @block.gpsimd
        def _(eng):
            n = [0]

            def link(ins):
                n[0] += 1
                ins.then_inc(pool_seq, 1)
                eng.wait_ge(pool_seq, n[0])

            eng.dma_start(x[:, :, :], x_in[0].rearrange("(t p) n -> p t n", p=P)).then_inc(x_loaded, 16)
            eng.dma_start(cwn[:, :], conv_qk.rearrange("l j (c p) -> (l j c) p", p=P)).then_inc(consts_loaded, 16)
            eng.dma_start(bif[:, :, :].rearrange("p l n -> p (l n)"),
                          b_gate_if.rearrange("l n -> (l n)").partition_broadcast(P)).then_inc(consts_loaded, 16)
            link(eng.memset(ones[:, :], 1.0))
            link(eng.memset(maskT[:, :], 0.0))

            def select(dst, src, op, fill, base, pattern, cm):
                link(eng.affine_select(out=dst, in_=src, compare_op=op, fill=fill, base=base, pattern=pattern,
                                       channel_multiplier=cm))

            select(ident[:, :], ones[:, :], ALU.is_equal, 0.0, 0, [[-1, P]], 1)
            select(upper[:, :], ones[:, :], ALU.is_ge, 0.0, 0, [[1, P]], -1)
            select(upper_s[:, :], ones[:, :], ALU.is_ge, 0.0, -1, [[1, P]], -1)
            select(dmask[:, 0, 0:P], maskT[:, :], ALU.is_ge, NEG, 0, [[-1, P]], 1)
            select(dmask[:, 0, 2 * P:3 * P], maskT[:, :], ALU.is_ge, NEG, 0, [[-1, P]], 1)
            select(dmask[:, 0, P:2 * P], maskT[:, :], ALU.is_ge, NEG, 0, [[1, P]], -1)
            select(maskT[:, :], maskT[:, :], ALU.is_ge, NEG, 0, [[1, P]], -1)
            select(lt[:, :, :], ones[:, 0:E * E].rearrange("p (a b) -> p a b", a=E), ALU.is_ge, 0.0, -1,
                   [[1, E], [-1, E]], 0)
            link(eng.iota(slots[:, :, :], [[P, 2], [1, P]], base=0, channel_multiplier=0,
                          allow_small_or_imprecise_dtypes=True))
            link(eng.iota(diff[:, :], [[-1, P]], base=0, channel_multiplier=1))
            link(eng.memset(vaug[:, :, :, MD:MD + 1], 1.0))
            link(eng.memset(vaug[:, :, :, MD + 1:VA], 0.0))
            eng.memset(tab[:, E, :], 1e6).then_inc(consts_made, 1)
            eng.wait_ge(masks_made, 1)
            for g in range(1, DG):
                select(dmask[:, g, 0:P], resid[:, g - 1, :], ALU.is_ge, NEG, 0, [[-1, P]], 1)
                select(dmask[:, g, 2 * P:3 * P], resid[:, g - 1, :], ALU.is_ge, NEG, 0, [[-1, P]], 1)
                last = eng.tensor_copy(dmask[:, g, P:2 * P], resid[:, g - 1, :])
                if g < DG - 1:
                    link(last)
            last.then_inc(consts_made, 1)
            for n_, g in norms:
                if n_:
                    eng.wait_ge(normed, TT * n_)
                if n_ % 3 == 2:
                    eng.wait_ge(tr_psum, tr_merged[n_ // 3])
                eng.dma_start(gain[:, :], g.partition_broadcast(P)).then_inc(gain_loaded, 16)
                if n_ % 3 == 0 and n_ < 3 * L:
                    l = n_ // 3
                    if l:
                        eng.wait_ge(tr_psum, tr_norm[n_])
                        eng.wait_ge(hm_ready, l)
                    eng.dma_start(xn[:, :, :], mem_in[0].rearrange("(t p) n -> p t n", p=P)).then_inc(mem_loaded, 16)
                    eng.dma_start(mln[:, :], mlstm_norm[l].partition_broadcast(P)).then_inc(mln_loaded, 16)

        @block.scalar
        def _(eng):
            n = [0]

            def link(ins):
                n[0] += 1
                ins.then_inc(act_seq, 1)
                eng.wait_ge(act_seq, n[0])

            def act(dst, src, func=ACT.Copy, **kw):
                return eng.activation(dst, src, func, **kw)

            def split_hi(c):
                if c >= NDC:
                    return
                kt, n_ = chunks[c][1:]
                eng.wait_ge(raw_loaded[c % RAW], 16 * (c // RAW + 1))
                if c >= SPL:
                    eng.wait_ge(chunk_used, c - SPL + 1)
                act(whi[:, c % SPL, 0:kt * n_], raw[c % RAW][:, 0:kt * n_]).then_inc(hi_done, 1)

            def transposed_hi(tr, dst):
                eng.wait_ge(tr_psum, tr + 1)
                act(dst, ps[:, 5 + tr % 2, :]).then_inc(tr_hi, 1)

            def norm(a):
                eng.wait_ge(vars_, a["n"] + 1)
                link(act(lnv[:, :], var[:, :], ACT.Ln))
                act(r0[:, :], lnv[:, :], ACT.Exp, scale=-0.5).then_inc(rstd0, 1)
                if a["n"] < 3 * L:
                    xt(a["tr"])

            def xt(tr):
                if used_before[tr]:
                    eng.wait_ge(chunk_used, used_before[tr])
                for q in range(KT // 2):
                    transposed_hi(tr + q, xthi[:, 2 * q:2 * q + 2, :].rearrange("p k s -> p (k s)"))

            def unit(a):
                (kind, i), l, u = a["to"], a["l"], a["u"]
                eng.wait_ge(*product[u])
                src = ps[:, u % 2, :]
                fm2 = src.rearrange("p (f s) -> p f s", f=2)
                cols = slice(i * UC, (i + 1) * UC)
                if kind in ("km", "qx", "qd", "kd"):
                    dst = {"km": kmT, "qx": qx, "qd": qd, "kd": kd}[kind]
                    act(dst[:, 2 * i:2 * i + 2, :], fm2).then_inc(unit_act, 1)
                elif kind in ("vm", "vd"):
                    act({"vm": vm, "vd": vd}[kind][:, :, cols], fm2).then_inc(unit_act, 1)
                elif kind == "vml":
                    act(vaug[:, :, 2 * i:2 * i + 2, 0:MD],
                        src.rearrange("p (t h d) -> p t h d", t=TT, h=2)).then_inc(unit_act, 1)
                elif kind in ("qm", "km2"):
                    ci = i + 2 * (kind == "km2")
                    if ci >= 2:
                        eng.wait_ge(conv_acc, 4 * l + ci - 1)
                    act(convx[:, ci % 2, :, 3:3 + S], fm2).then_inc(unit_act, 1)
                elif kind == "om":
                    act(so[:, :, cols], fm2, ACT.Tanh, scale=0.5).then_inc(unit_act, 1)
                elif kind == "g":
                    b, q = i // 4, i % 4
                    act(gates[:, b, :, q * UC:(q + 1) * UC], fm2, ACT.Tanh, scale=0.5).then_inc(unit_act, 1)
                else:
                    w, dst = (2 * MH, ifr) if kind == "if" else (E, lg)
                    act(dst[:, :, :], src[:, 0:TT * w].rearrange("p (t n) -> p t n", t=TT)).then_inc(unit_act, 1)
                if kind == "if":
                    eng.wait_ge(if_neg, l + 1)
                    link(act(ef[:, :, :], nab[:, :, :], ACT.Exp))
                    act(ef[:, :, :], ef[:, :, :], ACT.Ln, bias=1.0).then_inc(if_ln, 1)
                if kind == "route":
                    eng.wait_ge(route_sel, 1)
                    act(eg[:, :, :], eg[:, :, :], ACT.Exp).then_inc(route_exp, 1)
                for name, k in a["ex"]:
                    extra(name, k, l, a)

            def extra(name, k, l, a):
                pt = slots_mem * l + k + (XH if name[0] == "d" else 0)
                mix = mixes * l + k + {"m": 0, "d": XH + MH}.get(name[0], 0)
                if name == "memA":
                    eng.wait_ge(max_mem, XH * l + k + 1)
                    for t in range(TT):
                        last = act(probs[:, k % 2, 0:2, :].rearrange("p a b -> p (a b)")[:, t * NM:(t + 1) * NM],
                                   ps[:, 2 + k % 2, t * NM:(t + 1) * NM], ACT.Exp, scale=XD ** -0.5,
                                   bias=nb[:, k % 2, t:t + 1], accum_out=den[:, k % 2, t:t + 1])
                    last.then_inc(p_mem, 1)
                elif name == "memC":
                    eng.wait_ge(pt_psum, pt + 1)
                    if mix:
                        eng.wait_ge(mix_psum, mix)
                    act(probsT[:, :, :].rearrange("p a b -> p (a b)")[:, 0:4 * P], ps[:, 5, :]).then_inc(pt_ready, 1)
                elif name == "conv":
                    eng.wait_ge(conv_acc, 4 * l + k + 1)
                    act(convt[:, k % 2, :], convy[:, k % 2, :], ACT.Tanh, scale=0.5).then_inc(conv_tanh, 1)
                elif name == "brow":
                    eng.wait_ge(em_in, l + 1)
                    act(em[:, :, :], fm[:, :, :], ACT.Exp, scale=-1.0).then_inc(em_ready, 1)
                elif name == "mrow":
                    eng.wait_ge(rows_read, 2 * l + 2)
                    for h in range(MH):
                        act(wml[:, h, 0:S], wml[:, h, 0:S], ACT.Exp, bias=bb[:, 0, h:h + 1])
                        last = act(wml[:, h, S:S + P], wml[:, h, S:S + P], ACT.Exp, bias=bb[:, 1, h:h + 1])
                    last.then_inc(wml_ready, 1)
                elif name == "mlF":
                    eng.wait_ge(ml_var, l + 1)
                    link(act(lv8[:, :], v8[:, :], ACT.Ln))
                    act(r8[:, :], lv8[:, :], ACT.Exp, scale=-0.5).then_inc(ml_rstd, 1)
                elif name == "dR":
                    eng.wait_ge(max_d, DHG * l + k + 1)
                    for t, cols in enumerate((slice(0, P), slice(P, 3 * P))):
                        last = act(probs[:, k % 2, :, cols], probs[:, k % 2, :, cols], ACT.Exp, scale=DD ** -0.5,
                                   bias=nb[:, k % 2, t:t + 1], accum_out=den[:, k % 2, t:t + 1])
                    last.then_inc(p_d, 1)
                elif name == "dT":
                    eng.wait_ge(pt_psum, pt + 1)
                    eng.wait_ge(mix_psum, mix)
                    act(probsT[:, :, :], ps[:, 5:8, 0:3 * P]).then_inc(pt_ready, 1)
                elif name == "ht":
                    _, _, dst, k0 = ht_src(k)
                    transposed_hi(a["tr"][k], dst[0][:, k0:k0 + 2, :].rearrange("p k s -> p (k s)"))

            split_hi(0)
            split_hi(1)
            for kind, a in plan:
                if "c" in a:
                    split_hi(a["c"] + 2)
                if kind == "norm":
                    norm(a)
                elif kind == "merged":
                    xt(a["tr"])
                elif kind == "unit":
                    unit(a)
                elif kind == "gate":
                    p = a["p"]
                    eng.wait_ge(chunk_used, a["c"] + 1)
                    if p >= 2:
                        eng.wait_ge(hid_done, p - 1)
                    act(sg[:, p % 2, :], ps[:, (2 * p) % 4, :], ACT.Silu).then_inc(silu_done, 1)
                elif kind == "up":
                    p = a["p"]
                    eng.wait_ge(hid_done, p + 1)
                    if p >= 2:
                        eng.wait_ge(chunk_used, chunk_of["down", p - 2] + 1)
                    act(hThi[:, p % 2, :], hh[:, p % 2, :]).then_inc(hid_hi, 1)

            def split_hi_moe(r, e, m):
                eng.wait_ge(moe_loaded[m % MRAW], e * (16 * EC // MRAW) + 16 * (m // MRAW + 1 + r * E * EC // MRAW))
                eng.wait_ge(chunk_used, e * EC + (NDC + r * E * EC + m - SPL + 1))
                act(whi[:, m % SPL, :], raw_moe[m % MRAW][:, :]).then_inc(hi_done, 1)

            def hidden_hi(r, e, j):
                eng.wait_ge(m_tp, e * NJ + (r * E * NJ + j + 1))
                act(hThi[:, j % 2, :], ps[:, 4 + j % 2, :]).then_inc(m_thi, 1)

            def gathered_hi(r, e):
                eng.wait_ge(m_gath, e + (r * (E + 1) + 1))
                act(xehi[:, :, :].rearrange("p k s -> p (k s)"), ps[:, 2:4, :].rearrange("p a b -> p (a b)"))\
                    .then_inc(m_xehi, 1)

            def experts(r):
                split_hi_moe(r, 0, 0)
                split_hi_moe(r, 0, 1)
                gathered_hi(r, 0)
                with eng.Fori(0, E) as e:
                    for k, (kind, j, part) in enumerate(moe_chunks):
                        if k + 2 < EC:
                            split_hi_moe(r, e, k + 2)
                        else:
                            with eng.If(e < E - 1):
                                split_hi_moe(r, e, k + 2)
                        if kind == "g" and part == 1:
                            eng.wait_ge(chunk_used, e * EC + (NDC + r * E * EC + k + 1))
                            if j >= 2:
                                eng.wait_ge(m_hid, e * NJ + (r * E * NJ + j - 1))
                            act(sg[:, j % 2, :], ps[:, 2 * (j % 2), :], ACT.Silu).then_inc(m_silu, 1)
                            if j:
                                hidden_hi(r, e, j - 1)
                        if kind == "u" and part == 1 and j == 1:
                            eng.wait_ge(m_putp, e + (r * E + 1))
                            act(put[:, :, :].rearrange("p t s -> p (t s)"), ps[:, 5, 0:TT * P]).then_inc(m_put, 1)
                        if k == EC - 3:
                            hidden_hi(r, e, NJ - 1)
                            gathered_hi(r, e + 1)
                    eng.wait_ge(chunk_used, e * EC + (NDC + (r * E + 1) * EC))
                    act(ye[:, :], ps[:, 6:8, :].rearrange("p a b -> p (a b)")).then_inc(m_y, 1)

            experts(0)
            eng.wait_ge(flag_ready, 1)
            over = eng.value_load(flag[0:1, 0:1], min_val=0, max_val=1)
            with eng.If(over > 0):
                experts(1)
            norm(dict(n=3 * L))

        @block.tensor
        def _(eng):
            def mm3(dst, a, b, first, last):
                eng.matmul(dst, a[0], b[0], start=first, stop=False)
                eng.matmul(dst, a[0], b[1], start=False, stop=False)
                return eng.matmul(dst, a[1], b[0], start=False, stop=last)

            def mm(dst, pairs):
                for i, (a, b) in enumerate(pairs):
                    last = eng.matmul(dst, a, b, start=i == 0, stop=i == len(pairs) - 1)
                return last

            def parts(pair, *index):
                return tuple(t[index] for t in pair)

            XT = (xthi, xtlo)

            def weights(c):
                kt, n_ = chunks[c][1:]
                return view(whi[:, c % SPL, :], n_, kt), view(wlo[:, c % SPL, :], n_, kt)

            def transposes(tr, src, ks):
                if tr >= 2:
                    eng.wait_ge(tr_lo, tr - 1)
                for i, k in enumerate(ks):
                    for t in range(TT):
                        last = eng.transpose(ps[:, 5 + tr % 2, (i * TT + t) * P:(i * TT + t + 1) * P],
                                             src[:, t, k * P:(k + 1) * P], ident[:, :])
                last.then_inc(tr_psum, 1)

            def unit(a):
                c, u, l = a["c"], a["u"], a["l"]
                kt, n_ = chunks[c][1:]
                w = weights(c)
                wait_bank(eng, u)
                if a["form"] == "F":
                    for f in range(n_ // P):
                        for k in range(kt):
                            last = mm3(ps[:, u % 2, f * S:(f + 1) * S], parts(w, slice(None), k, slice(f * P, (f + 1) * P)),
                                       parts(XT, slice(None), k), k == 0, k == kt - 1)
                else:
                    for t in range(TT):
                        for k in range(kt):
                            last = mm3(ps[:, u % 2, t * n_:(t + 1) * n_], parts(XT, slice(None), k, slice(t * P, (t + 1) * P)),
                                       parts(w, slice(None), k), k == 0, k == kt - 1)
                last.then_inc(chunk_used, 1)
                for name, k in a["ex"]:
                    extra(name, k, l, a)

            def extra(name, k, l, a):
                pt = slots_mem * l + k + (XH if name[0] == "d" else 0)
                mix = mixes * l + k + {"m": XH if name[:2] == "ml" else 0, "d": XH + MH}.get(name[0], 0)
                if name == "memA":
                    eng.wait_ge(unit_act, evac(l, "qx"))
                    if k >= 2:
                        eng.wait_ge(p_mem, XH * l + k - 1)
                    for t in range(TT):
                        last = mm(ps[:, 2 + k % 2, t * NM:(t + 1) * NM], [(qx[:, k, t * P:(t + 1) * P], kmT[:, k, :])])
                    last.then_inc(s_mem, 1)
                elif name == "memC":
                    eng.wait_ge(p_mem, XH * l + k + 1)
                    eng.wait_ge(tr_lo, tr_norm[3 * l + 1] + KT // 2)
                    if pt:
                        eng.wait_ge(pt_ready, pt)
                    pv = probs[:, k % 2, 0:2, :].rearrange("p a b -> p (a b)")
                    for i in range(4):
                        last = eng.transpose(ps[:, 5, i * P:(i + 1) * P], pv[:, i * P:(i + 1) * P], ident[:, :])
                    last.then_inc(pt_psum, 1)
                elif name == "memE":
                    eng.wait_ge(pt_ready, pt + 1)
                    if mix:
                        eng.wait_ge(mix_read, mix)
                    tv = probsT[:, :, :].rearrange("p a b -> p (a b)")
                    for t in range(TT):
                        last = mm(ps[:, 4, t * P:(t + 1) * P],
                                  [(tv[:, (2 * t + m) * P:(2 * t + m + 1) * P], vm[:, m, k * XD:(k + 1) * XD])
                                   for m in range(2)])
                    last.then_inc(mix_psum, 1)
                elif name == "cum":
                    eng.wait_ge(logf, l + 1)
                    mm(ps[:, 7, 0:MH], [(upper[:, :], lf[:, 0, :])])
                    mm(ps[:, 7, MH:2 * MH], [(ones[:, :], lf[:, 0, :]), (upper[:, :], lf[:, 1, :])]).then_inc(cum_psum, 1)
                elif name in ("brow", "mrow"):
                    n_ = 2 * l + (name == "mrow")
                    eng.wait_ge(diag_ready, n_ + 1)
                    eng.wait_ge(pt_ready, slots_mem * l + XH)
                    if n_:
                        eng.wait_ge(rows_read, n_)
                    for t in range(TT):
                        last = mm(ps[:, 5 + t, :], [(ones[:, :], diag[:, t, :, :].rearrange("p h j -> p (h j)"))])
                    last.then_inc(rows_psum, 1)
                elif name == "mlA":
                    eng.wait_ge(conv_done, 4 * (l + 1))
                    if k >= 2:
                        eng.wait_ge(sw_ml, MH * l + k - 1)
                    mm(ps[:, 2 + k % 2, 0:S], [(qk[:, MH + k, 0:P], qk[:, k, :])])
                    mm(ps[:, 2 + k % 2, S:S + P], [(qk[:, MH + k, P:S], qk[:, k, P:S])]).then_inc(s_ml, 1)
                elif name == "mlE":
                    eng.wait_ge(sw_ml, MH * l + k + 1)
                    eng.wait_ge(unit_act, evac(l, "vml"))
                    eng.wait_ge(mix_read, mix)
                    sw = probs[:, k % 2, 0, :]
                    mm(ps[:, 4, 0:VA], [(sw[:, 0:P], vaug[:, 0, k, :])])
                    mm(ps[:, 4, VA:2 * VA], [(sw[:, P:S], vaug[:, 0, k, :]), (sw[:, S:S + P], vaug[:, 1, k, :])])\
                        .then_inc(mix_psum, 1)
                elif name in ("dS", "dR"):
                    o, tile = (k % 2) * DD, k // 2
                    if name == "dS":
                        eng.wait_ge(unit_act, evac(l, "kd"))
                        eng.wait_ge(sw_ml, MH * (l + 1))
                        if k:
                            eng.wait_ge(d_masked, DG * (DHG * l + k))
                    else:
                        eng.wait_ge(d_masked, DG * (DHG * l + k) + 1)
                    for g in ((0, 1) if name == "dS" else (2,)):
                        q_, k_ = qd[o:o + DD, 2 * g + tile, :], kd[o:o + DD, 2 * g + tile, :]
                        mm(ps[:, 2 + g % 2, 0:P], [(q_[:, 0:P], k_[:, 0:P])])
                        mm(ps[:, 2 + g % 2, P:3 * P], [(q_[:, P:S], k_)]).then_inc(s_d, 1)
                elif name == "dT":
                    eng.wait_ge(p_d, DHG * l + k + 1)
                    eng.wait_ge(pt_ready, pt)
                    if not k:
                        eng.wait_ge(rows_read, 2 * l + 2)
                    for b in range(3):
                        for g in range(DG):
                            last = eng.transpose(ps[:, 5 + b, g * P:(g + 1) * P],
                                                 probs[:, k % 2, g, b * P:(b + 1) * P], ident[:, :])
                    last.then_inc(pt_psum, 1)
                elif name == "dE":
                    eng.wait_ge(pt_ready, pt + 1)
                    eng.wait_ge(mix_read, mix)
                    v_ = [[vd[:, t, g * DHG * DD + k * DD:g * DHG * DD + (k + 1) * DD] for g in range(DG)] for t in range(TT)]
                    pT = [[probsT[:, b, g * P:(g + 1) * P] for g in range(DG)] for b in range(3)]
                    mm(ps[:, 4, 0:DD], [(pT[0][g], v_[0][g]) for g in range(DG)])
                    mm(ps[:, 4, DD:2 * DD], [(pT[1 + t][g], v_[t][g]) for t in range(TT) for g in range(DG)])\
                        .then_inc(mix_psum, 1)
                elif name == "ht":
                    src, ks, _, _ = ht_src(k)
                    if k == 0:
                        eng.wait_ge(pt_ready, slots_mem * (l + 1))
                    if k < 2:
                        eng.wait_ge(mix_read, mixes * l + XH)
                    elif k < 4:
                        eng.wait_ge(hm_ready, l + 1)
                    else:
                        eng.wait_ge(mix_read, mixes * (l + 1))
                    transposes(a["tr"][k], src, ks)

            eng.wait_ge(consts_made, 1)
            eng.wait_ge(consts_loaded, 32)
            eng.transpose(ps[:, 7, 0:L * 32], cwn[:, :], ident[0:L * 32, 0:L * 32]).then_inc(cw_psum, 1)
            eng.wait_ge(cw_ready, 1)
            for kind, a in plan:
                l = a.get("l")
                if kind == "norm":
                    if a["n"] == 3:
                        eng.wait_ge(y_read, 4)
                    eng.wait_ge(normed, TT * (a["n"] + 1))
                    for q in range(KT // 2):
                        transposes(a["tr"] + q, xn, (2 * q, 2 * q + 1))
                elif kind == "merged":
                    eng.wait_ge(merged_ready, 4 * (a["l"] + 1))
                    for q in range(KT // 2):
                        transposes(a["tr"] + q, merged, (2 * q, 2 * q + 1))
                if kind in ("norm", "merged"):
                    eng.wait_ge(tr_lo, a["tr"] + KT // 2)
                if "c" not in a:
                    continue
                c = a["c"]
                eng.wait_ge(lo_done, c + 1)
                w = weights(c)
                if kind == "unit":
                    unit(a)
                elif kind == "branch":
                    hT = (hmT, hdT, hxT)[a["b"]]
                    eng.wait_ge(tr_lo, tr_merged[l])
                    for i, h in enumerate(a["halves"]):
                        for t in range(TT):
                            u = a["u"] + TT * i + t
                            wait_bank(eng, u)
                            for k in range(a["kt"]):
                                last = mm3(ps[:, u % 2, :], parts(hT, slice(None), k, slice(t * P, (t + 1) * P)),
                                           parts(w, slice(None), k, slice(i * HC, (i + 1) * HC)), k == 0, k == a["kt"] - 1)
                            last.then_inc(chunk_used if product[u][0] is chunk_used else unit_done, 1)
                elif kind == "outproj":
                    for t in range(TT):
                        u = a["u"] + t
                        if a["q"] == 0:
                            wait_bank(eng, u)
                        for k in range(4):
                            last = mm3(ps[:, u % 2, :], parts(XT, slice(None), 4 * a["q"] + k, slice(t * P, (t + 1) * P)),
                                       parts(w, slice(None), k), a["q"] == 0 and k == 0, a["q"] == 1 and k == 3)
                        if a["q"] == 1 and t == 0:
                            last.then_inc(unit_done, 1)
                    last.then_inc(chunk_used, 1)
                elif kind in ("gate", "up"):
                    p = a["p"]
                    if p >= 2:
                        eng.wait_ge(silu_done if kind == "gate" else hid_done, p - 1)
                    b = (2 * p + (kind == "up")) % 4
                    for f in range(2):
                        for k in range(KT):
                            last = mm3(ps[:, b, f * S:(f + 1) * S], parts(w, slice(None), k, slice(f * P, (f + 1) * P)),
                                       parts(XT, slice(None), k), k == 0, k == KT - 1)
                    last.then_inc(chunk_used, 1)
                elif kind == "down":
                    p = a["p"]
                    eng.wait_ge(hid_lo, p + 1)
                    for f in range(2):
                        for t in range(TT):
                            hT = parts((hThi, hTlo), slice(None), p % 2, slice(f * S + t * P, f * S + (t + 1) * P))
                            for h in range(2):
                                last = mm3(ps[:, 4 + 2 * t + h, :], hT, parts(w, slice(None), f, slice(h * HC, (h + 1) * HC)),
                                           p == 0 and f == 0, p == NP_ - 1 and f == 1)
                    last.then_inc(chunk_used, 1)

            eng.wait_ge(route_sel, 1)
            mm(ps[:, 7, 0:E], [(upper_s[:, :], sel[:, 0, :])])
            mm(ps[:, 7, E:2 * E], [(ones[:, :], sel[:, 0, :]), (upper_s[:, :], sel[:, 1, :])])
            mm(ps[:, 7, 2 * E:3 * E], [(ones[:, :], sel[:, 0, :]), (ones[:, :], sel[:, 1, :])]).then_inc(route_pos, 1)

            def gather(r, e):
                eng.wait_ge(m_pick, e + (r * (E + 1) + 1))
                for k in range(KT):
                    last = mm(ps[:, 2 + k // 4, (k % 4) * P:(k % 4 + 1) * P],
                              [(xn[:, t, k * P:(k + 1) * P], pick[:, t, :]) for t in range(TT)])
                last.then_inc(m_gath, 1)

            def scatter(r, e):
                eng.wait_ge(m_y, e + (r * (E + 1) + 1))
                eng.wait_ge(m_put, e + (r * (E + 1) + 1))
                for i in range(4):
                    t, h = i // 2, i % 2
                    if i >= 2:
                        eng.wait_ge(m_added, e * 4 + (r * (E + 1) * 4 + i - 1))
                    mm(ps[:, 4 + i % 2, :], [(put[:, t, :], ye[:, h * HC:(h + 1) * HC])]).then_inc(m_scat, 1)

            def hidden_T(r, e, j):
                eng.wait_ge(m_hid, e * NJ + (r * E * NJ + j + 1))
                for i in range(4):
                    last = eng.transpose(ps[:, 4 + j % 2, i * P:(i + 1) * P], hh[:, j % 2, i * P:(i + 1) * P], ident[:, :])
                last.then_inc(m_tp, 1)

            def experts_all(r):
                gather(r, 0)
                with eng.Fori(0, E) as e:
                    eng.wait_ge(m_xelo, e + (r * (E + 1) + 1))
                    for k in range(EC):
                        expert_chunk(r, e, k)
                        if k == EC - 3:
                            eng.wait_ge(m_tlo, e * NJ + (r * E * NJ + NJ - 2))
                            hidden_T(r, e, NJ - 1)
                            gather(r, e + 1)
                scatter(r, E)

            def expert_chunk(r, e, k):
                kind, j, part = moe_chunks[k]
                eng.wait_ge(lo_done, e * EC + (NDC + r * E * EC + k + 1))
                if kind == "d":
                    w = view(whi[:, k % SPL, :], D, 2), view(wlo[:, k % SPL, :], D, 2)
                    if part == 0:
                        eng.wait_ge(m_tlo, e * NJ + (r * E * NJ + j + 1))
                    for i in range(2):
                        kk = 2 * part + i
                        hT = parts((hThi, hTlo), slice(None), j % 2, slice(kk * P, (kk + 1) * P))
                        for h in range(2):
                            last = mm3(ps[:, 6 + h, :], hT, parts(w, slice(None), i, slice(h * HC, (h + 1) * HC)),
                                       j == 0 and kk == 0, j == NJ - 1 and kk == 3)
                    last.then_inc(chunk_used, 1)
                    return
                w = view(whi[:, k % SPL, :], HC, 4), view(wlo[:, k % SPL, :], HC, 4)
                if part == 0 and j >= 2:
                    eng.wait_ge(m_silu if kind == "g" else m_hid, e * NJ + (r * E * NJ + j - 1))
                b = 2 * (j % 2) + (kind == "u")
                for i in range(4):
                    kk = 4 * part + i
                    last = mm3(ps[:, b, :], (xehi[:, kk, :], xelo[:, kk, :]), parts(w, slice(None), i), kk == 0, kk == KT - 1)
                last.then_inc(chunk_used, 1)
                if part == 0:
                    return
                if kind == "g" and j == 0:
                    scatter(r, e)
                elif kind == "g":
                    if j == 1:
                        eng.wait_ge(m_added, e * 4 + (r * (E + 1) * 4 + 3))
                    elif j == 2:
                        eng.wait_ge(m_put, e + (r * (E + 1) + 2))
                    else:
                        eng.wait_ge(m_tlo, e * NJ + (r * E * NJ + j - 2))
                    hidden_T(r, e, j - 1)
                elif j == 1:
                    eng.wait_ge(m_added, e * 4 + (r * (E + 1) * 4 + 4))
                    for t in range(TT):
                        last = eng.transpose(ps[:, 5, t * P:(t + 1) * P], pickg[:, t, :], ident[:, :])
                    last.then_inc(m_putp, 1)

            experts_all(0)
            eng.wait_ge(flag_ready, 1)
            over = eng.value_load(flag[0:1, 0:1], min_val=0, max_val=1)
            with eng.If(over > 0):
                experts_all(1)

        @block.vector
        def _(eng):
            n = [0]

            def link(ins):
                n[0] += 1
                ins.then_inc(dve_seq, 1)
                eng.wait_ge(dve_seq, n[0])

            tt, ts, stt = eng.tensor_tensor, eng.tensor_scalar, eng.scalar_tensor_tensor

            def split_lo(c):
                if c >= NDC:
                    return
                kt, n_ = chunks[c][1:]
                eng.wait_ge(hi_done, c + 1)
                tt(wlo[:, c % SPL, 0:kt * n_], raw[c % RAW][:, 0:kt * n_], whi[:, c % SPL, 0:kt * n_].bitcast(f32),
                   ALU.subtract).then_inc(lo_done, 1)

            def transposed_lo(tr, dst, hi):
                eng.wait_ge(tr_hi, tr + 1)
                tt(dst, ps[:, 5 + tr % 2, :], hi.bitcast(f32), ALU.subtract).then_inc(tr_lo, 1)

            def xt(tr):
                for q in range(KT // 2):
                    transposed_lo(tr + q, *(t[:, 2 * q:2 * q + 2, :].rearrange("p k s -> p (k s)") for t in (xtlo, xthi)))

            def newton(r, r_first, v, t):
                link(tt(t, r_first, r_first, ALU.mult))
                link(tt(t, t, v, ALU.mult))
                link(ts(t, t, -0.5, 1.5, ALU.mult, ALU.add))
                link(tt(r, r_first, t, ALU.mult))

            def norm(a):
                n_ = a["n"]
                l = n_ // 3
                src = x
                if n_ % 3 == 0 and n_ < 3 * L:
                    src = xn
                    eng.wait_ge(mem_loaded, 16 * (l + 1))
                elif n_ == 1:
                    eng.wait_ge(x_loaded, 16)
                if n_ % 3:
                    eng.wait_ge(tr_psum, tr_norm[n_])
                junk = gates[:, 0, :, :] if src is xn else xn
                for t in range(TT):
                    last = eng.tensor_tensor_reduce(junk[:, t, :], src[:, t, :], src[:, t, :], 1.0 / D, EPS,
                                                    ALU.mult, ALU.add, var[:, t:t + 1])
                last.then_inc(vars_, 1)
                eng.wait_ge(rstd0, n_ + 1)
                newton(rstd[:, :], r0[:, :], var[:, :], nt[:, :])
                eng.wait_ge(gain_loaded, 16 * (n_ + 1))
                for t in range(TT):
                    stt(xn[:, t, :], src[:, t, :], rstd[:, t:t + 1], gain[:, :], ALU.mult, ALU.mult).then_inc(normed, 1)
                if n_ < 3 * L:
                    xt(a["tr"])

            def conv(l, ci, u):
                eng.wait_ge(unit_act, read_count(u))
                for j in (3, 2, 1, 0):
                    for f in range(2):
                        y = convy[:, ci % 2, f * S:(f + 1) * S]
                        xx = convx[:, ci % 2, f, j:j + S]
                        row = (l * 4 + j) * 8 + 2 * ci + f
                        if j == 3:
                            last = ts(y, xx, cw[:, row:row + 1], None, ALU.mult)
                        else:
                            last = stt(y, xx, cw[:, row:row + 1], y, ALU.mult, ALU.add)
                    if j:
                        link(last)
                last.then_inc(conv_acc, 1)

            def diags(src):
                for t in range(TT):
                    for h in range(MH):
                        last = ts(diag[:, t, h, :], ident[:, :], src[:, t, h:h + 1], None, ALU.mult)
                last.then_inc(diag_ready, 1)

            def unit(a):
                (kind, i), l, u = a["to"], a["l"], a["u"]
                cols = slice(i * UC, (i + 1) * UC)
                if kind in ("qm", "km2"):
                    conv(l, i + 2 * (kind == "km2"), u)
                elif kind == "om":
                    eng.wait_ge(unit_act, read_count(u))
                    link(ts(so[:, :, cols], so[:, :, cols], 0.5, 0.5, ALU.mult, ALU.add))
                elif kind == "g":
                    eng.wait_ge(unit_act, read_count(u))
                    v = gates[:, i // 4, :, (i % 4) * UC:(i % 4 + 1) * UC]
                    ts(v, v, 0.5, 0.5, ALU.mult, ALU.add).then_inc(gate_done, 1)
                elif kind == "if":
                    eng.wait_ge(unit_act, read_count(u))
                    link(tt(ifb[:, :, :], ifr[:, :, :], bif[:, l:l + 1, :].broadcast_to([P, TT, 2 * MH]), ALU.add))
                    f_ = ifb[:, :, MH:2 * MH]
                    stt(nab[:, :, :], f_, -1.0, f_, ALU.mult, ALU.min).then_inc(if_neg, 1)
                    eng.wait_ge(if_ln, l + 1)
                    stt(lf[:, :, :], f_, 0.0, ef[:, :, :], ALU.min, ALU.subtract).then_inc(logf, 1)
                elif kind == "route":
                    route(u)
                for name, k in a["ex"]:
                    extra(name, k, l, a)

            def extra(name, k, l, a):
                mix = mixes * l + k + {"m": XH if name[:2] == "ml" else 0, "d": XH + MH}.get(name[0], 0)
                if name == "memA":
                    eng.wait_ge(s_mem, XH * l + k + 1)
                    link(eng.tensor_reduce(mx[:, k % 2, :], ps[:, 2 + k % 2, :].rearrange("p (t n) -> p t n", t=TT), AX.X, ALU.max))
                    ts(nb[:, k % 2, :], mx[:, k % 2, :], -(XD ** -0.5), None, ALU.mult).then_inc(max_mem, 1)
                elif name in ("memE", "dE"):
                    eng.wait_ge(mix_psum, mix + 1)
                    link(eng.reciprocal(rec[:, :], den[:, k % 2, :]))
                    dst, w_ = (hx, XD) if name == "memE" else (hd, DD)
                    for t in range(TT):
                        last = ts(dst[:, t, k * w_:(k + 1) * w_], ps[:, 4, t * w_:(t + 1) * w_], rec[:, t:t + 1], None, ALU.mult)
                    last.then_inc(mix_read, 1)
                elif name == "conv":
                    eng.wait_ge(conv_tanh, 4 * l + k + 1)
                    link(ts(convt[:, k % 2, :], convt[:, k % 2, :], 0.5, 0.5, ALU.mult, ALU.add))
                    tt(qk[:, 2 * k:2 * k + 2, :].rearrange("p f s -> p (f s)"), convy[:, k % 2, :], convt[:, k % 2, :],
                       ALU.mult).then_inc(conv_done, 1)
                elif name == "cum":
                    eng.wait_ge(cum_psum, l + 1)
                    link(eng.tensor_copy(cumf[:, :, :].rearrange("p t h -> p (t h)"), ps[:, 7, 0:TT * MH]))
                    link(tt(bb[:, :, :], ifb[:, :, 0:MH], cumf[:, :, :], ALU.subtract))
                    diags(bb)
                elif name == "brow":
                    eng.wait_ge(rows_psum, 2 * l + 1)
                    heads = [ps[:, 5 + t, :].rearrange("p (h j) -> p h j", h=MH) for t in range(TT)]
                    cm = dmask[:, 0:1, 0:P].broadcast_to([P, MH, P])
                    tt(wml[:, :, 0:P], heads[0], cm, ALU.add)
                    link(tt(wml[:, :, P:2 * P], heads[1], cm, ALU.add))
                    eng.tensor_reduce(m2[:, 1, :], heads[0], AX.X, ALU.max).then_inc(rows_read, 1)
                    eng.tensor_reduce(mm_[:, 0, :], wml[:, :, 0:P], AX.X, ALU.max)
                    link(eng.tensor_reduce(m2[:, 0, :], wml[:, :, P:2 * P], AX.X, ALU.max))
                    link(tt(mm_[:, 1, :], m2[:, 0, :], m2[:, 1, :], ALU.max))
                    tt(fm[:, :, :], cumf[:, :, :], mm_[:, :, :], ALU.add).then_inc(em_in, 1)
                    link(ts(ngm[:, :, :], mm_[:, :, :], -1.0, None, ALU.mult))
                    diags(ngm)
                elif name == "mrow":
                    eng.wait_ge(rows_psum, 2 * l + 2)
                    heads = [ps[:, 5 + t, :].rearrange("p (h j) -> p h j", h=MH) for t in range(TT)]
                    cm = maskT[:, :].unsqueeze(1).broadcast_to([P, MH, P])
                    tt(wml[:, :, 0:P], heads[0], cm, ALU.add)
                    eng.tensor_copy(wml[:, :, P:2 * P], heads[1])
                    tt(wml[:, :, 2 * P:3 * P], heads[1], cm, ALU.add).then_inc(rows_read, 1)
                elif name == "mlA":
                    eng.wait_ge(s_ml, MH * l + k + 1)
                    eng.wait_ge(wml_ready, l + 1)
                    stt(probs[:, k % 2, 0, :], ps[:, 2 + k % 2, 0:3 * P], MD ** -0.5, wml[:, k, :], ALU.mult, ALU.mult)\
                        .then_inc(sw_ml, 1)
                elif name == "mlE":
                    eng.wait_ge(mix_psum, mix + 1)
                    eng.wait_ge(em_ready, l + 1)
                    link(eng.tensor_copy(dn[:, :], ps[:, 4, MD:2 * VA:VA]))
                    link(stt(dn[:, :], dn[:, :], -1.0, dn[:, :], ALU.mult, ALU.max))
                    link(tt(dn[:, :], dn[:, :], em[:, :, k], ALU.max))
                    link(eng.reciprocal(rec[:, :], dn[:, :]))
                    for t in range(TT):
                        last = ts(hraw[:, t, k, :], ps[:, 4, t * VA:t * VA + MD], rec[:, t:t + 1], None, ALU.mult)
                    last.then_inc(mix_read, 1)
                    eng.wait_ge(mix_read, mix + 1)
                    for t in range(TT):
                        link(eng.bn_stats(st[:, :], hraw[:, t, k, :]))
                        link(eng.bn_aggr(mv[:, t * MH + k, :], st[:, :]))
                    if k == MH - 1:
                        ts(v8[:, :], mv[:, :, 1], EPS, None, ALU.add).then_inc(ml_var, 1)
                elif name == "mlF":
                    eng.wait_ge(ml_rstd, l + 1)
                    newton(n8[:, :], r8[:, :], v8[:, :], lv8[:, :])
                    eng.wait_ge(mln_loaded, 16 * (l + 1))
                    for t in range(TT):
                        for h in range(MH):
                            i = t * MH + h
                            last = ts(hm[:, t, h * MD:(h + 1) * MD], hraw[:, t, h, :], mv[:, i, 0:1], n8[:, i:i + 1],
                                      ALU.subtract, ALU.mult)
                    link(last)
                    link(tt(hm[:, :, :], hm[:, :, :], mln[:, :].unsqueeze(1).broadcast_to([P, TT, MW]), ALU.mult))
                    tt(hm[:, :, :], hm[:, :, :], so[:, :, :], ALU.mult).then_inc(hm_ready, 1)
                elif name in ("dS", "dR"):
                    eng.wait_ge(consts_made, 2)
                    for g in ((0, 1) if name == "dS" else (2,)):
                        eng.wait_ge(s_d, DG * (DHG * l + k) + g + 1)
                        tt(probs[:, k % 2, g, :], ps[:, 2 + g % 2, 0:3 * P], dmask[:, g, :], ALU.add).then_inc(d_masked, 1)
                    if name == "dR":
                        eng.wait_ge(d_masked, DG * (DHG * l + k + 1))
                        eng.tensor_reduce(mx[:, k % 2, 0:1], probs[:, k % 2, :, 0:P], AX.XY, ALU.max)
                        link(eng.tensor_reduce(mx[:, k % 2, 1:2], probs[:, k % 2, :, P:3 * P], AX.XY, ALU.max))
                        ts(nb[:, k % 2, :], mx[:, k % 2, :], -(DD ** -0.5), None, ALU.mult).then_inc(max_d, 1)
                elif name == "ht":
                    _, _, dst, k0 = ht_src(k)
                    transposed_lo(a["tr"][k], *(dst[i][:, k0:k0 + 2, :].rearrange("p k s -> p (k s)") for i in (1, 0)))

            def route(u):
                eng.wait_ge(unit_act, read_count(u))
                for t in range(TT):
                    link(eng.tensor_reduce(m1[:, t:t + 1], lg[:, t, :], AX.X, ALU.max))
                    others = lg[:, t, :].unsqueeze(1).broadcast_to([P, E, E])
                    own = lg[:, t, :].unsqueeze(2).broadcast_to([P, E, E])
                    tt(gt[:, :, :], others, own, ALU.is_gt)
                    link(tt(eq[:, :, :], others, own, ALU.is_equal))
                    link(tt(eq[:, :, :], eq[:, :, :], lt[:, :, :], ALU.mult))
                    link(tt(gt[:, :, :], gt[:, :, :], eq[:, :, :], ALU.add))
                    link(eng.tensor_reduce(cnt[:, t, :], gt[:, :, :], AX.X, ALU.add))
                    link(ts(eg[:, t, :], lg[:, t, :], m1[:, t:t + 1], None, ALU.subtract))
                ts(sel[:, :, :], cnt[:, :, :], 1.5, None, ALU.is_lt).then_inc(route_sel, 1)
                eng.wait_ge(route_sel, 1)
                eng.wait_ge(route_exp, 1)
                link(tt(eg[:, :, :], eg[:, :, :], sel[:, :, :], ALU.mult))
                link(eng.tensor_reduce(dg[:, :], eg[:, :, :], AX.X, ALU.add))
                link(eng.reciprocal(dg[:, :], dg[:, :]))
                eng.wait_ge(route_pos, 1)
                link(ts(cnt[:, :, :], sel[:, :, :], -1e6, 1e6, ALU.mult, ALU.add))
                link(tt(posm[:, :, :], ps[:, 7, 0:TT * E].rearrange("p (t e) -> p t e", t=TT), cnt[:, :, :], ALU.add))
                for t in range(TT):
                    eng.tensor_copy(tab[:, 0:E, t], posm[:, t, :])
                    link(ts(tab[:, 0:E, 2 + t], eg[:, t, :], dg[:, t:t + 1], None, ALU.mult))
                link(eng.tensor_reduce(tmx[:, :], ps[:, 7, 2 * E:3 * E], AX.X, ALU.max))
                ts(flag[:, :], tmx[:, :], float(P) + 0.5, None, ALU.is_gt).then_inc(flag_ready, 1)

            eng.wait_ge(consts_made, 1)
            for g, dil in enumerate((4, 16)):
                link(ts(diffm[:, g, :], diff[:, :], dil - 1, None, ALU.bitwise_and))
                link(eng.tensor_copy(resid[:, g, :], diffm[:, g, :]))
                link(ts(resid[:, g, :], resid[:, g, :], 0.5, NEG, ALU.is_gt, ALU.mult))
            eng.memset(mx[:, :, :], 0.0).then_inc(masks_made, 1)
            eng.wait_ge(cw_psum, 1)
            eng.tensor_copy(cw[:, :], ps[:, 7, 0:L * 32]).then_inc(cw_ready, 1)
            eng.wait_ge(cw_ready, 1)
            split_lo(0)
            split_lo(1)
            for kind, a in plan:
                l = a.get("l")
                if "c" in a:
                    split_lo(a["c"] + 2)
                if kind == "norm":
                    norm(a)
                    if a["n"] % 3 == 1:
                        link(eng.memset(convx[:, :, :, 0:3], 0.0))
                elif kind == "merged":
                    xt(a["tr"])
                elif kind == "unit":
                    unit(a)
                elif kind == "branch":
                    b = a["b"]
                    if b == 0:
                        eng.wait_ge(gate_done, 12 * (l + 1))
                        eng.wait_ge(tr_psum, tr_merged[l])
                    for i, h in enumerate(a["halves"]):
                        for t in range(TT):
                            u = a["u"] + TT * i + t
                            cols = slice(h * HC, (h + 1) * HC)
                            g_ = gates[:, b, t, cols]
                            eng.wait_ge(*product[u])
                            dst = merged[:, t, cols] if b == 0 else g_
                            tt(dst, ps[:, u % 2, :], g_, ALU.mult).then_inc(unit_dve, 1)
                            eng.wait_ge(unit_dve, read_count(u))
                            if b:
                                last = tt(merged[:, t, cols], merged[:, t, cols], g_, ALU.add)
                                if b == 2:
                                    last.then_inc(merged_ready, 1)
                                else:
                                    link(last)
                elif kind == "outproj" and a["q"] == 1:
                    for t in range(TT):
                        u = a["u"] + t
                        eng.wait_ge(*product[u])
                        cols = slice(a["h"] * HC, (a["h"] + 1) * HC)
                        tt(x[:, t, cols], ps[:, u % 2, :], x[:, t, cols], ALU.add).then_inc(unit_dve, 1)
                        eng.wait_ge(unit_dve, read_count(u))
                elif kind == "up":
                    p = a["p"]
                    eng.wait_ge(chunk_used, a["c"] + 1)
                    eng.wait_ge(silu_done, p + 1)
                    tt(hh[:, p % 2, :], ps[:, (2 * p + 1) % 4, :], sg[:, p % 2, :], ALU.mult).then_inc(hid_done, 1)
                    eng.wait_ge(hid_done, p + 1)
                    eng.wait_ge(hid_hi, p + 1)
                    tt(hTlo[:, p % 2, :], hh[:, p % 2, :], hThi[:, p % 2, :].bitcast(f32), ALU.subtract).then_inc(hid_lo, 1)
                elif kind == "ffn_end":
                    eng.wait_ge(chunk_used, chunk_of["down", NP_ - 1] + 1)
                    for t in range(TT):
                        for h in range(2):
                            cols = slice(h * HC, (h + 1) * HC)
                            tt(x[:, t, cols], ps[:, 4 + 2 * t + h, :], x[:, t, cols], ALU.add).then_inc(y_read, 1)
                    eng.wait_ge(y_read, 4)

            def split_lo_moe(r, e, m):
                eng.wait_ge(hi_done, e * EC + (NDC + r * E * EC + m + 1))
                tt(wlo[:, m % SPL, :], raw_moe[m % MRAW][:, :], whi[:, m % SPL, :].bitcast(f32), ALU.subtract)\
                    .then_inc(lo_done, 1)

            def picks(r, e):
                eng.tensor_copy(cur[:, :].unsqueeze(1), tab[:, bass.ds(e, 1), :]).then_inc(m_cur, 1)
                eng.wait_ge(m_cur, e + (r * (E + 1) + 1))
                for t in range(TT):
                    ts(pickg[:, t, :], slots[:, r, :], cur[:, t:t + 1], cur[:, 2 + t:3 + t], ALU.is_equal, ALU.mult)
                for t in range(TT):
                    last = ts(pick[:, t, :], slots[:, r, :], cur[:, t:t + 1], None, ALU.is_equal)
                last.then_inc(m_pick, 1)

            def gathered_lo(r, e):
                eng.wait_ge(m_xehi, e + (r * (E + 1) + 1))
                tt(xelo[:, :, :].rearrange("p k s -> p (k s)"), ps[:, 2:4, :].rearrange("p a b -> p (a b)"),
                   xehi[:, :, :].rearrange("p k s -> p (k s)").bitcast(f32), ALU.subtract).then_inc(m_xelo, 1)

            def hidden_lo(r, e, j):
                eng.wait_ge(m_thi, e * NJ + (r * E * NJ + j + 1))
                tt(hTlo[:, j % 2, :], ps[:, 4 + j % 2, :], hThi[:, j % 2, :].bitcast(f32), ALU.subtract).then_inc(m_tlo, 1)

            def scattered(r, e):
                for i in range(4):
                    t, h = i // 2, i % 2
                    eng.wait_ge(m_scat, e * 4 + (r * (E + 1) * 4 + i + 1))
                    cols = slice(h * HC, (h + 1) * HC)
                    tt(x[:, t, cols], ps[:, 4 + i % 2, :], x[:, t, cols], ALU.add).then_inc(m_added, 1)

            def experts(r):
                eng.memset(ye[:, :], 0.0).then_inc(m_y, 1)
                eng.memset(put[:, :, :], 0.0).then_inc(m_put, 1)
                picks(r, 0)
                split_lo_moe(r, 0, 0)
                split_lo_moe(r, 0, 1)
                gathered_lo(r, 0)
                with eng.Fori(0, E) as e:
                    for k, (kind, j, part) in enumerate(moe_chunks):
                        if k + 2 < EC:
                            split_lo_moe(r, e, k + 2)
                        else:
                            with eng.If(e < E - 1):
                                split_lo_moe(r, e, k + 2)
                        if kind == "g" and part == 1:
                            if j == 0:
                                scattered(r, e)
                            else:
                                hidden_lo(r, e, j - 1)
                            if j == 3:
                                picks(r, e + 1)
                        if kind == "u" and part == 1:
                            eng.wait_ge(chunk_used, e * EC + (NDC + r * E * EC + k + 1))
                            eng.wait_ge(m_silu, e * NJ + (r * E * NJ + j + 1))
                            tt(hh[:, j % 2, :], ps[:, 2 * (j % 2) + 1, :], sg[:, j % 2, :], ALU.mult).then_inc(m_hid, 1)
                        if k == EC - 3:
                            hidden_lo(r, e, NJ - 1)
                            gathered_lo(r, e + 1)
                scattered(r, E)
                eng.wait_ge(m_added, (r + 1) * (E + 1) * 4)

            experts(0)
            eng.wait_ge(flag_ready, 1)
            over = eng.value_load(flag[0:1, 0:1], min_val=0, max_val=1)
            with eng.If(over > 0):
                experts(1)
            norm(dict(n=3 * L))


_INS = ['x', 'mem', 'norm_mix', 'w_in', 'conv_qk', 'b_gate_if', 'mlstm_norm', 'norm_mem', 'w_mem_kv', 'w_br_m', 'w_br_d',
        'w_br_x', 'w_out', 'norm_ffn', 'ffn_w_gate', 'ffn_w_up', 'ffn_w_down', 'moe_router', 'moe_w_gate', 'moe_w_up',
        'moe_w_down', 'norm_final']


def kernel(**inputs):
    import numpy as _np
    import concourse.bacc as _bacc
    from concourse import mybir as _mybir
    from concourse.bass_utils import run_bass_kernel_spmd as _run

    nc = _bacc.Bacc("TRN2", target_bir_lowering=False, num_devices=1)
    arrays, args = {}, []
    for name in _INS:
        a = _np.ascontiguousarray(inputs[name])
        arrays[f"in_{name}_dram"] = a
        args.append(nc.dram_tensor(f"in_{name}_dram", a.shape, _mybir.dt.from_np(a.dtype), kind="ExternalInput").ap())
    shape = arrays["in_x_dram"].shape
    args.append(nc.dram_tensor("out_0_dram", shape, _mybir.dt.float32, kind="ExternalOutput").ap())
    hybrid_trunk(nc, *args)
    r = _run(nc, [arrays], core_ids=[0])
    return r.results[0]["out_0_dram"]
```

```python
import concourse.bass as bass
from concourse import mybir
from contextlib import ExitStack


def hybrid_trunk(nc: bass.Bass, x_in, mem_in, norm_mix, w_in, conv_qk, b_gate_if, mlstm_norm, norm_mem,
                 w_mem_kv, w_br_m, w_br_d, w_br_x, w_out, norm_ffn, ffn_w_gate, ffn_w_up, ffn_w_down,
                 moe_router, moe_w_gate, moe_w_up, moe_w_down, norm_final, out):
    f32, f32r, i32 = mybir.dt.float32, mybir.dt.float32r, mybir.dt.int32
    ALU, ACT, AX = mybir.AluOpType, mybir.ActivationFunctionType, mybir.AxisListType

    P = 128
    S, D = x_in.shape[1], x_in.shape[2]
    L = w_in.shape[0]
    TT, KT = S // P, D // P
    NM = mem_in.shape[1]
    MH, MD = 4, 128
    MW = MH * MD
    XH, XD = 4, 128
    XW = XH * XD
    DG, DHG, DD = 3, 4, 64
    DW = DG * DHG * DD
    E = moe_router.shape[2]
    FF = ffn_w_gate.shape[2]
    FE = moe_w_gate.shape[3]
    EPS, NEG = 1e-6, -1e30
    assert TT == 2 and NM == S and MD == P and XD == P and E == 8

    C_QM, C_KM, C_VM, C_OM = 0, MW, 2 * MW, 3 * MW
    C_IF = 4 * MW
    C_QD = C_IF + 2 * MH
    C_VD = C_QD + 2 * DW
    C_QX = C_VD + DW
    C_G = C_QX + XW

    CH = 2048
    UC = CH // KT
    RAW, HI = 5, 4
    MRAW, MHI = 7, 7
    AHEAD, MAHEAD = 3, 4
    HC = 512

    def rows(w, k0, nk, c0, nc_):
        return w[k0 * P:(k0 + nk) * P, c0:c0 + nc_].rearrange("(t p) n -> p t n", p=P)

    chunks = []

    def chunk(w, k0, nk, c0, n):
        chunks.append((rows(w, k0, nk, c0, n), nk, n))
        return len(chunks) - 1

    plan = []

    def step(kind, **a):
        plan.append((kind, a))

    def mixer_plan(l):
        mem = w_mem_kv[l]
        units = [(i * UC, "F", ("km", i)) for i in range(XW // UC)] + [(XW + i * UC, "T", ("vm", i)) for i in range(XW // UC)]
        for i, (c0, form, to) in enumerate(units):
            step("unit", c=chunk(mem, 0, KT, c0, UC), form=form, to=to, l=l, ex=[], src="mem")
            if i == 0:
                step("stats", n=3 * l + 1)
            if i == 2:
                step("xt", n=3 * l + 1, src="x")
        w = w_in[l]
        units = []

        def add(kind, c0, width, form):
            for i in range(width // UC):
                units.append((c0 + i * UC, UC, form, (kind, i)))

        add("qx", C_QX, XW, "F")
        units.append((C_IF, 2 * MH, "T", ("if", 0)))
        add("qm", C_QM, MW, "F")
        add("km2", C_KM, MW, "F")
        add("vml", C_VM, MW, "T")
        add("qd", C_QD, DW, "F")
        add("kd", C_QD + DW, DW, "F")
        add("vd", C_VD, DW, "T")
        add("om", C_OM, MW, "T")
        add("g", C_G, 3 * D, "T")
        extras = {
            2: [("memA", 0)], 3: [("memC", 0), ("memA", 1)],
            4: [("conv", 0), ("memE", 0), ("memC", 1), ("memA", 2)],
            5: [("conv", 1), ("memE", 1), ("memC", 2), ("memA", 3)],
            6: [("conv", 2), ("memE", 2), ("memC", 3)],
            7: [("conv", 3), ("memE", 3)],
            8: [("cum", 0)], 9: [("brow", 0)], 10: [("mrow", 0)],
            12: [("mlA", 0)], 13: [("mlA", 1), ("mlE", 0)], 14: [("mlA", 2), ("mlE", 1)],
            15: [("mlA", 3), ("mlE", 2)], 16: [("mlE", 3)],
            18: [("dS", 0)], 19: [("dR", 0)],
            20: [("mlF", 0), ("dT", 0), ("dS", 1)], 21: [("dE", 0), ("dR", 1)],
            22: [("dT", 1), ("dS", 2)], 23: [("dE", 1), ("dR", 2)],
            24: [("dT", 2), ("dS", 3)], 25: [("dE", 2), ("dR", 3)],
            26: [("dT", 3)], 27: [("dE", 3)],
            28: [("ht", 0)], 29: [("ht", 1)], 30: [("ht", 2)], 31: [("ht", 3), ("ht", 4)],
        }
        for s, (c0, n, form, to) in enumerate(units):
            plan.append(("unit", dict(c=chunk(w, 0, KT, c0, n), form=form, to=to, l=l, ex=extras.pop(s, []), src="x")))
        assert not extras
        for b, (wb, kt) in enumerate(((w_br_m[l], MW // P), (w_br_d[l], DHG * DD // P), (w_br_x[l], XW // P))):
            if kt * D <= CH:
                c = chunk(wb, 0, kt, 0, D)
                plan.append(("branch", dict(c=c, b=b, kt=kt, halves=(0, 1), l=l)))
            else:
                for h in range(2):
                    plan.append(("branch", dict(c=chunk(wb, 0, kt, h * HC, HC), b=b, kt=kt, halves=(h,), l=l)))
        step("merged", l=l)
        for h in range(2):
            for q in range(2):
                plan.append(("outproj", dict(c=chunk(w_out[l], 4 * q, 4, h * HC, HC), h=h, q=q, l=l)))
        step("stats", n=3 * l + 2)
        step("xt", n=3 * l + 2, src="x")

    NP_ = FF // UC

    step("stats", n=0)
    step("split", m=0)
    step("xt", n=0, src="mem")
    for m in range(1, AHEAD):
        step("split", m=m)
    mixer_plan(0)
    for p in range(NP_ + 1):
        if p < NP_:
            plan.append(("gate", dict(c=chunk(ffn_w_gate[0], 0, KT, p * UC, UC), p=p)))
            plan.append(("up", dict(c=chunk(ffn_w_up[0], 0, KT, p * UC, UC), p=p)))
        if p == 0:
            step("xt", n=3, src="mem")
        if p:
            plan.append(("down", dict(c=chunk(ffn_w_down[0], 2 * (p - 1), 2, 0, D), p=p - 1)))
    plan.append(("ffn_end", {}))
    mixer_plan(1)
    plan.append(("unit", dict(c=chunk(moe_router[0], 0, KT, 0, E), form="T", to=("route", 0), l=1, ex=[], src="x")))
    NDC = len(chunks)

    NJ = FE // HC
    moe_chunks = []
    for j in range(NJ):
        moe_chunks += [("g", j, 0), ("g", j, 1), ("u", j, 0), ("u", j, 1)]
        if j:
            moe_chunks += [("d", j - 1, 0), ("d", j - 1, 1)]
    moe_chunks += [("d", NJ - 1, 0), ("d", NJ - 1, 1)]
    EC = len(moe_chunks)
    assert EC % MRAW == 0 and EC % MHI == 0

    ctx = ExitStack()
    with ctx:
        base = (nc.sbuf_base + 31) // 32 * 32
        top = [base]

        def at(name, shape, dt=f32, off=None):
            size = 4
            for n in shape[1:]:
                size *= n
            if off is None:
                off = top[0]
                top[0] += (size + 31) // 32 * 32
            return nc.alloc_sbuf_tensor_at(name, shape, dt, offset=off)

        raw = [at(f"raw{i}", [P, CH]) for i in range(RAW)]
        lo = [at(f"w_lo{i}", [P, CH], f32r, off=base + i * CH * 4) for i in range(RAW)]
        hi = [at(f"w_hi{i}", [P, CH], f32r) for i in range(HI)]
        xthi = at("xT_hi", [P, KT, S], f32r)
        xtlo = at("xT_lo", [P, KT, S], f32r)
        o_x = top[0]
        x = at("x", [P, TT, D])
        xn = at("x_normed", [P, TT, D])
        gain = at("gain", [P, D])
        g0 = top[0]
        gates = at("gates", [P, 3, TT, D])
        CW = S + 4
        convx = at("conv_x", [P, 2, 2, CW], off=g0)
        convy = at("conv_y", [P, 2, 2 * S], off=g0 + 4160)
        convt = at("conv_t", [P, 2, 2 * S], off=g0 + 8256)
        diag = at("diag", [P, TT, MH, P], off=g0 + 12352)
        wml = at("mlstm_w", [P, MH, 3 * P], off=g0 + 16448)
        mthi = at("memT_hi", [P, KT, NM], f32r, off=g0)
        mtlo = at("memT_lo", [P, KT, NM], f32r, off=g0 + KT * NM * 4)
        mem = at("mem", [P, TT, D], off=g0 + 2 * KT * NM * 4)
        VA = MD + 2
        vaug = at("v_aug", [P, TT, MH, VA])
        r1 = top[0]
        qk = at("qk_mT", [P, 2 * MH, S])
        hmT = [at("hmT_hi", [P, 4, S], f32r, off=r1), at("hmT_lo", [P, 4, S], f32r, off=r1 + 4 * S * 4)]
        r2 = top[0]
        qd = at("q_dT", [P, DW // P, S])
        kd = at("k_dT", [P, DW // P, S])
        qx = at("q_xT", [P, XH, S], off=r2)
        kmT = at("k_memT", [P, XH, NM], off=r2 + 4096)
        vm = at("v_mem", [P, TT, XW], off=r2 + 8192)
        hxT = [at("hxT_hi", [P, 4, S], f32r, off=r2), at("hxT_lo", [P, 4, S], f32r, off=r2 + 4096)]
        hdT = [at("hdT_hi", [P, 2, S], f32r, off=r2 + 8192), at("hdT_lo", [P, 2, S], f32r, off=r2 + 8192 + 2048)]
        so = at("sig_o", [P, TT, MW])
        vd = at("v_d", [P, TT, DW])
        probs = at("probs", [P, 2, 3, 3 * P])
        probsT = at("probsT", [P, 3, 3 * P])
        hraw = at("h_raw", [P, TT, MH, MD])
        top[0] = max(top[0], r1 + 52 * 1024)
        rawn = [at(f"raw_new{i}", [P, CH], off=g0 + i * CH * 4) for i in range(MRAW - RAW)]
        lon = [at(f"w_lo_new{i}", [P, CH], f32r, off=g0 + i * CH * 4) for i in range(MRAW - RAW)]
        hin = [at(f"w_hi_new{i}", [P, CH], f32r, off=o) for i, o in enumerate((g0 + 2 * CH * 4, r1 + 36864, r1 + 45056))]
        raw_moe = rawn + [raw[(NDC + i) % RAW] for i in range(RAW)]
        lo_moe = lon + [lo[(NDC + i) % RAW] for i in range(RAW)]
        hi_moe = hin + [hi[(NDC + i) % HI] for i in range(HI)]
        o_xn = o_x + TT * D * 4
        hm = at("h_m", [P, TT, MW], off=o_xn)
        hx = at("h_x", [P, TT, XW], off=o_xn + TT * MW * 4)
        hd = at("h_d", [P, TT, DHG * DD], off=o_xn + TT * D * 4)
        merged = at("merged", [P, TT, D], off=o_xn)
        f0 = r1 + 20480
        junk = at("junk", [P, TT, D], off=f0)
        sg = at("silu_g", [P, 2, HC], off=f0)
        hh = at("hidden", [P, 2, HC], off=f0 + 4096)
        hThi = at("hiddenT_hi", [P, 2, 4 * P], f32r, off=f0 + 8192)
        hTlo = at("hiddenT_lo", [P, 2, 4 * P], f32r, off=f0 + 12288)
        xehi = at("xe_hi", [P, KT, P], f32r, off=r1)
        xelo = at("xe_lo", [P, KT, P], f32r, off=r1 + 4096)
        ye = at("y_e", [P, D], off=r1 + 8192)
        pick = at("pick", [P, TT, P], off=r1 + 12288)
        pickg = at("pick_gated", [P, TT, P], off=r1 + 13312)
        put = at("put", [P, TT, P], off=r1 + 14336)
        dmask = at("dil_mask", [P, DG, 3 * P])
        maskT = at("causal_maskT", [P, P])
        ident = at("ident", [P, P])
        ones = at("ones", [P, P])
        upper = at("upper", [P, P])
        upper_s = at("upper_strict", [P, P])
        slots = at("slots", [P, 2, P])
        resid = at("residue", [P, 2, P])
        diff = at("diff", [P, P], i32, off=r1)
        diffm = at("diff_masked", [P, 2, P], i32, off=r1 + 512)
        NCW, NROWS = L * 4 * 8, L * 4 * 8 + 3 * L * KT
        cwn = at("channel_rows", [NROWS, P], off=r1 + 2048)
        cw = at("channel_cols", [P, NROWS])
        rdm = at("rstd_diag_mem", [P, TT, P])
        rdx = at("rstd_diag_x", [P, TT, P])
        bif = at("b_if", [P, L, 2 * MH])
        mln = at("mlstm_gain", [P, MW])
        ss = at("mean_sq_halves", [P, TT, 2])
        var = at("var", [P, TT])
        nt = at("newton", [P, TT])
        nti = at("half_bits", [P, TT], i32)
        rstd = at("rstd", [P, TT])
        ifr = at("if_raw", [P, TT, 2 * MH])
        ifb = at("if_pre", [P, TT, 2 * MH])
        nab = at("neg_abs_f", [P, TT, MH])
        ef = at("exp_f", [P, TT, MH])
        lf = at("log_f", [P, TT, MH])
        cumf = at("cum_f", [P, TT, MH])
        bb = at("b", [P, TT, MH])
        mm_ = at("m_minus_f", [P, TT, MH])
        m2 = at("m2", [P, 2, MH])
        ngm = at("neg_m", [P, TT, MH])
        fm = at("m_row", [P, TT, MH])
        em = at("exp_neg_m", [P, TT, MH])
        den = at("den", [P, 2, 2])
        dn = at("den_abs", [P, 2])
        rec = at("rec", [P, 2])
        mx = at("row_max", [P, 2, 2])
        nb = at("neg_max", [P, 2, 2])
        st = at("bn", [P, 6])
        mv = at("mean_var", [P, TT * MH, 2])
        r8 = at("rstd8", [P, TT * MH])
        ni8 = at("half_bits8", [P, TT * MH], i32)
        v8 = at("var8", [P, TT * MH])
        n8 = at("newton8", [P, TT * MH])
        lg = at("logits", [P, TT, E])
        m1 = at("top1", [P, TT])
        gt = at("greater", [P, E, E])
        eq = at("equal", [P, E, E])
        lt = at("earlier", [P, E, E])
        cnt = at("rank", [P, TT, E])
        sel = at("selected", [P, TT, E])
        eg = at("exp_logits", [P, TT, E])
        dg = at("gate_den", [P, TT])
        posm = at("position", [P, TT, E])
        tmx = at("most_tokens", [P, 1])
        tab = at("route_table", [P, E + 1, 4])
        cur = at("route_now", [P, 4])
        flag = at("overflow", [P, 1], i32)
        assert top[0] <= nc.sbuf_usable_end, (top[0], nc.sbuf_usable_end)

        ps = nc.alloc_psum_tensor("ps", [P, 8, HC], f32)

        def sem(name):
            return ctx.enter_context(nc.semaphore(name))

        raw_loaded = [sem(f"raw_loaded{i}") for i in range(RAW)]
        moe_loaded = [sem(f"moe_loaded{i}") for i in range(MRAW)]
        hi_done, lo_done, chunk_used = sem("hi_done"), sem("lo_done"), sem("chunk_used")
        ident_made, bif_loaded = sem("ident_made"), sem("gate_bias_loaded")
        consts_loaded, consts_made, masks_made = sem("consts_loaded"), sem("consts_made"), sem("masks_made")
        cw_psum, cw_ready = sem("conv_w_psum"), sem("conv_w_ready")
        x_loaded, mem_loaded = ([sem(f"{n_}_loaded{t}") for t in range(TT)] for n_ in ("x", "mem"))
        mem_reloaded = sem("mem_reloaded")
        gain_loaded, mln_loaded = sem("gain_loaded"), sem("mlstm_gain_loaded")
        rstd_ready, normed = sem("rstd_diag_ready"), sem("normed")
        tr_psum, tr_hi, tr_lo = sem("transposed"), sem("transposed_hi"), sem("transposed_lo")
        unit_done, unit_act, unit_dve = sem("unit_done"), sem("unit_read_act"), sem("unit_read_dve")
        conv_acc, conv_tanh, conv_done = sem("conv_acc"), sem("conv_tanh"), sem("conv_done")
        gate_done = sem("gates_done")
        if_neg, if_ln, logf = sem("neg_abs_ready"), sem("softplus_ready"), sem("log_f_ready")
        cum_psum, diag_ready, rows_psum, rows_read = sem("cum_psum"), sem("diag_ready"), sem("rows_psum"), sem("rows_read")
        em_in, em_ready, wml_ready = sem("m_row_ready"), sem("exp_neg_m_ready"), sem("mlstm_w_ready")
        s_mem, s_ml, s_d = sem("mem_scores"), sem("mlstm_scores"), sem("dil_scores")
        max_mem, max_d, d_masked = sem("mem_max"), sem("dil_max"), sem("dil_masked")
        p_mem, p_d, sw_ml = sem("mem_probs"), sem("dil_probs"), sem("mlstm_weighted")
        pt_psum, pt_ready = sem("probsT_psum"), sem("probsT_ready")
        mix_psum, mix_read = sem("mix_psum"), sem("mix_read")
        hm_ready = sem("h_m_ready")
        act_seq, dve_seq, pool_seq = sem("act_seq"), sem("dve_seq"), sem("pool_seq")
        merged_ready = sem("merged_ready")
        m_cur = sem("moe_route_now")
        silu_done, hid_done, hid_hi, hid_lo, y_read = sem("silu_done"), sem("hidden_done"), sem("hidden_hi"), sem("hidden_lo"), sem("y_read")
        route_exp, route_sel, route_pos, flag_ready = (sem(n) for n in ("route_exp", "route_selected", "route_pos", "flag_ready"))
        m_silu, m_hid, m_tp, m_thi, m_tlo = (sem("moe_" + n) for n in ("silu", "hidden", "hiddenT_psum", "hiddenT_hi", "hiddenT_lo"))
        m_pick, m_gath, m_xehi, m_xelo, m_putp, m_put, m_y, m_scat, m_added = (sem("moe_" + n) for n in ("pick", "gathered", "xe_hi", "xe_lo", "put_psum", "put", "y", "scattered", "added"))
        m_squares = sem("moe_squares")
        out_stored = sem("out_stored")

        gunits = []
        for kind, a in plan:
            if kind == "unit":
                a["u"] = len(gunits)
                gunits.append("act")
            elif kind == "branch":
                a["u"] = len(gunits)
                gunits += ["dve"] * (TT * len(a["halves"]))
            elif kind == "outproj" and a["q"] == 0:
                a["u"] = len(gunits)
                gunits += ["dve"] * TT
            elif kind == "outproj":
                a["u"] = len(gunits) - TT

        product, n_unit_done = {}, 0
        for kind, a in plan:
            if kind == "unit":
                product[a["u"]] = (chunk_used, a["c"] + 1)
            elif kind == "branch" or (kind == "outproj" and a["q"] == 1):
                m = TT * len(a.get("halves", (0,)))
                for i in range(m - 1):
                    n_unit_done += 1
                    product[a["u"] + i] = (unit_done, n_unit_done)
                product[a["u"] + m - 1] = (chunk_used, a["c"] + 1)

        chunk_of = {(kind, a["p"]): a["c"] for kind, a in plan if kind in ("gate", "up", "down")}

        def read_count(u):
            return sum(g == gunits[u] for g in gunits[:u + 1])

        def wait_bank(eng, u):
            if u >= 2:
                eng.wait_ge(unit_act if gunits[u - 2] == "act" else unit_dve, read_count(u - 2))

        n_tr = 0
        for kind, a in plan:
            if kind == "xt":
                a["tr"] = n_tr
                n_tr += KT // 2
            elif kind == "merged":
                a["tr"] = n_tr
                n_tr += KT // 2
            elif kind == "unit":
                for name, i in a["ex"]:
                    if name == "ht":
                        a.setdefault("tr", {})[i] = n_tr
                        n_tr += 1

        def view(t, n, kt):
            return t[:, 0:n * kt].rearrange("p (k n) -> p k n", k=kt)

        new, n_rstd, seen = {}, {}, 0
        for kind, a in plan:
            if kind == "stats":
                seen += 1
                n_rstd[a["n"]] = seen
            elif kind == "xt":
                new[a["src"]] = a["tr"]
                a["rstd"] = n_rstd[0 if a["src"] == "mem" else a["n"]]
            elif kind in ("unit", "gate"):
                a["fresh"] = new.pop(a.get("src", "x"), None)

        def gain_col(n, k):
            i = NCW + (n % 3 * L + n // 3) * KT + k
            return cw[:, i:i + 1]

        def ht_src(i):
            if i < 2:
                return hx, [2 * i, 2 * i + 1], hxT, 2 * i
            if i < 4:
                return hm, [2 * i - 4, 2 * i - 3], hmT, 2 * i - 4
            return hd, [0, 1], hdT, 0

        block = ctx.enter_context(nc.Block())

        def evac(l, kind, i=None):
            found = [a["u"] for k_, a in plan if k_ == "unit" and a["l"] == l and a["to"][0] == kind
                     and (i is None or a["to"][1] == i)]
            return read_count(found[-1])

        tr_norm = {a["n"]: a["tr"] for k_, a in plan if k_ == "xt"}
        tr_out = [a["tr"][4] for k_, a in plan if k_ == "unit" and 4 in a.get("tr", {})]
        tr_merged = [a["tr"] for k_, a in plan if k_ == "merged"]
        slots_mem = 2 * MH
        mixes = XH + MH + DHG

        @block.sync
        def _(eng):
            for t in range(TT):
                eng.dma_start(mem[:, t, :], mem_in[0, t * P:(t + 1) * P, :]).then_inc(mem_loaded[t], 16)
            eng.dma_start(cwn[0:NCW, :], conv_qk.rearrange("l j (c p) -> (l j c) p", p=P)).then_inc(consts_loaded, 16)
            for i, g in enumerate((norm_mem, norm_mix, norm_ffn)):
                eng.dma_start(cwn[NCW + i * L * KT:NCW + (i + 1) * L * KT, :], g.rearrange("l (c p) -> (l c) p", p=P))\
                    .then_inc(consts_loaded, 16)
            for c, (src, kt, n) in enumerate(chunks):
                if c == 2:
                    for t in range(TT):
                        eng.dma_start(x[:, t, :], x_in[0, t * P:(t + 1) * P, :]).then_inc(x_loaded[t], 16)
                if c >= RAW:
                    eng.wait_ge(chunk_used, c - RAW + 1)
                eng.dma_start(view(raw[c % RAW], n, kt), src).then_inc(raw_loaded[c % RAW], 16)
            eng.wait_ge(merged_ready, 4 * L)

            def experts(r):
                with eng.Fori(0, E) as e:
                    for k, (kind, j, part) in enumerate(moe_chunks):
                        eng.wait_ge(chunk_used, e * EC + (NDC + r * E * EC + k - MRAW + 1))
                        w = {"g": moe_w_gate, "u": moe_w_up, "d": moe_w_down}[kind][0][bass.ds(e, 1)]
                        if kind == "d":
                            k0 = 4 * j + 2 * part
                            src = w[:, k0 * P:(k0 + 2) * P, 0:D]
                            dst = view(raw_moe[k % MRAW], D, 2)
                        else:
                            src = w[:, 4 * part * P:4 * (part + 1) * P, j * HC:(j + 1) * HC]
                            dst = view(raw_moe[k % MRAW], HC, 4)
                        eng.dma_start(dst, src.rearrange("e (t p) n -> p (e t) n", p=P))\
                           .then_inc(moe_loaded[k % MRAW], 16)

            experts(0)
            eng.wait_ge(flag_ready, 1)
            over = eng.value_load(flag[0:1, 0:1], min_val=0, max_val=1)
            with eng.If(over > 0):
                experts(1)
            for t in range(TT):
                eng.wait_ge(normed, TT + t + 1)
                eng.dma_start(out[0, t * P:(t + 1) * P, :], xn[:, t, :]).then_inc(out_stored, 16)
            eng.wait_ge(out_stored, 16 * TT)

        @block.gpsimd
        def _(eng):
            n = [0]

            def link(ins):
                n[0] += 1
                ins.then_inc(pool_seq, 1)
                eng.wait_ge(pool_seq, n[0])

            eng.dma_start(bif[:, :, :].rearrange("p l n -> p (l n)"),
                          b_gate_if.rearrange("l n -> (l n)").partition_broadcast(P)).then_inc(bif_loaded, 16)
            eng.dma_start(mln[:, :], mlstm_norm[0].partition_broadcast(P)).then_inc(mln_loaded, 16)
            link(eng.memset(ones[:, :], 1.0))
            link(eng.memset(maskT[:, :], 0.0))

            def select(dst, src, op, fill, base, pattern, cm):
                link(eng.affine_select(out=dst, in_=src, compare_op=op, fill=fill, base=base, pattern=pattern,
                                       channel_multiplier=cm))

            eng.affine_select(out=ident[:, :], in_=ones[:, :], compare_op=ALU.is_equal, fill=0.0, base=0, pattern=[[-1, P]],
                              channel_multiplier=1).then_inc(ident_made, 1)
            select(upper[:, :], ones[:, :], ALU.is_ge, 0.0, 0, [[1, P]], -1)
            select(upper_s[:, :], ones[:, :], ALU.is_ge, 0.0, -1, [[1, P]], -1)
            select(dmask[:, 0, 0:P], maskT[:, :], ALU.is_ge, NEG, 0, [[-1, P]], 1)
            select(dmask[:, 0, 2 * P:3 * P], maskT[:, :], ALU.is_ge, NEG, 0, [[-1, P]], 1)
            select(dmask[:, 0, P:2 * P], maskT[:, :], ALU.is_ge, NEG, 0, [[1, P]], -1)
            select(maskT[:, :], maskT[:, :], ALU.is_ge, NEG, 0, [[1, P]], -1)
            select(lt[:, :, :], ones[:, 0:E * E].rearrange("p (a b) -> p a b", a=E), ALU.is_ge, 0.0, -1,
                   [[1, E], [-1, E]], 0)
            link(eng.iota(slots[:, :, :], [[P, 2], [1, P]], base=0, channel_multiplier=0,
                          allow_small_or_imprecise_dtypes=True))
            link(eng.iota(diff[:, :], [[-1, P]], base=0, channel_multiplier=1))
            link(eng.memset(vaug[:, :, :, MD:MD + 1], 1.0))
            link(eng.memset(vaug[:, :, :, MD + 1:VA], 0.0))
            eng.memset(tab[:, E, :], 1e6).then_inc(consts_made, 1)
            eng.wait_ge(masks_made, 1)
            for g in range(1, DG):
                select(dmask[:, g, 0:P], resid[:, g - 1, :], ALU.is_ge, NEG, 0, [[-1, P]], 1)
                select(dmask[:, g, 2 * P:3 * P], resid[:, g - 1, :], ALU.is_ge, NEG, 0, [[-1, P]], 1)
                last = eng.tensor_copy(dmask[:, g, P:2 * P], resid[:, g - 1, :])
                if g < DG - 1:
                    link(last)
            last.then_inc(consts_made, 1)
            for l in range(1, L):
                eng.wait_ge(merged_ready, 4 * l)
                eng.dma_start(mem[:, :, :], mem_in[0].rearrange("(t p) n -> p t n", p=P)).then_inc(mem_reloaded, 16)
                eng.wait_ge(hm_ready, l)
                eng.dma_start(mln[:, :], mlstm_norm[l].partition_broadcast(P)).then_inc(mln_loaded, 16)
            eng.wait_ge(tr_psum, tr_out[L - 1] + 1)
            eng.dma_start(gain[:, :], norm_ffn[L - 1].partition_broadcast(P)).then_inc(gain_loaded, 16)
            eng.wait_ge(normed, TT)
            eng.dma_start(gain[:, :], norm_final.partition_broadcast(P)).then_inc(gain_loaded, 16)

        @block.scalar
        def _(eng):
            n = [0]

            def link(ins):
                n[0] += 1
                ins.then_inc(act_seq, 1)
                eng.wait_ge(act_seq, n[0])

            def act(dst, src, func=ACT.Copy, **kw):
                return eng.activation(dst, src, func, **kw)

            def split_hi(c):
                if c >= NDC:
                    split_hi_moe(0, 0, c - NDC)
                    return
                kt, n_ = chunks[c][1:]
                eng.wait_ge(raw_loaded[c % RAW], 16 * (c // RAW + 1))
                if c >= HI:
                    eng.wait_ge(chunk_used, c - HI + 1)
                act(hi[c % HI][:, 0:kt * n_], raw[c % RAW][:, 0:kt * n_]).then_inc(hi_done, 1)

            def split_hi_moe(r, e, m):
                eng.wait_ge(moe_loaded[m % MRAW], e * (16 * EC // MRAW) + 16 * (m // MRAW + 1 + r * E * EC // MRAW))
                eng.wait_ge(chunk_used, e * EC + (NDC + r * E * EC + m - MHI + 1))
                act(hi_moe[m % MHI][:, :], raw_moe[m % MRAW][:, :]).then_inc(hi_done, 1)

            def transposed_hi(tr, bank, dst):
                eng.wait_ge(tr_psum, tr + 1)
                act(dst, ps[:, bank, :]).then_inc(tr_hi, 1)

            def xt(a):
                dst = mthi if a["src"] == "mem" else xthi
                for q in range(KT // 2):
                    eng.wait_ge(tr_psum, a["tr"] + q + 1)
                    for i in range(2):
                        last = act(dst[:, 2 * q + i, :], ps[:, 4 + q, i * S:(i + 1) * S], scale=gain_col(a["n"], 2 * q + i))
                    last.then_inc(tr_hi, 1)

            def unit(a):
                (kind, i), l, u = a["to"], a["l"], a["u"]
                eng.wait_ge(*product[u])
                src = ps[:, u % 2, :]
                fm2 = src.rearrange("p (f s) -> p f s", f=2)
                cols = slice(i * UC, (i + 1) * UC)
                if kind in ("km", "qx", "qd", "kd"):
                    dst = {"km": kmT, "qx": qx, "qd": qd, "kd": kd}[kind]
                    act(dst[:, 2 * i:2 * i + 2, :], fm2).then_inc(unit_act, 1)
                elif kind in ("vm", "vd"):
                    act({"vm": vm, "vd": vd}[kind][:, :, cols], fm2).then_inc(unit_act, 1)
                elif kind == "vml":
                    act(vaug[:, :, 2 * i:2 * i + 2, 0:MD],
                        src.rearrange("p (t h d) -> p t h d", t=TT, h=2)).then_inc(unit_act, 1)
                elif kind in ("qm", "km2"):
                    ci = i + 2 * (kind == "km2")
                    if ci >= 2:
                        eng.wait_ge(conv_acc, 4 * l + ci - 1)
                    act(convx[:, ci % 2, :, 3:3 + S], fm2).then_inc(unit_act, 1)
                elif kind == "om":
                    act(so[:, :, cols], fm2, ACT.Tanh, scale=0.5).then_inc(unit_act, 1)
                elif kind == "g":
                    b, q = i // 4, i % 4
                    act(gates[:, b, :, q * UC:(q + 1) * UC], fm2, ACT.Tanh, scale=0.5).then_inc(unit_act, 1)
                else:
                    w, dst = (2 * MH, ifr) if kind == "if" else (E, lg)
                    act(dst[:, :, :], src[:, 0:TT * w].rearrange("p (t n) -> p t n", t=TT)).then_inc(unit_act, 1)
                if kind == "if":
                    eng.wait_ge(if_neg, l + 1)
                    link(act(ef[:, :, :], nab[:, :, :], ACT.Exp))
                    act(ef[:, :, :], ef[:, :, :], ACT.Ln, bias=1.0).then_inc(if_ln, 1)
                if kind == "route":
                    eng.wait_ge(route_sel, 1)
                    act(eg[:, :, :], eg[:, :, :], ACT.Exp).then_inc(route_exp, 1)
                for name, k in a["ex"]:
                    extra(name, k, l, a)

            def extra(name, k, l, a):
                pt = slots_mem * l + k + (XH if name[0] == "d" else 0)
                mix = mixes * l + k + {"m": 0, "d": XH + MH}.get(name[0], 0)
                if name == "memA":
                    eng.wait_ge(max_mem, XH * l + k + 1)
                    for t in range(TT):
                        last = act(probs[:, k % 2, 0:2, :].rearrange("p a b -> p (a b)")[:, t * NM:(t + 1) * NM],
                                   ps[:, 2 + k % 2, t * NM:(t + 1) * NM], ACT.Exp, scale=XD ** -0.5,
                                   bias=nb[:, k % 2, t:t + 1], accum_out=den[:, k % 2, t:t + 1])
                    last.then_inc(p_mem, 1)
                elif name == "memC":
                    eng.wait_ge(pt_psum, pt + 1)
                    if mix:
                        eng.wait_ge(mix_psum, mix)
                    act(probsT[:, :, :].rearrange("p a b -> p (a b)")[:, 0:4 * P], ps[:, 5, :]).then_inc(pt_ready, 1)
                elif name == "conv":
                    eng.wait_ge(conv_acc, 4 * l + k + 1)
                    act(convt[:, k % 2, :], convy[:, k % 2, :], ACT.Tanh, scale=0.5).then_inc(conv_tanh, 1)
                elif name == "brow":
                    eng.wait_ge(em_in, l + 1)
                    act(em[:, :, :], fm[:, :, :], ACT.Exp, scale=-1.0).then_inc(em_ready, 1)
                elif name == "mrow":
                    eng.wait_ge(rows_read, 2 * l + 2)
                    for h in range(MH):
                        act(wml[:, h, 0:S], wml[:, h, 0:S], ACT.Exp, bias=bb[:, 0, h:h + 1])
                        last = act(wml[:, h, S:S + P], wml[:, h, S:S + P], ACT.Exp, bias=bb[:, 1, h:h + 1])
                    last.then_inc(wml_ready, 1)
                elif name == "dR":
                    eng.wait_ge(max_d, DHG * l + k + 1)
                    for t, cols in enumerate((slice(0, P), slice(P, 3 * P))):
                        last = act(probs[:, k % 2, :, cols], probs[:, k % 2, :, cols], ACT.Exp, scale=DD ** -0.5,
                                   bias=nb[:, k % 2, t:t + 1], accum_out=den[:, k % 2, t:t + 1])
                    last.then_inc(p_d, 1)
                elif name == "dT":
                    eng.wait_ge(pt_psum, pt + 1)
                    eng.wait_ge(mix_psum, mix)
                    act(probsT[:, :, :], ps[:, 5:8, 0:3 * P]).then_inc(pt_ready, 1)
                elif name == "ht":
                    _, _, dst, k0 = ht_src(k)
                    transposed_hi(a["tr"][k], 5 + k % 2, dst[0][:, k0:k0 + 2, :].rearrange("p k s -> p (k s)"))

            for kind, a in plan:
                if "c" in a:
                    split_hi(a["c"] + AHEAD)
                if kind == "split":
                    split_hi(a["m"])
                elif kind == "xt":
                    xt(a)
                elif kind == "merged":
                    for q in range(KT // 2):
                        transposed_hi(a["tr"] + q, 4 + q, xthi[:, 2 * q:2 * q + 2, :].rearrange("p k s -> p (k s)"))
                elif kind == "unit":
                    unit(a)
                elif kind == "gate":
                    p = a["p"]
                    eng.wait_ge(chunk_used, a["c"] + 1)
                    if p >= 2:
                        eng.wait_ge(hid_done, p - 1)
                    act(sg[:, p % 2, :], ps[:, (2 * p) % 4, :], ACT.Silu).then_inc(silu_done, 1)
                elif kind == "up":
                    p = a["p"]
                    eng.wait_ge(hid_done, p + 1)
                    if p >= 2:
                        eng.wait_ge(chunk_used, chunk_of["down", p - 2] + 1)
                    act(hThi[:, p % 2, :], hh[:, p % 2, :]).then_inc(hid_hi, 1)

            def hidden_hi(r, e, j):
                eng.wait_ge(m_tp, e * NJ + (r * E * NJ + j + 1))
                act(hThi[:, j % 2, :], ps[:, 4 + j % 2, :]).then_inc(m_thi, 1)

            def gathered_hi(r, e):
                eng.wait_ge(m_gath, e + (r * (E + 1) + 1))
                act(xehi[:, :, :].rearrange("p k s -> p (k s)"), ps[:, 2:4, :].rearrange("p a b -> p (a b)"))\
                    .then_inc(m_xehi, 1)

            def experts(r):
                for m in range(0 if r else AHEAD, MAHEAD):
                    split_hi_moe(r, 0, m)
                gathered_hi(r, 0)
                with eng.Fori(0, E) as e:
                    for k, (kind, j, part) in enumerate(moe_chunks):
                        if k + MAHEAD < EC:
                            split_hi_moe(r, e, k + MAHEAD)
                        else:
                            with eng.If(e < E - 1):
                                split_hi_moe(r, e, k + MAHEAD)
                        if kind == "g" and part == 1:
                            eng.wait_ge(chunk_used, e * EC + (NDC + r * E * EC + k + 1))
                            if j >= 2:
                                eng.wait_ge(m_hid, e * NJ + (r * E * NJ + j - 1))
                            act(sg[:, j % 2, :], ps[:, 2 * (j % 2), :], ACT.Silu).then_inc(m_silu, 1)
                            if j:
                                hidden_hi(r, e, j - 1)
                        if kind == "u" and part == 1 and j == 1:
                            eng.wait_ge(m_putp, e + (r * E + 1))
                            act(put[:, :, :].rearrange("p t s -> p (t s)"), ps[:, 5, 0:TT * P]).then_inc(m_put, 1)
                        if k == EC - 3:
                            hidden_hi(r, e, NJ - 1)
                            gathered_hi(r, e + 1)
                    eng.wait_ge(chunk_used, e * EC + (NDC + (r * E + 1) * EC))
                    act(ye[:, :], ps[:, 6:8, :].rearrange("p a b -> p (a b)")).then_inc(m_y, 1)

            experts(0)
            eng.wait_ge(flag_ready, 1)
            over = eng.value_load(flag[0:1, 0:1], min_val=0, max_val=1)
            with eng.If(over > 0):
                experts(1)

        @block.tensor
        def _(eng):
            def mm3(dst, a, b, first, last):
                eng.matmul(dst, a[0], b[0], start=first, stop=False)
                eng.matmul(dst, a[0], b[1], start=False, stop=False)
                return eng.matmul(dst, a[1], b[0], start=False, stop=last)

            def mm(dst, pairs):
                for i, (a, b) in enumerate(pairs):
                    last = eng.matmul(dst, a, b, start=i == 0, stop=i == len(pairs) - 1)
                return last

            def parts(pair, *index):
                return tuple(t[index] for t in pair)

            XT = (xthi, xtlo)

            def weights(c):
                kt, n_ = chunks[c][1:]
                return view(hi[c % HI], n_, kt), view(lo[c % RAW], n_, kt)

            def transposes(bank, src, ks):
                for i, k in enumerate(ks):
                    for t in range(TT):
                        last = eng.transpose(ps[:, bank, (i * TT + t) * P:(i * TT + t + 1) * P],
                                             src[:, t, k * P:(k + 1) * P], ident[:, :])
                last.then_inc(tr_psum, 1)

            def xt_part(a, first, k):
                if first and k % 2 == 0 and a.get("fresh") is not None:
                    eng.wait_ge(tr_lo, a["fresh"] + k // 2 + 1)

            def unit(a):
                c, u, l = a["c"], a["u"], a["l"]
                kt, n_ = chunks[c][1:]
                w = weights(c)
                wait_bank(eng, u)
                xT = (mthi, mtlo) if a["src"] == "mem" else XT
                if a["form"] == "F":
                    for f in range(n_ // P):
                        for k in range(kt):
                            xt_part(a, f == 0, k)
                            last = mm3(ps[:, u % 2, f * S:(f + 1) * S], parts(w, slice(None), k, slice(f * P, (f + 1) * P)),
                                       parts(xT, slice(None), k), k == 0, k == kt - 1)
                else:
                    for t in range(TT):
                        for k in range(kt):
                            xt_part(a, t == 0, k)
                            last = mm3(ps[:, u % 2, t * n_:(t + 1) * n_], parts(xT, slice(None), k, slice(t * P, (t + 1) * P)),
                                       parts(w, slice(None), k), k == 0, k == kt - 1)
                last.then_inc(chunk_used, 1)
                for name, k in a["ex"]:
                    extra(name, k, l, a)

            def extra(name, k, l, a):
                pt = slots_mem * l + k + (XH if name[0] == "d" else 0)
                mix = mixes * l + k + {"m": XH if name[:2] == "ml" else 0, "d": XH + MH}.get(name[0], 0)
                if name == "memA":
                    eng.wait_ge(unit_act, evac(l, "qx"))
                    if k >= 2:
                        eng.wait_ge(p_mem, XH * l + k - 1)
                    for t in range(TT):
                        last = mm(ps[:, 2 + k % 2, t * NM:(t + 1) * NM], [(qx[:, k, t * P:(t + 1) * P], kmT[:, k, :])])
                    last.then_inc(s_mem, 1)
                elif name == "memC":
                    eng.wait_ge(p_mem, XH * l + k + 1)
                    if pt:
                        eng.wait_ge(pt_ready, pt)
                    pv = probs[:, k % 2, 0:2, :].rearrange("p a b -> p (a b)")
                    for i in range(4):
                        last = eng.transpose(ps[:, 5, i * P:(i + 1) * P], pv[:, i * P:(i + 1) * P], ident[:, :])
                    last.then_inc(pt_psum, 1)
                elif name == "memE":
                    eng.wait_ge(pt_ready, pt + 1)
                    if mix:
                        eng.wait_ge(mix_read, mix)
                    tv = probsT[:, :, :].rearrange("p a b -> p (a b)")
                    for t in range(TT):
                        last = mm(ps[:, 4, t * P:(t + 1) * P],
                                  [(tv[:, (2 * t + m) * P:(2 * t + m + 1) * P], vm[:, m, k * XD:(k + 1) * XD])
                                   for m in range(2)])
                    last.then_inc(mix_psum, 1)
                elif name == "cum":
                    eng.wait_ge(logf, l + 1)
                    mm(ps[:, 7, 0:MH], [(upper[:, :], lf[:, 0, :])])
                    mm(ps[:, 7, MH:2 * MH], [(ones[:, :], lf[:, 0, :]), (upper[:, :], lf[:, 1, :])]).then_inc(cum_psum, 1)
                elif name in ("brow", "mrow"):
                    n_ = 2 * l + (name == "mrow")
                    eng.wait_ge(diag_ready, n_ + 1)
                    eng.wait_ge(pt_ready, slots_mem * l + XH)
                    if n_:
                        eng.wait_ge(rows_read, n_)
                    for t in range(TT):
                        last = mm(ps[:, 5 + t, :], [(ones[:, :], diag[:, t, :, :].rearrange("p h j -> p (h j)"))])
                    last.then_inc(rows_psum, 1)
                elif name == "mlA":
                    eng.wait_ge(conv_done, 4 * (l + 1))
                    if k >= 2:
                        eng.wait_ge(sw_ml, MH * l + k - 1)
                    mm(ps[:, 2 + k % 2, 0:S], [(qk[:, MH + k, 0:P], qk[:, k, :])])
                    mm(ps[:, 2 + k % 2, S:S + P], [(qk[:, MH + k, P:S], qk[:, k, P:S])]).then_inc(s_ml, 1)
                elif name == "mlE":
                    eng.wait_ge(sw_ml, MH * l + k + 1)
                    eng.wait_ge(unit_act, evac(l, "vml"))
                    eng.wait_ge(mix_read, mix)
                    sw = probs[:, k % 2, 0, :]
                    mm(ps[:, 4, 0:VA], [(sw[:, 0:P], vaug[:, 0, k, :])])
                    mm(ps[:, 4, VA:2 * VA], [(sw[:, P:S], vaug[:, 0, k, :]), (sw[:, S:S + P], vaug[:, 1, k, :])])\
                        .then_inc(mix_psum, 1)
                elif name in ("dS", "dR"):
                    o, tile = (k % 2) * DD, k // 2
                    if name == "dS":
                        eng.wait_ge(unit_act, evac(l, "kd"))
                        eng.wait_ge(sw_ml, MH * (l + 1))
                        if k:
                            eng.wait_ge(d_masked, DG * (DHG * l + k))
                    else:
                        eng.wait_ge(d_masked, DG * (DHG * l + k) + 1)
                    for g in ((0, 1) if name == "dS" else (2,)):
                        q_, k_ = qd[o:o + DD, 2 * g + tile, :], kd[o:o + DD, 2 * g + tile, :]
                        mm(ps[:, 2 + g % 2, 0:P], [(q_[:, 0:P], k_[:, 0:P])])
                        mm(ps[:, 2 + g % 2, P:3 * P], [(q_[:, P:S], k_)]).then_inc(s_d, 1)
                elif name == "dT":
                    eng.wait_ge(p_d, DHG * l + k + 1)
                    eng.wait_ge(pt_ready, pt)
                    if not k:
                        eng.wait_ge(rows_read, 2 * l + 2)
                    for b in range(3):
                        for g in range(DG):
                            last = eng.transpose(ps[:, 5 + b, g * P:(g + 1) * P],
                                                 probs[:, k % 2, g, b * P:(b + 1) * P], ident[:, :])
                    last.then_inc(pt_psum, 1)
                elif name == "dE":
                    eng.wait_ge(pt_ready, pt + 1)
                    eng.wait_ge(mix_read, mix)
                    v_ = [[vd[:, t, g * DHG * DD + k * DD:g * DHG * DD + (k + 1) * DD] for g in range(DG)] for t in range(TT)]
                    pT = [[probsT[:, b, g * P:(g + 1) * P] for g in range(DG)] for b in range(3)]
                    mm(ps[:, 4, 0:DD], [(pT[0][g], v_[0][g]) for g in range(DG)])
                    mm(ps[:, 4, DD:2 * DD], [(pT[1 + t][g], v_[t][g]) for t in range(TT) for g in range(DG)])\
                        .then_inc(mix_psum, 1)
                elif name == "ht":
                    src, ks, _, _ = ht_src(k)
                    if k == 0:
                        eng.wait_ge(pt_ready, slots_mem * (l + 1))
                    if k < 2:
                        eng.wait_ge(mix_read, mixes * l + XH)
                    elif k < 4:
                        eng.wait_ge(hm_ready, l + 1)
                    else:
                        eng.wait_ge(mix_read, mixes * (l + 1))
                    if k >= 2:
                        eng.wait_ge(tr_lo, a["tr"][k] - 1)
                    transposes(5 + k % 2, src, ks)

            def normed_transposes(a):
                src, rd = (mem, rdm) if a["src"] == "mem" else (x, rdx)
                eng.wait_ge(rstd_ready, a["rstd"])
                if a["src"] == "mem":
                    if a["n"]:
                        eng.wait_ge(mem_reloaded, 16 * (a["n"] // 3))
                    else:
                        for t in range(TT):
                            eng.wait_ge(mem_loaded[t], 16)
                if a["tr"]:
                    eng.wait_ge(tr_lo, a["tr"])
                if a["n"] == 4:
                    eng.wait_ge(y_read, 4)
                for q in range(KT // 2):
                    for i in range(2):
                        for t in range(TT):
                            last = eng.matmul(ps[:, 4 + q, (i * TT + t) * P:(i * TT + t + 1) * P],
                                              src[:, t, (2 * q + i) * P:(2 * q + i + 1) * P], rd[:, t, :],
                                              start=True, stop=True)
                    last.then_inc(tr_psum, 1)

            eng.wait_ge(ident_made, 1)
            eng.wait_ge(consts_loaded, 64)
            eng.transpose(ps[:, 3, 0:NROWS], cwn[:, :], ident[0:NROWS, 0:NROWS]).then_inc(cw_psum, 1)
            for kind, a in plan:
                l = a.get("l")
                if kind == "xt":
                    normed_transposes(a)
                elif kind == "merged":
                    eng.wait_ge(tr_lo, a["tr"])
                    for q in range(KT // 2):
                        eng.wait_ge(merged_ready, 4 * a["l"] + 2 * (q // 2 + 1))
                        transposes(4 + q, merged, (2 * q, 2 * q + 1))
                if "c" not in a:
                    continue
                c = a["c"]
                eng.wait_ge(lo_done, c + 1)
                w = weights(c)
                if kind == "unit":
                    unit(a)
                elif kind == "branch":
                    hT = (hmT, hdT, hxT)[a["b"]]
                    eng.wait_ge(tr_lo, tr_merged[l])
                    for i, h in enumerate(a["halves"]):
                        for t in range(TT):
                            u = a["u"] + TT * i + t
                            wait_bank(eng, u)
                            for k in range(a["kt"]):
                                last = mm3(ps[:, u % 2, :], parts(hT, slice(None), k, slice(t * P, (t + 1) * P)),
                                           parts(w, slice(None), k, slice(i * HC, (i + 1) * HC)), k == 0, k == a["kt"] - 1)
                            last.then_inc(chunk_used if product[u][0] is chunk_used else unit_done, 1)
                elif kind == "outproj":
                    for t in range(TT):
                        u = a["u"] + t
                        if a["q"] == 0:
                            wait_bank(eng, u)
                        for k in range(4):
                            if a["h"] == 0 and t == 0 and k % 2 == 0:
                                eng.wait_ge(tr_lo, tr_merged[l] + 2 * a["q"] + k // 2 + 1)
                            last = mm3(ps[:, u % 2, :], parts(XT, slice(None), 4 * a["q"] + k, slice(t * P, (t + 1) * P)),
                                       parts(w, slice(None), k), a["q"] == 0 and k == 0, a["q"] == 1 and k == 3)
                        if a["q"] == 1 and t == 0:
                            last.then_inc(unit_done, 1)
                    last.then_inc(chunk_used, 1)
                elif kind in ("gate", "up"):
                    p = a["p"]
                    if p >= 2:
                        eng.wait_ge(silu_done if kind == "gate" else hid_done, p - 1)
                    b = (2 * p + (kind == "up")) % 4
                    for f in range(2):
                        for k in range(KT):
                            xt_part(a, f == 0, k)
                            last = mm3(ps[:, b, f * S:(f + 1) * S], parts(w, slice(None), k, slice(f * P, (f + 1) * P)),
                                       parts(XT, slice(None), k), k == 0, k == KT - 1)
                    last.then_inc(chunk_used, 1)
                elif kind == "down":
                    p = a["p"]
                    eng.wait_ge(hid_lo, p + 1)
                    if p == 0:
                        eng.wait_ge(tr_lo, tr_norm[3] + KT // 2)
                    for f in range(2):
                        for t in range(TT):
                            hT = parts((hThi, hTlo), slice(None), p % 2, slice(f * S + t * P, f * S + (t + 1) * P))
                            for h in range(2):
                                last = mm3(ps[:, 4 + 2 * t + h, :], hT, parts(w, slice(None), f, slice(h * HC, (h + 1) * HC)),
                                           p == 0 and f == 0, p == NP_ - 1 and f == 1)
                    last.then_inc(chunk_used, 1)

            eng.wait_ge(route_sel, 1)
            mm(ps[:, 7, 0:E], [(upper_s[:, :], sel[:, 0, :])])
            mm(ps[:, 7, E:2 * E], [(ones[:, :], sel[:, 0, :]), (upper_s[:, :], sel[:, 1, :])])
            mm(ps[:, 7, 2 * E:3 * E], [(ones[:, :], sel[:, 0, :]), (ones[:, :], sel[:, 1, :])]).then_inc(route_pos, 1)

            def gather(r, e, first=False):
                eng.wait_ge(m_pick, e + (r * (E + 1) + 1))
                if first:
                    eng.wait_ge(normed, TT)
                for k in range(KT):
                    last = mm(ps[:, 2 + k // 4, (k % 4) * P:(k % 4 + 1) * P],
                              [(xn[:, t, k * P:(k + 1) * P], pick[:, t, :]) for t in range(TT)])
                last.then_inc(m_gath, 1)

            def scatter(r, e):
                eng.wait_ge(m_y, e + (r * (E + 1) + 1))
                eng.wait_ge(m_put, e + (r * (E + 1) + 1))
                for i in range(4):
                    t, h = i // 2, i % 2
                    if i >= 2:
                        eng.wait_ge(m_added, e * 4 + (r * (E + 1) * 4 + i - 1))
                    mm(ps[:, 4 + i % 2, :], [(put[:, t, :], ye[:, h * HC:(h + 1) * HC])]).then_inc(m_scat, 1)

            def hidden_T(r, e, j):
                eng.wait_ge(m_hid, e * NJ + (r * E * NJ + j + 1))
                for i in range(4):
                    last = eng.transpose(ps[:, 4 + j % 2, i * P:(i + 1) * P], hh[:, j % 2, i * P:(i + 1) * P], ident[:, :])
                last.then_inc(m_tp, 1)

            def experts_all(r):
                gather(r, 0, first=True)
                with eng.Fori(0, E) as e:
                    eng.wait_ge(m_xelo, e + (r * (E + 1) + 1))
                    for k in range(EC):
                        expert_chunk(r, e, k)
                        if k == EC - 3:
                            eng.wait_ge(m_tlo, e * NJ + (r * E * NJ + NJ - 2))
                            hidden_T(r, e, NJ - 1)
                            gather(r, e + 1)
                scatter(r, E)

            def expert_chunk(r, e, k):
                kind, j, part = moe_chunks[k]
                eng.wait_ge(lo_done, e * EC + (NDC + r * E * EC + k + 1))
                if kind == "d":
                    w = view(hi_moe[k % MHI], D, 2), view(lo_moe[k % MRAW], D, 2)
                    if part == 0:
                        eng.wait_ge(m_tlo, e * NJ + (r * E * NJ + j + 1))
                    for i in range(2):
                        kk = 2 * part + i
                        hT = parts((hThi, hTlo), slice(None), j % 2, slice(kk * P, (kk + 1) * P))
                        for h in range(2):
                            last = mm3(ps[:, 6 + h, :], hT, parts(w, slice(None), i, slice(h * HC, (h + 1) * HC)),
                                       j == 0 and kk == 0, j == NJ - 1 and kk == 3)
                    last.then_inc(chunk_used, 1)
                    return
                w = view(hi_moe[k % MHI], HC, 4), view(lo_moe[k % MRAW], HC, 4)
                if part == 0 and j >= 2:
                    eng.wait_ge(m_silu if kind == "g" else m_hid, e * NJ + (r * E * NJ + j - 1))
                b = 2 * (j % 2) + (kind == "u")
                for i in range(4):
                    kk = 4 * part + i
                    last = mm3(ps[:, b, :], (xehi[:, kk, :], xelo[:, kk, :]), parts(w, slice(None), i), kk == 0, kk == KT - 1)
                last.then_inc(chunk_used, 1)
                if part == 0:
                    return
                if kind == "g" and j == 0:
                    scatter(r, e)
                elif kind == "g":
                    if j == 1:
                        eng.wait_ge(m_added, e * 4 + (r * (E + 1) * 4 + 3))
                    elif j == 2:
                        eng.wait_ge(m_put, e + (r * (E + 1) + 2))
                    else:
                        eng.wait_ge(m_tlo, e * NJ + (r * E * NJ + j - 2))
                    hidden_T(r, e, j - 1)
                elif j == 1:
                    eng.wait_ge(m_added, e * 4 + (r * (E + 1) * 4 + 4))
                    for t in range(TT):
                        last = eng.transpose(ps[:, 5, t * P:(t + 1) * P], pickg[:, t, :], ident[:, :])
                    last.then_inc(m_putp, 1)

            experts_all(0)
            eng.wait_ge(flag_ready, 1)
            over = eng.value_load(flag[0:1, 0:1], min_val=0, max_val=1)
            with eng.If(over > 0):
                experts_all(1)

        @block.vector
        def _(eng):
            n = [0]

            def link(ins):
                n[0] += 1
                ins.then_inc(dve_seq, 1)
                eng.wait_ge(dve_seq, n[0])

            tt, ts, stt = eng.tensor_tensor, eng.tensor_scalar, eng.scalar_tensor_tensor

            def split_lo(c):
                if c >= NDC:
                    split_lo_moe(0, 0, c - NDC)
                    return
                kt, n_ = chunks[c][1:]
                eng.wait_ge(hi_done, c + 1)
                tt(lo[c % RAW][:, 0:kt * n_], raw[c % RAW][:, 0:kt * n_], hi[c % HI][:, 0:kt * n_].bitcast(f32),
                   ALU.subtract).then_inc(lo_done, 1)

            def split_lo_moe(r, e, m):
                eng.wait_ge(hi_done, e * EC + (NDC + r * E * EC + m + 1))
                tt(lo_moe[m % MRAW][:, :], raw_moe[m % MRAW][:, :], hi_moe[m % MHI][:, :].bitcast(f32), ALU.subtract)\
                    .then_inc(lo_done, 1)

            def transposed_lo(tr, bank, dst, hi_):
                eng.wait_ge(tr_hi, tr + 1)
                tt(dst, ps[:, bank, :], hi_.bitcast(f32), ALU.subtract).then_inc(tr_lo, 1)

            def rsqrt(r, v, t, ti):
                link(ts(ti, v.bitcast(i32), 1, None, ALU.logical_shift_right))
                link(ts(r.bitcast(i32), ti, -1.0, float(0x5F3759DF), ALU.mult, ALU.add))
                for _ in range(3):
                    link(tt(t, r, r, ALU.mult))
                    link(stt(t, t, -0.5, v, ALU.mult, ALU.mult))
                    link(stt(r, t, 1.5, r, ALU.add, ALU.mult))

            def mean_square(src, t, h, junk=xn):
                cols = slice(h * HC, (h + 1) * HC)
                return eng.tensor_tensor_reduce(junk[:, t, cols], src[:, t, cols], src[:, t, cols], 1.0 / D, EPS / 2,
                                                ALU.mult, ALU.add, ss[:, t, h:h + 1])

            def row_scale():
                link(tt(var[:, :], ss[:, :, 0], ss[:, :, 1], ALU.add))
                rsqrt(rstd[:, :], var[:, :], nt[:, :], nti[:, :])

            def stats(n_):
                src, rd = (mem, rdm) if n_ == 0 else (x, rdx)
                if n_ % 3 != 2:
                    for t in range(TT):
                        if n_ < 2:
                            eng.wait_ge((x_loaded if n_ else mem_loaded)[t], 16)
                        for h in range(2):
                            last = mean_square(src, t, h)
                    link(last)
                row_scale()
                for t in range(TT):
                    last = ts(rd[:, t, :], ident[:, :], rstd[:, t:t + 1], None, ALU.mult)
                last.then_inc(rstd_ready, 1)

            def xt(a):
                hi_, lo_ = (mthi, mtlo) if a["src"] == "mem" else (xthi, xtlo)
                for q in range(KT // 2):
                    eng.wait_ge(tr_hi, a["tr"] + q + 1)
                    for i in range(2):
                        k = 2 * q + i
                        last = stt(lo_[:, k, :], ps[:, 4 + q, i * S:(i + 1) * S], gain_col(a["n"], k), hi_[:, k, :].bitcast(f32),
                                   ALU.mult, ALU.subtract)
                    last.then_inc(tr_lo, 1)

            def normed_rows(i):
                eng.wait_ge(gain_loaded, 16 * (i + 1))
                for t in range(TT):
                    stt(xn[:, t, :], x[:, t, :], rstd[:, t:t + 1], gain[:, :], ALU.mult, ALU.mult).then_inc(normed, 1)

            def conv(l, ci, u):
                eng.wait_ge(unit_act, read_count(u))
                for j in (3, 2, 1, 0):
                    for f in range(2):
                        y = convy[:, ci % 2, f * S:(f + 1) * S]
                        xx = convx[:, ci % 2, f, j:j + S]
                        row = (l * 4 + j) * 8 + 2 * ci + f
                        if j == 3:
                            last = ts(y, xx, cw[:, row:row + 1], None, ALU.mult)
                        else:
                            last = stt(y, xx, cw[:, row:row + 1], y, ALU.mult, ALU.add)
                    if j:
                        link(last)
                last.then_inc(conv_acc, 1)

            def diags(src):
                for t in range(TT):
                    for h in range(MH):
                        last = ts(diag[:, t, h, :], ident[:, :], src[:, t, h:h + 1], None, ALU.mult)
                last.then_inc(diag_ready, 1)

            def unit(a):
                (kind, i), l, u = a["to"], a["l"], a["u"]
                cols = slice(i * UC, (i + 1) * UC)
                if kind in ("qm", "km2"):
                    conv(l, i + 2 * (kind == "km2"), u)
                elif kind == "om":
                    eng.wait_ge(unit_act, read_count(u))
                    link(ts(so[:, :, cols], so[:, :, cols], 0.5, 0.5, ALU.mult, ALU.add))
                elif kind == "g":
                    eng.wait_ge(unit_act, read_count(u))
                    v = gates[:, i // 4, :, (i % 4) * UC:(i % 4 + 1) * UC]
                    ts(v, v, 0.5, 0.5, ALU.mult, ALU.add).then_inc(gate_done, 1)
                elif kind == "if":
                    eng.wait_ge(unit_act, read_count(u))
                    link(eng.memset(convx[:, :, :, 0:3], 0.0))
                    if l == 0:
                        eng.wait_ge(bif_loaded, 16)
                    link(tt(ifb[:, :, :], ifr[:, :, :], bif[:, l:l + 1, :].broadcast_to([P, TT, 2 * MH]), ALU.add))
                    f_ = ifb[:, :, MH:2 * MH]
                    stt(nab[:, :, :], f_, -1.0, f_, ALU.mult, ALU.min).then_inc(if_neg, 1)
                    eng.wait_ge(if_ln, l + 1)
                    stt(lf[:, :, :], f_, 0.0, ef[:, :, :], ALU.min, ALU.subtract).then_inc(logf, 1)
                elif kind == "route":
                    route(u)
                for name, k in a["ex"]:
                    extra(name, k, l, a)

            def extra(name, k, l, a):
                mix = mixes * l + k + {"m": XH if name[:2] == "ml" else 0, "d": XH + MH}.get(name[0], 0)
                if name == "memA":
                    eng.wait_ge(s_mem, XH * l + k + 1)
                    link(eng.tensor_reduce(mx[:, k % 2, :], ps[:, 2 + k % 2, :].rearrange("p (t n) -> p t n", t=TT), AX.X, ALU.max))
                    ts(nb[:, k % 2, :], mx[:, k % 2, :], -(XD ** -0.5), None, ALU.mult).then_inc(max_mem, 1)
                elif name in ("memE", "dE"):
                    eng.wait_ge(mix_psum, mix + 1)
                    link(eng.reciprocal(rec[:, :], den[:, k % 2, :]))
                    dst, w_ = (hx, XD) if name == "memE" else (hd, DD)
                    for t in range(TT):
                        last = ts(dst[:, t, k * w_:(k + 1) * w_], ps[:, 4, t * w_:(t + 1) * w_], rec[:, t:t + 1], None, ALU.mult)
                    last.then_inc(mix_read, 1)
                elif name == "conv":
                    eng.wait_ge(conv_tanh, 4 * l + k + 1)
                    link(ts(convt[:, k % 2, :], convt[:, k % 2, :], 0.5, 0.5, ALU.mult, ALU.add))
                    tt(qk[:, 2 * k:2 * k + 2, :].rearrange("p f s -> p (f s)"), convy[:, k % 2, :], convt[:, k % 2, :],
                       ALU.mult).then_inc(conv_done, 1)
                elif name == "cum":
                    eng.wait_ge(cum_psum, l + 1)
                    link(eng.tensor_copy(cumf[:, :, :].rearrange("p t h -> p (t h)"), ps[:, 7, 0:TT * MH]))
                    link(tt(bb[:, :, :], ifb[:, :, 0:MH], cumf[:, :, :], ALU.subtract))
                    diags(bb)
                elif name == "brow":
                    eng.wait_ge(rows_psum, 2 * l + 1)
                    heads = [ps[:, 5 + t, :].rearrange("p (h j) -> p h j", h=MH) for t in range(TT)]
                    cm = dmask[:, 0:1, 0:P].broadcast_to([P, MH, P])
                    tt(wml[:, :, 0:P], heads[0], cm, ALU.add)
                    link(tt(wml[:, :, P:2 * P], heads[1], cm, ALU.add))
                    eng.tensor_reduce(m2[:, 1, :], heads[0], AX.X, ALU.max).then_inc(rows_read, 1)
                    eng.tensor_reduce(mm_[:, 0, :], wml[:, :, 0:P], AX.X, ALU.max)
                    link(eng.tensor_reduce(m2[:, 0, :], wml[:, :, P:2 * P], AX.X, ALU.max))
                    link(tt(mm_[:, 1, :], m2[:, 0, :], m2[:, 1, :], ALU.max))
                    tt(fm[:, :, :], cumf[:, :, :], mm_[:, :, :], ALU.add).then_inc(em_in, 1)
                    link(ts(ngm[:, :, :], mm_[:, :, :], -1.0, None, ALU.mult))
                    diags(ngm)
                elif name == "mrow":
                    eng.wait_ge(rows_psum, 2 * l + 2)
                    heads = [ps[:, 5 + t, :].rearrange("p (h j) -> p h j", h=MH) for t in range(TT)]
                    cm = maskT[:, :].unsqueeze(1).broadcast_to([P, MH, P])
                    tt(wml[:, :, 0:P], heads[0], cm, ALU.add)
                    eng.tensor_copy(wml[:, :, P:2 * P], heads[1])
                    tt(wml[:, :, 2 * P:3 * P], heads[1], cm, ALU.add).then_inc(rows_read, 1)
                elif name == "mlA":
                    eng.wait_ge(s_ml, MH * l + k + 1)
                    eng.wait_ge(wml_ready, l + 1)
                    stt(probs[:, k % 2, 0, :], ps[:, 2 + k % 2, 0:3 * P], MD ** -0.5, wml[:, k, :], ALU.mult, ALU.mult)\
                        .then_inc(sw_ml, 1)
                elif name == "mlE":
                    eng.wait_ge(mix_psum, mix + 1)
                    eng.wait_ge(em_ready, l + 1)
                    link(eng.tensor_copy(dn[:, :], ps[:, 4, MD:2 * VA:VA]))
                    link(stt(dn[:, :], dn[:, :], -1.0, dn[:, :], ALU.mult, ALU.max))
                    link(tt(dn[:, :], dn[:, :], em[:, :, k], ALU.max))
                    link(eng.reciprocal(rec[:, :], dn[:, :]))
                    for t in range(TT):
                        last = ts(hraw[:, t, k, :], ps[:, 4, t * VA:t * VA + MD], rec[:, t:t + 1], None, ALU.mult)
                    last.then_inc(mix_read, 1)
                    eng.wait_ge(mix_read, mix + 1)
                    for t in range(TT):
                        link(eng.bn_stats(st[:, :], hraw[:, t, k, :]))
                        link(eng.bn_aggr(mv[:, t * MH + k, :], st[:, :]))
                elif name == "mlF":
                    link(ts(v8[:, :], mv[:, :, 1], EPS, None, ALU.add))
                    rsqrt(r8[:, :], v8[:, :], n8[:, :], ni8[:, :])
                    eng.wait_ge(mln_loaded, 16 * (l + 1))
                    for t in range(TT):
                        for h in range(MH):
                            i = t * MH + h
                            last = ts(hm[:, t, h * MD:(h + 1) * MD], hraw[:, t, h, :], mv[:, i, 0:1], r8[:, i:i + 1],
                                      ALU.subtract, ALU.mult)
                    link(last)
                    link(tt(hm[:, :, :], hm[:, :, :], mln[:, :].unsqueeze(1).broadcast_to([P, TT, MW]), ALU.mult))
                    tt(hm[:, :, :], hm[:, :, :], so[:, :, :], ALU.mult).then_inc(hm_ready, 1)
                elif name in ("dS", "dR"):
                    eng.wait_ge(consts_made, 2)
                    for g in ((0, 1) if name == "dS" else (2,)):
                        eng.wait_ge(s_d, DG * (DHG * l + k) + g + 1)
                        tt(probs[:, k % 2, g, :], ps[:, 2 + g % 2, 0:3 * P], dmask[:, g, :], ALU.add).then_inc(d_masked, 1)
                    if name == "dR":
                        eng.wait_ge(d_masked, DG * (DHG * l + k + 1))
                        eng.tensor_reduce(mx[:, k % 2, 0:1], probs[:, k % 2, :, 0:P], AX.XY, ALU.max)
                        link(eng.tensor_reduce(mx[:, k % 2, 1:2], probs[:, k % 2, :, P:3 * P], AX.XY, ALU.max))
                        ts(nb[:, k % 2, :], mx[:, k % 2, :], -(DD ** -0.5), None, ALU.mult).then_inc(max_d, 1)
                elif name == "ht":
                    _, _, dst, k0 = ht_src(k)
                    transposed_lo(a["tr"][k], 5 + k % 2, *(dst[i][:, k0:k0 + 2, :].rearrange("p k s -> p (k s)") for i in (1, 0)))

            def route(u):
                eng.wait_ge(unit_act, read_count(u))
                for t in range(TT):
                    link(eng.tensor_reduce(m1[:, t:t + 1], lg[:, t, :], AX.X, ALU.max))
                    others = lg[:, t, :].unsqueeze(1).broadcast_to([P, E, E])
                    own = lg[:, t, :].unsqueeze(2).broadcast_to([P, E, E])
                    tt(gt[:, :, :], others, own, ALU.is_gt)
                    link(tt(eq[:, :, :], others, own, ALU.is_equal))
                    link(tt(eq[:, :, :], eq[:, :, :], lt[:, :, :], ALU.mult))
                    link(tt(gt[:, :, :], gt[:, :, :], eq[:, :, :], ALU.add))
                    link(eng.tensor_reduce(cnt[:, t, :], gt[:, :, :], AX.X, ALU.add))
                    link(ts(eg[:, t, :], lg[:, t, :], m1[:, t:t + 1], None, ALU.subtract))
                ts(sel[:, :, :], cnt[:, :, :], 1.5, None, ALU.is_lt).then_inc(route_sel, 1)
                eng.wait_ge(route_sel, 1)
                eng.wait_ge(route_exp, 1)
                link(tt(eg[:, :, :], eg[:, :, :], sel[:, :, :], ALU.mult))
                link(eng.tensor_reduce(dg[:, :], eg[:, :, :], AX.X, ALU.add))
                link(eng.reciprocal(dg[:, :], dg[:, :]))
                eng.wait_ge(route_pos, 1)
                link(ts(cnt[:, :, :], sel[:, :, :], -1e6, 1e6, ALU.mult, ALU.add))
                link(tt(posm[:, :, :], ps[:, 7, 0:TT * E].rearrange("p (t e) -> p t e", t=TT), cnt[:, :, :], ALU.add))
                for t in range(TT):
                    eng.tensor_copy(tab[:, 0:E, t], posm[:, t, :])
                    link(ts(tab[:, 0:E, 2 + t], eg[:, t, :], dg[:, t:t + 1], None, ALU.mult))
                link(eng.tensor_reduce(tmx[:, :], ps[:, 7, 2 * E:3 * E], AX.X, ALU.max))
                ts(flag[:, :], tmx[:, :], float(P) + 0.5, None, ALU.is_gt).then_inc(flag_ready, 1)

            eng.wait_ge(cw_psum, 1)
            eng.tensor_copy(cw[:, :], ps[:, 3, 0:NROWS]).then_inc(cw_ready, 1)
            eng.wait_ge(cw_ready, 1)
            for kind, a in plan:
                l = a.get("l")
                if "c" in a:
                    split_lo(a["c"] + AHEAD)
                if kind == "split":
                    split_lo(a["m"])
                elif kind == "stats":
                    stats(a["n"])
                    if a["n"] == 1:
                        eng.wait_ge(consts_made, 1)
                        for g, dil in enumerate((4, 16)):
                            link(ts(diffm[:, g, :], diff[:, :], dil - 1, None, ALU.bitwise_and))
                            link(eng.tensor_copy(resid[:, g, :], diffm[:, g, :]))
                            link(ts(resid[:, g, :], resid[:, g, :], 0.5, NEG, ALU.is_gt, ALU.mult))
                        eng.memset(mx[:, :, :], 0.0).then_inc(masks_made, 1)
                elif kind == "xt":
                    xt(a)
                    if a["n"] == 3 * L - 1:
                        normed_rows(0)
                elif kind == "merged":
                    for q in range(KT // 2):
                        transposed_lo(a["tr"] + q, 4 + q, *(t[:, 2 * q:2 * q + 2, :].rearrange("p k s -> p (k s)")
                                                            for t in (xtlo, xthi)))
                elif kind == "unit":
                    unit(a)
                elif kind == "branch":
                    b = a["b"]
                    if b == 0:
                        eng.wait_ge(gate_done, 12 * (l + 1))
                        eng.wait_ge(tr_psum, tr_merged[l])
                    for i, h in enumerate(a["halves"]):
                        for t in range(TT):
                            u = a["u"] + TT * i + t
                            cols = slice(h * HC, (h + 1) * HC)
                            g_ = gates[:, b, t, cols]
                            eng.wait_ge(*product[u])
                            dst = merged[:, t, cols] if b == 0 else g_
                            tt(dst, ps[:, u % 2, :], g_, ALU.mult).then_inc(unit_dve, 1)
                            eng.wait_ge(unit_dve, read_count(u))
                            if b:
                                last = tt(merged[:, t, cols], merged[:, t, cols], g_, ALU.add)
                                if b == 2:
                                    last.then_inc(merged_ready, 1)
                                else:
                                    link(last)
                elif kind == "outproj" and a["q"] == 1:
                    for t in range(TT):
                        u = a["u"] + t
                        eng.wait_ge(*product[u])
                        cols = slice(a["h"] * HC, (a["h"] + 1) * HC)
                        tt(x[:, t, cols], ps[:, u % 2, :], x[:, t, cols], ALU.add).then_inc(unit_dve, 1)
                        eng.wait_ge(unit_dve, read_count(u))
                        link(mean_square(x, t, a["h"]))
                elif kind == "up":
                    p = a["p"]
                    eng.wait_ge(chunk_used, a["c"] + 1)
                    eng.wait_ge(silu_done, p + 1)
                    tt(hh[:, p % 2, :], ps[:, (2 * p + 1) % 4, :], sg[:, p % 2, :], ALU.mult).then_inc(hid_done, 1)
                    eng.wait_ge(hid_done, p + 1)
                    eng.wait_ge(hid_hi, p + 1)
                    tt(hTlo[:, p % 2, :], hh[:, p % 2, :], hThi[:, p % 2, :].bitcast(f32), ALU.subtract).then_inc(hid_lo, 1)
                elif kind == "ffn_end":
                    eng.wait_ge(chunk_used, chunk_of["down", NP_ - 1] + 1)
                    for t in range(TT):
                        for h in range(2):
                            cols = slice(h * HC, (h + 1) * HC)
                            tt(x[:, t, cols], ps[:, 4 + 2 * t + h, :], x[:, t, cols], ALU.add).then_inc(y_read, 1)
                    eng.wait_ge(y_read, 4)

            def picks(r, e):
                eng.tensor_copy(cur[:, :].unsqueeze(1), tab[:, bass.ds(e, 1), :]).then_inc(m_cur, 1)
                eng.wait_ge(m_cur, e + (r * (E + 1) + 1))
                for t in range(TT):
                    ts(pickg[:, t, :], slots[:, r, :], cur[:, t:t + 1], cur[:, 2 + t:3 + t], ALU.is_equal, ALU.mult)
                for t in range(TT):
                    last = ts(pick[:, t, :], slots[:, r, :], cur[:, t:t + 1], None, ALU.is_equal)
                last.then_inc(m_pick, 1)

            def gathered_lo(r, e):
                eng.wait_ge(m_xehi, e + (r * (E + 1) + 1))
                tt(xelo[:, :, :].rearrange("p k s -> p (k s)"), ps[:, 2:4, :].rearrange("p a b -> p (a b)"),
                   xehi[:, :, :].rearrange("p k s -> p (k s)").bitcast(f32), ALU.subtract).then_inc(m_xelo, 1)

            def hidden_lo(r, e, j):
                eng.wait_ge(m_thi, e * NJ + (r * E * NJ + j + 1))
                tt(hTlo[:, j % 2, :], ps[:, 4 + j % 2, :], hThi[:, j % 2, :].bitcast(f32), ALU.subtract).then_inc(m_tlo, 1)

            def scattered(r, e, last=False):
                for i in range(4):
                    t, h = i // 2, i % 2
                    eng.wait_ge(m_scat, e * 4 + (r * (E + 1) * 4 + i + 1))
                    cols = slice(h * HC, (h + 1) * HC)
                    tt(x[:, t, cols], ps[:, 4 + i % 2, :], x[:, t, cols], ALU.add).then_inc(m_added, 1)
                    if last:
                        eng.wait_ge(m_added, (r + 1) * (E + 1) * 4 - 3 + i)
                        mean_square(x, t, h, junk).then_inc(m_squares, 1)

            def experts(r):
                eng.memset(ye[:, :], 0.0).then_inc(m_y, 1)
                eng.memset(put[:, :, :], 0.0).then_inc(m_put, 1)
                picks(r, 0)
                for m in range(0 if r else AHEAD, MAHEAD):
                    split_lo_moe(r, 0, m)
                gathered_lo(r, 0)
                with eng.Fori(0, E) as e:
                    for k, (kind, j, part) in enumerate(moe_chunks):
                        if k + MAHEAD < EC:
                            split_lo_moe(r, e, k + MAHEAD)
                        else:
                            with eng.If(e < E - 1):
                                split_lo_moe(r, e, k + MAHEAD)
                        if kind == "g" and part == 1:
                            if j == 0:
                                scattered(r, e)
                            else:
                                hidden_lo(r, e, j - 1)
                            if j == 3:
                                picks(r, e + 1)
                        if kind == "u" and part == 1:
                            eng.wait_ge(chunk_used, e * EC + (NDC + r * E * EC + k + 1))
                            eng.wait_ge(m_silu, e * NJ + (r * E * NJ + j + 1))
                            tt(hh[:, j % 2, :], ps[:, 2 * (j % 2) + 1, :], sg[:, j % 2, :], ALU.mult).then_inc(m_hid, 1)
                        if k == EC - 3:
                            hidden_lo(r, e, NJ - 1)
                            gathered_lo(r, e + 1)
                scattered(r, E, last=True)
                eng.wait_ge(m_squares, 4 * (r + 1))

            experts(0)
            eng.wait_ge(flag_ready, 1)
            over = eng.value_load(flag[0:1, 0:1], min_val=0, max_val=1)
            with eng.If(over > 0):
                experts(1)
            row_scale()
            normed_rows(1)


_INS = ['x', 'mem', 'norm_mix', 'w_in', 'conv_qk', 'b_gate_if', 'mlstm_norm', 'norm_mem', 'w_mem_kv', 'w_br_m', 'w_br_d',
        'w_br_x', 'w_out', 'norm_ffn', 'ffn_w_gate', 'ffn_w_up', 'ffn_w_down', 'moe_router', 'moe_w_gate', 'moe_w_up',
        'moe_w_down', 'norm_final']


def kernel(**inputs):
    import numpy as _np
    import concourse.bacc as _bacc
    from concourse import mybir as _mybir
    from concourse.bass_utils import run_bass_kernel_spmd as _run

    nc = _bacc.Bacc("TRN2", target_bir_lowering=False, num_devices=1)
    arrays, args = {}, []
    for name in _INS:
        a = _np.ascontiguousarray(inputs[name])
        arrays[f"in_{name}_dram"] = a
        args.append(nc.dram_tensor(f"in_{name}_dram", a.shape, _mybir.dt.from_np(a.dtype), kind="ExternalInput").ap())
    shape = arrays["in_x_dram"].shape
    args.append(nc.dram_tensor("out_0_dram", shape, _mybir.dt.float32, kind="ExternalOutput").ap())
    hybrid_trunk(nc, *args)
    r = _run(nc, [arrays], core_ids=[0])
    return r.results[0]["out_0_dram"]
```

```python
import concourse.bass as bass
from concourse import mybir
from contextlib import ExitStack


def hybrid_trunk(nc: bass.Bass, x_in, mem_in, norm_mix, w_in, conv_qk, b_gate_if, mlstm_norm, norm_mem,
                 w_mem_kv, w_br_m, w_br_d, w_br_x, w_out, norm_ffn, ffn_w_gate, ffn_w_up, ffn_w_down,
                 moe_router, moe_w_gate, moe_w_up, moe_w_down, norm_final, out):
    f32, f32r, i32 = mybir.dt.float32, mybir.dt.float32r, mybir.dt.int32
    ALU, ACT, AX = mybir.AluOpType, mybir.ActivationFunctionType, mybir.AxisListType

    P = 128
    S, D = x_in.shape[1], x_in.shape[2]
    L = w_in.shape[0]
    TT, KT = S // P, D // P
    NM = mem_in.shape[1]
    MH, MD = 4, 128
    MW = MH * MD
    XH, XD = 4, 128
    XW = XH * XD
    DG, DHG, DD = 3, 4, 64
    DW = DG * DHG * DD
    E = moe_router.shape[2]
    FF = ffn_w_gate.shape[2]
    FE = moe_w_gate.shape[3]
    EPS, NEG = 1e-6, -1e30
    assert TT == 2 and NM == S and MD == P and XD == P and E == 2 * MH == 8

    C_QM, C_KM, C_VM, C_OM = 0, MW, 2 * MW, 3 * MW
    C_IF = 4 * MW
    C_QD = C_IF + 2 * MH
    C_VD = C_QD + 2 * DW
    C_QX = C_VD + DW
    C_G = C_QX + XW

    CH = 2048
    UC = CH // KT
    RAW, HI = 5, 4
    MRAW, MHI = 7, 7
    AHEAD, MAHEAD = 3, 3
    HC = 512

    def rows(w, k0, nk, c0, nc_):
        return w[k0 * P:(k0 + nk) * P, c0:c0 + nc_].rearrange("(t p) n -> p t n", p=P)

    chunks = []

    def chunk(w, k0, nk, c0, n):
        chunks.append((rows(w, k0, nk, c0, n), nk, n))
        return len(chunks) - 1

    plan = []

    def step(kind, **a):
        plan.append((kind, a))

    def mixer_plan(l):
        mem = w_mem_kv[l]
        units = [(i * UC, "F", ("km", i)) for i in range(XW // UC)] + [(XW + i * UC, "T", ("vm", i)) for i in range(XW // UC)]
        for i, (c0, form, to) in enumerate(units):
            step("unit", c=chunk(mem, 0, KT, c0, UC), form=form, to=to, l=l, ex=[], src="mem")
            if i == 0:
                step("stats", n=3 * l + 1)
            if i == 2:
                step("xt", n=3 * l + 1, src="x")
        w = w_in[l]
        units = []

        def add(kind, c0, width, form):
            for i in range(width // UC):
                units.append((c0 + i * UC, UC, form, (kind, i)))

        add("qx", C_QX, XW, "F")
        units.append((C_IF, 2 * MH, "T", ("if", 0)))
        add("qm", C_QM, MW, "F")
        add("km2", C_KM, MW, "F")
        add("vml", C_VM, MW, "T")
        add("qd", C_QD, DW, "F")
        q0, q1, k0, k1, v0, v1, d0, *rest = units[3:]
        units[3:] = [q0, v0, q1, v1, k0, d0, k1, *rest]
        add("kd", C_QD + DW, DW, "F")
        add("om", C_OM, MW, "T")
        add("vd", C_VD, DW, "T")
        add("g", C_G, 3 * D, "T")
        extras = {
            2: [("memA", 0)], 3: [("memC", 0), ("cacc", 0)], 4: [("memE", 0), ("memA", 1), ("conv", 0)],
            5: [("memC", 1), ("cacc", 1)], 6: [("memE", 1), ("memA", 2), ("conv", 1)],
            7: [("memC", 2), ("cacc", 2)], 8: [("memE", 2), ("memA", 3), ("conv", 2)],
            9: [("memC", 3), ("cum", 0), ("cacc", 3)], 10: [("memE", 3), ("conv", 3)],
            11: [("brow", 0)], 12: [("mrow", 0)],
            14: [("mlA", 0)], 15: [("mlA", 1), ("mlE", 0)], 16: [("mlA", 2), ("mlE", 1)],
            17: [("mlA", 3), ("mlE", 2)], 18: [("mlE", 3), ("mlF", 0)],
            19: [("dS", 0)], 20: [("dR", 0)],
            21: [("dT", 0), ("dS", 1)], 22: [("dE", 0), ("dR", 1)],
            23: [("dT", 1), ("dS", 2)], 24: [("dE", 1), ("dR", 2)],
            25: [("dT", 2), ("dS", 3)], 26: [("dE", 2), ("dR", 3)],
            27: [("dT", 3)], 28: [("dE", 3)],
            29: [("ht", 4), ("ht", 2)], 30: [("ht", 3), ("ht", 0)], 31: [("ht", 1)],
        }
        for s, (c0, n, form, to) in enumerate(units):
            plan.append(("unit", dict(c=chunk(w, 0, KT, c0, n), form=form, to=to, l=l, ex=extras.pop(s, []), src="x")))
        assert not extras
        for pos, (b, wb, kt) in enumerate(((1, w_br_d[l], DHG * DD // P), (0, w_br_m[l], MW // P), (2, w_br_x[l], XW // P))):
            if kt * D <= CH:
                step("branch", c=chunk(wb, 0, kt, 0, D), b=b, pos=pos, kt=kt, halves=(0, 1), l=l)
            else:
                for h in range(2):
                    step("branch", c=chunk(wb, 0, kt, h * HC, HC), b=b, pos=pos, kt=kt, halves=(h,), l=l)
        step("merged", l=l)
        for h in range(2):
            for q in range(2):
                plan.append(("outproj", dict(c=chunk(w_out[l], 4 * q, 4, h * HC, HC), h=h, q=q, l=l)))
        step("stats", n=3 * l + 2)
        step("xt", n=3 * l + 2, src="x")

    NP_ = FF // UC

    step("stats", n=0)
    step("split", m=0)
    step("xt", n=0, src="mem")
    for m in range(1, AHEAD):
        step("split", m=m)
    mixer_plan(0)
    for p in range(NP_ + 1):
        if p < NP_:
            plan.append(("gate", dict(c=chunk(ffn_w_gate[0], 0, KT, p * UC, UC), p=p)))
            plan.append(("up", dict(c=chunk(ffn_w_up[0], 0, KT, p * UC, UC), p=p)))
        if p == 0:
            step("xt", n=3, src="mem")
        if p:
            plan.append(("down", dict(c=chunk(ffn_w_down[0], 2 * (p - 1), 2, 0, D), p=p - 1)))
    plan.append(("ffn_end", {}))
    mixer_plan(1)
    plan.append(("unit", dict(c=chunk(moe_router[0], 0, KT, 0, E), form="T", to=("route", 0), l=1, ex=[], src="x")))
    NDC = len(chunks)

    NJ = FE // HC
    moe_chunks = []
    for j in range(NJ):
        moe_chunks += [("g", j, 0), ("g", j, 1), ("u", j, 0), ("u", j, 1)]
        if j:
            moe_chunks += [("d", j - 1, 0), ("d", j - 1, 1)]
    moe_chunks += [("d", NJ - 1, 0), ("d", NJ - 1, 1)]
    EC = len(moe_chunks)
    assert EC % MRAW == 0 and EC % MHI == 0

    ctx = ExitStack()
    with ctx:
        base = (nc.sbuf_base + 31) // 32 * 32
        top = [base]

        def at(name, shape, dt=f32, off=None):
            size = 4
            for n in shape[1:]:
                size *= n
            if off is None:
                off = top[0]
                top[0] += (size + 31) // 32 * 32
            return nc.alloc_sbuf_tensor_at(name, shape, dt, offset=off)

        raw = [at(f"raw{i}", [P, CH]) for i in range(RAW)]
        lo = [at(f"w_lo{i}", [P, CH], f32r, off=base + i * CH * 4) for i in range(RAW)]
        hi = [at(f"w_hi{i}", [P, CH], f32r) for i in range(HI)]
        o_xthi = top[0]
        xthi = at("xT_hi", [P, KT, S], f32r)
        xtlo = at("xT_lo", [P, KT, S], f32r)
        o_x = top[0]
        x = at("x", [P, TT, D])
        xn = at("x_normed", [P, TT, D])
        gain = at("gain", [P, D])
        o_xn, o_gain = o_x + TT * D * 4, o_x + 2 * TT * D * 4
        g0 = top[0]
        gates = at("gates", [P, 3, TT, D])
        CW = S + 4
        convx = at("conv_x", [P, 2, 2, CW], off=g0)
        convy = at("conv_y", [P, 2, 2 * S], off=g0 + 4160)
        convt = at("conv_t", [P, 2, 2 * S], off=g0 + 8256)
        diag = at("diag", [P, TT, MH, P], off=g0 + 12352)
        wml = at("mlstm_w", [P, MH, 3 * P], off=g0 + 16448)
        mthi = at("memT_hi", [P, KT, NM], f32r, off=g0)
        mtlo = at("memT_lo", [P, KT, NM], f32r, off=g0 + KT * NM * 4)
        mem = at("mem", [P, TT, D], off=g0 + 2 * KT * NM * 4)
        VA = MD + 2
        o_vaug = top[0]
        vaug = at("v_aug", [P, TT, MH, VA])
        r1 = top[0]
        qk = at("qk_mT", [P, 2 * MH, S])
        hmT = [at("hmT_hi", [P, 4, S], f32r, off=r1), at("hmT_lo", [P, 4, S], f32r, off=r1 + 4 * S * 4)]
        r2 = top[0]
        qd = at("q_dT", [P, DW // P, S])
        kd = at("k_dT", [P, DW // P, S])
        qx = at("q_xT", [P, XH, S], off=r2)
        kmT = at("k_memT", [P, XH, NM], off=r2 + 4096)
        vm = at("v_mem", [P, TT, XW], off=r2 + 8192)
        hxT = [at("hxT_hi", [P, 4, S], f32r, off=r2), at("hxT_lo", [P, 4, S], f32r, off=r2 + 4096)]
        hdT = [at("hdT_hi", [P, 2, S], f32r, off=r2 + 8192), at("hdT_lo", [P, 2, S], f32r, off=r2 + 8192 + 2048)]
        so = at("sig_o", [P, TT, MW])
        vd = at("v_d", [P, TT, DW])
        probs = at("probs", [P, 2, 3, 3 * P])
        probsT = at("probsT", [P, 3, 3 * P])
        hraw = at("h_raw", [P, TT, MH, MD])
        top[0] = max(top[0], r1 + 52 * 1024)
        rawn = [at(f"raw_new{i}", [P, CH], off=g0 + i * CH * 4) for i in range(MRAW - RAW)]
        lon = [at(f"w_lo_new{i}", [P, CH], f32r, off=g0 + i * CH * 4) for i in range(MRAW - RAW)]
        hin = [at(f"w_hi_new{i}", [P, CH], f32r, off=o) for i, o in enumerate((g0 + 2 * CH * 4, r1 + 36864, r1 + 45056))]
        raw_moe = rawn + [raw[(NDC + i) % RAW] for i in range(RAW)]
        lo_moe = lon + [lo[(NDC + i) % RAW] for i in range(RAW)]
        hi_moe = hin + [hi[(NDC + i) % HI] for i in range(HI)]
        hm = at("h_m", [P, TT, MW], off=o_xn)
        hx = at("h_x", [P, TT, XW], off=o_xn + TT * MW * 4)
        hd = at("h_d", [P, TT, DHG * DD], off=o_xn + TT * D * 4)
        merged = at("merged", [P, TT, D], off=o_xn)
        f0 = r1 + 20480
        junk = at("junk", [P, TT, D], off=f0)
        sg = at("silu_g", [P, 2, HC], off=f0)
        hh = at("hidden", [P, 2, HC], off=f0 + 4096)
        hThi = at("hiddenT_hi", [P, 2, 4 * P], f32r, off=f0 + 8192)
        hTlo = at("hiddenT_lo", [P, 2, 4 * P], f32r, off=f0 + 12288)
        xehi = at("xe_hi", [P, KT, P], f32r, off=r1)
        xelo = at("xe_lo", [P, KT, P], f32r, off=r1 + 4096)
        yhi = at("y_hi", [P, D], f32r, off=r1 + 8192)
        ylo = at("y_lo", [P, D], f32r, off=r1 + 12288)
        pick = at("pick", [P, TT, P], f32r, off=r1 + 16384)
        put = at("put", [P, TT, P], f32r, off=r1 + 17408)
        gain_f = at("gain_final", [P, D], off=o_xthi + KT * S * 4)
        xnhi = [at(f"x_normed_hi{t}", [P, D], f32r, off=(o_vaug, o_gain)[t]) for t in range(TT)]
        xnlo = at("x_normed_lo", [P, TT, D], f32r, off=o_xn)
        dmask = at("dil_mask", [P, DG, 3 * P])
        maskT = at("causal_maskT", [P, P])
        ident = at("ident", [P, P])
        identr = at("ident_r", [P, P], f32r)
        ones = at("ones", [P, P])
        upper = at("upper", [P, P])
        upper_s = at("upper_strict", [P, P])
        slots = at("slots", [P, 2, P])
        resid = at("residue", [P, 2, P])
        diff = at("diff", [P, P], i32, off=r1)
        diffm = at("diff_masked", [P, 2, P], i32, off=r1 + 512)
        NCW, NROWS = L * 4 * 8, L * 4 * 8 + 3 * L * KT
        cwn = at("channel_rows", [NROWS, P], off=r1 + 2048)
        cw = at("channel_cols", [P, NROWS])
        rdm = at("rstd_diag_mem", [P, TT, P])
        rdx = at("rstd_diag_x", [P, TT, P])
        bif = at("b_if", [P, L, 2 * MH])
        mln = at("mlstm_gain", [P, MW])
        ss = at("mean_sq_halves", [P, TT, 2])
        var = at("var", [P, TT])
        nt = at("newton", [P, TT])
        nti = at("half_bits", [P, TT], i32)
        rstd = at("rstd", [P, TT])
        two = at("narrow_products", [P, TT, 2 * E])
        ifr = at("if_raw", [P, TT, 2 * MH])
        ifb = at("if_pre", [P, TT, 2 * MH])
        nab = at("neg_abs_f", [P, TT, MH])
        ef = at("exp_f", [P, TT, MH])
        lf = at("log_f", [P, TT, MH])
        cumf = at("cum_f", [P, TT, MH])
        bb = at("b", [P, TT, MH])
        mm_ = at("m_minus_f", [P, TT, MH])
        m2 = at("m2", [P, 2, MH])
        ngm = at("neg_m", [P, TT, MH])
        fm = at("m_row", [P, TT, MH])
        em = at("exp_neg_m", [P, TT, MH])
        den = at("den", [P, 2, 2])
        dn = at("den_abs", [P, 2])
        rec = at("rec", [P, 2])
        mx = at("row_max", [P, 2, 2])
        nb = at("neg_max", [P, 2, 2])
        st = at("bn", [P, 6])
        mv = at("mean_var", [P, TT * MH, 2])
        r8 = at("rstd8", [P, TT * MH])
        ni8 = at("half_bits8", [P, TT * MH], i32)
        v8 = at("var8", [P, TT * MH])
        n8 = at("newton8", [P, TT * MH])
        lg = at("logits", [P, TT, E])
        m1 = at("top1", [P, TT])
        gt = at("greater", [P, TT, E, E])
        eq = at("equal", [P, TT, E, E])
        lt = at("earlier", [P, E, E])
        cnt = at("rank", [P, TT, E])
        sel = at("selected", [P, TT, E])
        eg = at("exp_logits", [P, TT, E])
        dg = at("gate_den", [P, TT])
        posm = at("position", [P, TT, E])
        tmx = at("most_tokens", [P, 1])
        tab = at("route_table", [P, E + 1, TT])
        gtab = at("gate_table", [P, E + 1, TT, 2], f32r)
        geg = at("gates_e", [P, TT, E])
        warm = at("warm", [P, 1])
        cur = at("route_now", [P, TT])
        curg = at("gate_now", [P, TT, 2], f32r)
        gs2 = at("slot_gate_parts", [P, 2])
        gs = at("slot_gate", [P, 1])
        flag = at("overflow", [P, 1], i32)
        assert top[0] <= nc.sbuf_usable_end, (top[0], nc.sbuf_usable_end)

        ps = nc.alloc_psum_tensor("ps", [P, 8, HC], f32)

        def sem(name):
            return ctx.enter_context(nc.semaphore(name))

        raw_loaded = [sem(f"raw_loaded{i}") for i in range(RAW)]
        moe_loaded = [sem(f"moe_loaded{i}") for i in range(MRAW)]
        hi_done, lo_done, chunk_used = sem("hi_done"), sem("lo_done"), sem("chunk_used")
        ident_made, bif_loaded = sem("ident_made"), sem("gate_bias_loaded")
        consts_loaded, consts_made, masks_made = sem("consts_loaded"), sem("consts_made"), sem("masks_made")
        cw_psum, cw_ready = sem("conv_w_psum"), sem("conv_w_ready")
        x_loaded, mem_loaded = ([sem(f"{n_}_loaded{t}") for t in range(TT)] for n_ in ("x", "mem"))
        mem_reloaded = sem("mem_reloaded")
        gain_f_loaded = sem("final_gain_loaded")
        gain_loaded, mln_loaded = sem("gain_loaded"), sem("mlstm_gain_loaded")
        rstd_ready, normed = sem("rstd_diag_ready"), sem("normed")
        tr_psum, tr_hi, tr_lo = sem("transposed"), sem("transposed_hi"), sem("transposed_lo")
        unit_done, unit_act, unit_dve = sem("unit_done"), sem("unit_read_act"), sem("unit_read_dve")
        conv_acc, conv_tanh, conv_done = sem("conv_acc"), sem("conv_tanh"), sem("conv_done")
        gate_done = sem("gates_done")
        if_neg, if_ln, logf = sem("neg_abs_ready"), sem("softplus_ready"), sem("log_f_ready")
        cum_psum, diag_ready, rows_psum, rows_read = sem("cum_psum"), sem("diag_ready"), sem("rows_psum"), sem("rows_read")
        em_in, em_ready, wml_ready = sem("m_row_ready"), sem("exp_neg_m_ready"), sem("mlstm_w_ready")
        s_mem, s_ml, s_d = sem("mem_scores"), sem("mlstm_scores"), sem("dil_scores")
        max_mem, max_d, d_masked = sem("mem_max"), sem("dil_max"), sem("dil_masked")
        p_mem, p_d, sw_ml = sem("mem_probs"), sem("dil_probs"), sem("mlstm_weighted")
        pt_psum, pt_ready = sem("probsT_psum"), sem("probsT_ready")
        mix_psum, mix_read = sem("mix_psum"), sem("mix_read")
        hm_ready = sem("h_m_ready")
        act_seq, dve_seq, pool_seq = sem("act_seq"), sem("dve_seq"), sem("pool_seq")
        merged_ready = sem("merged_ready")
        m_cur = sem("moe_route_now")
        silu_done, hid_done, hid_hi, hid_lo, y_read = (
            sem(n) for n in ("silu_done", "hidden_done", "hidden_hi", "hidden_lo", "y_read"))
        route_exp, route_sel, route_pos, flag_ready = (
            sem(n) for n in ("route_exp", "route_selected", "route_pos", "flag_ready"))
        m_silu, m_hid, m_tp, m_thi, m_tlo = (
            sem("moe_" + n) for n in ("silu", "hidden", "hiddenT_psum", "hiddenT_hi", "hiddenT_lo"))
        m_pick, m_gath, m_xehi, m_xelo, m_putp, m_put, m_y, m_scat, m_added = (
            sem("moe_" + n) for n in ("pick", "gathered", "xe_hi", "xe_lo", "put_psum", "put", "y", "scattered", "added"))
        squares, m_squares = sem("mean_squares"), sem("moe_mean_squares")
        xn_hi, xn_lo = sem("x_normed_hi"), sem("x_normed_lo")
        m_gsp = sem("moe_slot_gate_parts")
        m_yhi, m_gs = sem("moe_y_hi"), sem("moe_slot_gate")
        out_stored = sem("out_stored")

        gunits = []
        for kind, a in plan:
            if kind == "unit":
                a["u"] = len(gunits)
                gunits.append("act")
            elif kind == "branch":
                a["u"] = len(gunits)
                gunits += ["dve"] * (TT * len(a["halves"]))
            elif kind == "outproj" and a["q"] == 0:
                a["u"] = len(gunits)
                gunits += ["dve"] * TT
            elif kind == "outproj":
                a["u"] = len(gunits) - TT

        product, n_unit_done = {}, 0
        for kind, a in plan:
            if kind == "unit":
                product[a["u"]] = (chunk_used, a["c"] + 1)
            elif kind == "branch" or (kind == "outproj" and a["q"] == 1):
                m = TT * len(a.get("halves", (0,)))
                for i in range(m - 1):
                    n_unit_done += 1
                    product[a["u"] + i] = (unit_done, n_unit_done)
                product[a["u"] + m - 1] = (chunk_used, a["c"] + 1)

        chunk_of = {(kind, a["p"]): a["c"] for kind, a in plan if kind in ("gate", "up", "down")}

        def read_count(u):
            return sum(g == gunits[u] for g in gunits[:u + 1])

        def wait_bank(eng, u):
            if u >= 2:
                eng.wait_ge(unit_act if gunits[u - 2] == "act" else unit_dve, read_count(u - 2))

        n_tr = 0
        for kind, a in plan:
            if kind == "xt":
                a["tr"] = n_tr
                n_tr += KT // 2
            elif kind == "merged":
                a["tr"] = n_tr
                n_tr += KT // 2
            elif kind == "unit":
                for name, i in a["ex"]:
                    if name == "ht":
                        a.setdefault("tr", {})[i] = n_tr
                        n_tr += 1

        def view(t, n, kt):
            return t[:, 0:n * kt].rearrange("p (k n) -> p k n", k=kt)

        new, n_rstd, seen = {}, {}, 0
        for kind, a in plan:
            if kind == "stats":
                seen += 1
                n_rstd[a["n"]] = seen
            elif kind == "xt":
                new[a["src"]] = a["tr"]
                a["rstd"] = n_rstd[0 if a["src"] == "mem" else a["n"]]
            elif kind in ("unit", "gate"):
                a["fresh"] = new.pop(a.get("src", "x"), None)

        def narrow(c):
            kt, n_ = chunks[c][1:]
            return hi[c % HI][:, 0:2 * kt * n_].rearrange("p (k b n) -> p k b n", k=kt, b=2)

        def gain_col(n, k):
            i = NCW + (n % 3 * L + n // 3) * KT + k
            return cw[:, i:i + 1]

        HT_ORDER = [4, 2, 3, 0, 1]
        HT_LAST = {1: 4, 0: 3, 2: 1}

        def ht_bank(i):
            return 5 + HT_ORDER.index(i) % 2

        def ht_src(i):
            if i < 2:
                return hx, [2 * i, 2 * i + 1], hxT, 2 * i
            if i < 4:
                return hm, [2 * i - 4, 2 * i - 3], hmT, 2 * i - 4
            return hd, [0, 1], hdT, 0

        block = ctx.enter_context(nc.Block())

        def evac(l, kind, i=None):
            found = [a["u"] for k_, a in plan if k_ == "unit" and a["l"] == l and a["to"][0] == kind
                     and (i is None or a["to"][1] == i)]
            return read_count(found[-1])

        tr_norm = {a["n"]: a["tr"] for k_, a in plan if k_ == "xt"}
        tr_ht = [{}, {}]
        for k_, a in plan:
            if k_ == "unit":
                tr_ht[a["l"]].update(a.get("tr", {}))
        tr_merged = [a["tr"] for k_, a in plan if k_ == "merged"]
        slots_mem = 2 * MH
        mixes = XH + MH + DHG

        @block.sync
        def _(eng):
            for t in range(TT):
                eng.dma_start(mem[:, t, :], mem_in[0, t * P:(t + 1) * P, :]).then_inc(mem_loaded[t], 16)
            eng.dma_start(cwn[0:NCW, :], conv_qk.rearrange("l j (c p) -> (l j c) p", p=P)).then_inc(consts_loaded, 16)
            for i, g in enumerate((norm_mem, norm_mix, norm_ffn)):
                eng.dma_start(cwn[NCW + i * L * KT:NCW + (i + 1) * L * KT, :], g.rearrange("l (c p) -> (l c) p", p=P))\
                    .then_inc(consts_loaded, 16)
            for c, (src, kt, n) in enumerate(chunks):
                if c == 2:
                    for t in range(TT):
                        eng.dma_start(x[:, t, :], x_in[0, t * P:(t + 1) * P, :]).then_inc(x_loaded[t], 16)
                if c >= RAW:
                    eng.wait_ge(chunk_used, c - RAW + 1)
                eng.dma_start(view(raw[c % RAW], n, kt), src).then_inc(raw_loaded[c % RAW], 16)
            eng.wait_ge(merged_ready, 4 * L)

            def experts(r):
                with eng.Fori(0, E) as e:
                    for k, (kind, j, part) in enumerate(moe_chunks):
                        eng.wait_ge(chunk_used, e * EC + (NDC + r * E * EC + k - MRAW + 1))
                        w = {"g": moe_w_gate, "u": moe_w_up, "d": moe_w_down}[kind][0][bass.ds(e, 1)]
                        if kind == "d":
                            k0 = 4 * j + 2 * part
                            src = w[:, k0 * P:(k0 + 2) * P, 0:D]
                            dst = view(raw_moe[k % MRAW], D, 2)
                        else:
                            src = w[:, 4 * part * P:4 * (part + 1) * P, j * HC:(j + 1) * HC]
                            dst = view(raw_moe[k % MRAW], HC, 4)
                        eng.dma_start(dst, src.rearrange("e (t p) n -> p (e t) n", p=P))\
                           .then_inc(moe_loaded[k % MRAW], 16)

            experts(0)
            eng.wait_ge(flag_ready, 1)
            over = eng.value_load(flag[0:1, 0:1], min_val=0, max_val=1)
            with eng.If(over > 0):
                experts(1)
            for i in range(2 * TT):
                t, cols = i // 2, slice(i % 2 * HC, (i % 2 + 1) * HC)
                eng.wait_ge(normed, 2 * TT + i + 1)
                eng.dma_start(out[0, t * P:(t + 1) * P, cols], xn[:, t, cols]).then_inc(out_stored, 16)
            eng.wait_ge(out_stored, 16 * 2 * TT)

        @block.gpsimd
        def _(eng):
            n = [0]

            def link(ins):
                n[0] += 1
                ins.then_inc(pool_seq, 1)
                eng.wait_ge(pool_seq, n[0])

            eng.dma_start(bif[:, :, :].rearrange("p l n -> p (l n)"),
                          b_gate_if.rearrange("l n -> (l n)").partition_broadcast(P)).then_inc(bif_loaded, 16)
            eng.dma_start(mln[:, :], mlstm_norm[0].partition_broadcast(P)).then_inc(mln_loaded, 16)
            link(eng.memset(ones[:, :], 1.0))
            link(eng.memset(maskT[:, :], 0.0))

            def select(dst, src, op, fill, base, pattern, cm):
                link(eng.affine_select(out=dst, in_=src, compare_op=op, fill=fill, base=base, pattern=pattern,
                                       channel_multiplier=cm))

            eng.affine_select(out=ident[:, :], in_=ones[:, :], compare_op=ALU.is_equal, fill=0.0, base=0, pattern=[[-1, P]],
                              channel_multiplier=1).then_inc(ident_made, 1)
            select(upper[:, :], ones[:, :], ALU.is_ge, 0.0, 0, [[1, P]], -1)
            select(upper_s[:, :], ones[:, :], ALU.is_ge, 0.0, -1, [[1, P]], -1)
            select(dmask[:, 0, 0:P], maskT[:, :], ALU.is_ge, NEG, 0, [[-1, P]], 1)
            select(dmask[:, 0, 2 * P:3 * P], maskT[:, :], ALU.is_ge, NEG, 0, [[-1, P]], 1)
            select(dmask[:, 0, P:2 * P], maskT[:, :], ALU.is_ge, NEG, 0, [[1, P]], -1)
            select(maskT[:, :], maskT[:, :], ALU.is_ge, NEG, 0, [[1, P]], -1)
            select(lt[:, :, :], ones[:, 0:E * E].rearrange("p (a b) -> p a b", a=E), ALU.is_ge, 0.0, -1,
                   [[1, E], [-1, E]], 0)
            link(eng.iota(slots[:, :, :], [[P, 2], [1, P]], base=0, channel_multiplier=0,
                          allow_small_or_imprecise_dtypes=True))
            link(eng.iota(diff[:, :], [[-1, P]], base=0, channel_multiplier=1))
            link(eng.memset(vaug[:, :, :, MD:MD + 1], 1.0))
            eng.memset(vaug[:, :, :, MD + 1:VA], 0.0).then_inc(consts_made, 1)
            eng.wait_ge(masks_made, 1)
            for g in range(1, DG):
                select(dmask[:, g, 0:P], resid[:, g - 1, :], ALU.is_ge, NEG, 0, [[-1, P]], 1)
                select(dmask[:, g, 2 * P:3 * P], resid[:, g - 1, :], ALU.is_ge, NEG, 0, [[-1, P]], 1)
                last = eng.tensor_copy(dmask[:, g, P:2 * P], resid[:, g - 1, :])
                if g < DG - 1:
                    link(last)
            last.then_inc(consts_made, 1)
            for l in range(1, L):
                eng.wait_ge(merged_ready, 4 * l)
                eng.dma_start(mem[:, :, :], mem_in[0].rearrange("(t p) n -> p t n", p=P)).then_inc(mem_reloaded, 16)
                eng.wait_ge(hm_ready, l)
                eng.dma_start(mln[:, :], mlstm_norm[l].partition_broadcast(P)).then_inc(mln_loaded, 16)
            eng.wait_ge(tr_psum, tr_ht[L - 1][4] + 1)
            eng.dma_start(gain[:, :], norm_ffn[L - 1].partition_broadcast(P)).then_inc(gain_loaded, 16)
            eng.wait_ge(merged_ready, 4 * L)
            eng.memset(yhi[:, :].bitcast(f32), 0.0)
            eng.memset(ylo[:, :].bitcast(f32), 0.0).then_inc(m_y, 2)
            eng.memset(put[:, :, :].bitcast(f32), 0.0).then_inc(m_put, 1)
            eng.wait_ge(chunk_used, NDC)
            eng.dma_start(gain_f[:, :], norm_final.partition_broadcast(P)).then_inc(gain_f_loaded, 16)

        @block.scalar
        def _(eng):
            n = [0]

            def link(ins):
                n[0] += 1
                ins.then_inc(act_seq, 1)
                eng.wait_ge(act_seq, n[0])

            def act(dst, src, func=ACT.Copy, **kw):
                return eng.activation(dst, src, func, **kw)

            def split_hi(c):
                if c >= NDC:
                    split_hi_moe(0, 0, c - NDC)
                    return
                kt, n_ = chunks[c][1:]
                eng.wait_ge(raw_loaded[c % RAW], 16 * (c // RAW + 1))
                if c >= HI:
                    eng.wait_ge(chunk_used, c - HI + 1)
                if n_ <= 2 * MH:
                    act(narrow(c)[:, :, 0, :], view(raw[c % RAW], n_, kt)).then_inc(hi_done, 1)
                    return
                act(hi[c % HI][:, 0:kt * n_], raw[c % RAW][:, 0:kt * n_]).then_inc(hi_done, 1)

            def split_hi_moe(r, e, m):
                eng.wait_ge(moe_loaded[m % MRAW], e * (16 * EC // MRAW) + 16 * (m // MRAW + 1 + r * E * EC // MRAW))
                eng.wait_ge(chunk_used, e * EC + (NDC + r * E * EC + m - MHI + 1))
                act(hi_moe[m % MHI][:, :], raw_moe[m % MRAW][:, :]).then_inc(hi_done, 1)

            def mean_square(scratch, t, h):
                cols = slice(h * HC, (h + 1) * HC)
                return act(scratch[:, t, cols], x[:, t, cols], ACT.Square, scale=D ** -0.5, accum_out=ss[:, t, h:h + 1])

            def transposed_hi(tr, bank, dst):
                eng.wait_ge(tr_psum, tr + 1)
                act(dst, ps[:, bank, :]).then_inc(tr_hi, 1)

            def xt(a):
                dst = mthi if a["src"] == "mem" else xthi
                if a["n"] == 0:
                    eng.wait_ge(cw_ready, 1)
                for q in range(KT // 2):
                    eng.wait_ge(tr_psum, a["tr"] + q + 1)
                    for i in range(2):
                        last = act(dst[:, 2 * q + i, :], ps[:, 4 + q, i * S:(i + 1) * S], scale=gain_col(a["n"], 2 * q + i))
                    last.then_inc(tr_hi, 1)

            def unit(a):
                (kind, i), l, u = a["to"], a["l"], a["u"]
                eng.wait_ge(*product[u])
                src = ps[:, u % 2, :]
                fm2 = src.rearrange("p (f s) -> p f s", f=2)
                cols = slice(i * UC, (i + 1) * UC)
                if kind in ("km", "qx", "qd", "kd"):
                    dst = {"km": kmT, "qx": qx, "qd": qd, "kd": kd}[kind]
                    act(dst[:, 2 * i:2 * i + 2, :], fm2).then_inc(unit_act, 1)
                elif kind in ("vm", "vd"):
                    act({"vm": vm, "vd": vd}[kind][:, :, cols], fm2).then_inc(unit_act, 1)
                elif kind == "vml":
                    act(vaug[:, :, 2 * i:2 * i + 2, 0:MD],
                        src.rearrange("p (t h d) -> p t h d", t=TT, h=2)).then_inc(unit_act, 1)
                elif kind in ("qm", "km2"):
                    ci = i + 2 * (kind == "km2")
                    if ci >= 2:
                        eng.wait_ge(conv_acc, 4 * l + ci - 1)
                    act(convx[:, ci % 2, :, 3:3 + S], fm2).then_inc(unit_act, 1)
                elif kind == "om":
                    act(so[:, :, cols], fm2, ACT.Tanh, scale=0.5).then_inc(unit_act, 1)
                elif kind == "g":
                    b, q = i // 4, i % 4
                    act(gates[:, b, :, q * UC:(q + 1) * UC], fm2, ACT.Tanh, scale=0.5).then_inc(unit_act, 1)
                else:
                    act(two[:, :, :], src[:, 0:2 * TT * E].rearrange("p (t n) -> p t n", t=TT)).then_inc(unit_act, 1)
                if kind == "if":
                    eng.wait_ge(if_neg, l + 1)
                    link(act(ef[:, :, :], nab[:, :, :], ACT.Exp))
                    act(ef[:, :, :], ef[:, :, :], ACT.Ln, bias=1.0).then_inc(if_ln, 1)
                if kind == "route":
                    eng.wait_ge(route_sel, 1)
                    act(eg[:, :, :], eg[:, :, :], ACT.Exp).then_inc(route_exp, 1)
                for name, k in a["ex"]:
                    extra(name, k, l, a)

            def extra(name, k, l, a):
                pt = slots_mem * l + k + (XH if name[0] == "d" else 0)
                mix = mixes * l + k + {"m": 0, "d": XH + MH}.get(name[0], 0)
                if name == "memA":
                    eng.wait_ge(max_mem, XH * l + k + 1)
                    for t in range(TT):
                        last = act(probs[:, k % 2, 0:2, :].rearrange("p a b -> p (a b)")[:, t * NM:(t + 1) * NM],
                                   ps[:, 2 + k % 2, t * NM:(t + 1) * NM], ACT.Exp, scale=XD ** -0.5,
                                   bias=nb[:, k % 2, t:t + 1], accum_out=den[:, k % 2, t:t + 1])
                    last.then_inc(p_mem, 1)
                elif name == "memC":
                    eng.wait_ge(pt_psum, pt + 1)
                    if mix:
                        eng.wait_ge(mix_psum, mix)
                    act(probsT[:, :, :].rearrange("p a b -> p (a b)")[:, 0:4 * P], ps[:, 5, :]).then_inc(pt_ready, 1)
                elif name == "conv":
                    eng.wait_ge(conv_acc, 4 * l + k + 1)
                    act(convt[:, k % 2, :], convy[:, k % 2, :], ACT.Tanh, scale=0.5).then_inc(conv_tanh, 1)
                elif name == "brow":
                    eng.wait_ge(em_in, l + 1)
                    act(em[:, :, :], fm[:, :, :], ACT.Exp, scale=-1.0).then_inc(em_ready, 1)
                elif name == "mrow":
                    eng.wait_ge(rows_read, 2 * l + 2)
                    for h in range(MH):
                        act(wml[:, h, 0:S], wml[:, h, 0:S], ACT.Exp, bias=bb[:, 0, h:h + 1])
                        last = act(wml[:, h, S:S + P], wml[:, h, S:S + P], ACT.Exp, bias=bb[:, 1, h:h + 1])
                    last.then_inc(wml_ready, 1)
                elif name == "dR":
                    eng.wait_ge(max_d, DHG * l + k + 1)
                    for t, cols in enumerate((slice(0, P), slice(P, 3 * P))):
                        last = act(probs[:, k % 2, :, cols], probs[:, k % 2, :, cols], ACT.Exp, scale=DD ** -0.5,
                                   bias=nb[:, k % 2, t:t + 1], accum_out=den[:, k % 2, t:t + 1])
                    last.then_inc(p_d, 1)
                elif name == "dT":
                    eng.wait_ge(pt_psum, pt + 1)
                    eng.wait_ge(mix_psum, mix)
                    act(probsT[:, :, :], ps[:, 5:8, 0:3 * P]).then_inc(pt_ready, 1)
                elif name == "ht":
                    _, _, dst, k0 = ht_src(k)
                    transposed_hi(a["tr"][k], ht_bank(k), dst[0][:, k0:k0 + 2, :].rearrange("p k s -> p (k s)"))

            for kind, a in plan:
                if "c" in a and a["c"] != NDC - 1:
                    split_hi(a["c"] + AHEAD)
                if kind == "split":
                    split_hi(a["m"])
                elif kind == "xt":
                    xt(a)
                    if a["n"] == 3 * L - 1:
                        split_hi(NDC - 1 + AHEAD)
                        for t in range(TT):
                            eng.wait_ge(normed, 2 * TT)
                            act(xnhi[t][:, :], xn[:, t, :]).then_inc(xn_hi, 1)
                elif kind == "merged":
                    for q in range(KT // 2):
                        transposed_hi(a["tr"] + q, 4 + q, xthi[:, 2 * q:2 * q + 2, :].rearrange("p k s -> p (k s)"))
                elif kind == "unit":
                    unit(a)
                elif kind == "outproj" and a["q"] == 1:
                    for t in range(TT):
                        eng.wait_ge(unit_dve, read_count(a["u"] + t))
                        mean_square(xn, t, a["h"]).then_inc(squares, 1)
                elif kind == "gate":
                    p = a["p"]
                    eng.wait_ge(chunk_used, a["c"] + 1)
                    if p >= 2:
                        eng.wait_ge(hid_done, p - 1)
                    act(sg[:, p % 2, :], ps[:, (2 * p) % 4, :], ACT.Silu).then_inc(silu_done, 1)
                elif kind == "up":
                    p = a["p"]
                    eng.wait_ge(hid_done, p + 1)
                    if p >= 2:
                        eng.wait_ge(chunk_used, chunk_of["down", p - 2] + 1)
                    act(hThi[:, p % 2, :], hh[:, p % 2, :]).then_inc(hid_hi, 1)

            def hidden_hi(r, e, j):
                eng.wait_ge(m_tp, e * NJ + (r * E * NJ + j + 1))
                act(hThi[:, j % 2, :], ps[:, 4 + j % 2, :]).then_inc(m_thi, 1)

            def gathered_hi(r, e):
                eng.wait_ge(m_gath, e + (r * E + 1))
                act(xehi[:, :, :].rearrange("p k s -> p (k s)"), ps[:, 2:4, :].rearrange("p a b -> p (a b)"))\
                    .then_inc(m_xehi, 1)

            def experts(r):
                for m in range(0 if r else AHEAD, MAHEAD):
                    split_hi_moe(r, 0, m)
                gathered_hi(r, 0)
                with eng.Fori(0, E) as e:
                    act(warm[:, :], ident[:, 0:1], ACT.Silu)
                    for k, (kind, j, part) in enumerate(moe_chunks):
                        if kind == "g" and part == 1:
                            eng.wait_ge(chunk_used, e * EC + (NDC + r * E * EC + k + 1))
                            if j >= 2:
                                eng.wait_ge(m_hid, e * NJ + (r * E * NJ + j - 1))
                            act(sg[:, j % 2, :], ps[:, 2 * (j % 2), :], ACT.Silu).then_inc(m_silu, 1)
                            if j:
                                hidden_hi(r, e, j - 1)
                        if kind == "u" and part == 1 and j == 1:
                            eng.wait_ge(m_putp, e + (r * E + 1))
                            act(put[:, :, :].rearrange("p t s -> p (t s)"), ps[:, 5, 0:TT * P]).then_inc(m_put, 1)
                        if k == EC - 4:
                            hidden_hi(r, e, NJ - 1)
                        if k == EC - 3:
                            with eng.If(e < E - 1):
                                gathered_hi(r, e + 1)
                        if k + MAHEAD < EC:
                            split_hi_moe(r, e, k + MAHEAD)
                        else:
                            with eng.If(e < E - 1):
                                split_hi_moe(r, e, k + MAHEAD)
                    eng.wait_ge(chunk_used, e * EC + (NDC + (r * E + 1) * EC))
                    eng.wait_ge(m_gs, e + (r * E + 1))
                    for h in range(2):
                        act(yhi[:, h * HC:(h + 1) * HC], ps[:, 6 + h, :], scale=gs[:, 0:1]).then_inc(m_yhi, 1)
                for i in range(4):
                    eng.wait_ge(m_added, (r + 1) * (E + 1) * 4 - 3 + i)
                    mean_square(junk, i % 2, i // 2).then_inc(m_squares, 1)

            eng.wait_ge(flag_ready, 1)
            over = eng.value_load(flag[0:1, 0:1], min_val=0, max_val=1)
            experts(0)
            with eng.If(over > 0):
                experts(1)

        @block.tensor
        def _(eng):
            def mm3(dst, a, b, first, last):
                eng.matmul(dst, a[0], b[0], start=first, stop=False)
                eng.matmul(dst, a[0], b[1], start=False, stop=False)
                return eng.matmul(dst, a[1], b[0], start=False, stop=last)

            def mm(dst, pairs):
                for i, (a, b) in enumerate(pairs):
                    last = eng.matmul(dst, a, b, start=i == 0, stop=i == len(pairs) - 1)
                return last

            def parts(pair, *index):
                return tuple(t[index] for t in pair)

            XT = (xthi, xtlo)

            def weights(c):
                kt, n_ = chunks[c][1:]
                return view(hi[c % HI], n_, kt), view(lo[c % RAW], n_, kt)

            def transposes(bank, src, ks):
                for i, k in enumerate(ks):
                    for t in range(TT):
                        last = eng.transpose(ps[:, bank, (i * TT + t) * P:(i * TT + t + 1) * P],
                                             src[:, t, k * P:(k + 1) * P], ident[:, :])
                last.then_inc(tr_psum, 1)

            def xt_part(a, first, k):
                if first and k % 2 == 0 and a.get("fresh") is not None:
                    eng.wait_ge(tr_lo, a["fresh"] + k // 2 + 1)

            def unit(a):
                c, u, l = a["c"], a["u"], a["l"]
                kt, n_ = chunks[c][1:]
                w = weights(c)
                wait_bank(eng, u)
                xT = (mthi, mtlo) if a["src"] == "mem" else XT
                if a["form"] == "F":
                    for f in range(n_ // P):
                        for k in range(kt):
                            xt_part(a, f == 0, k)
                            last = mm3(ps[:, u % 2, f * S:(f + 1) * S], parts(w, slice(None), k, slice(f * P, (f + 1) * P)),
                                       parts(xT, slice(None), k), k == 0, k == kt - 1)
                elif n_ <= 2 * MH:
                    w2 = narrow(c)
                    for t in range(TT):
                        o = t * 2 * n_
                        for k in range(kt):
                            xt_part(a, t == 0, k)
                            xk = parts(xT, slice(None), k, slice(t * P, (t + 1) * P))
                            both = w2[:, k, :, :].rearrange("p b n -> p (b n)")
                            if k == 0:
                                eng.matmul(ps[:, u % 2, o:o + 2 * n_], xk[0], both, start=True, stop=False)
                            last = eng.matmul(ps[:, u % 2, o:o + n_], xk[1], w2[:, k, 0, :], start=False, stop=False)
                            if k:
                                last = eng.matmul(ps[:, u % 2, o:o + 2 * n_], xk[0], both, start=False, stop=k == kt - 1)
                else:
                    for t in range(TT):
                        for k in range(kt):
                            xt_part(a, t == 0, k)
                            last = mm3(ps[:, u % 2, t * n_:(t + 1) * n_], parts(xT, slice(None), k, slice(t * P, (t + 1) * P)),
                                       parts(w, slice(None), k), k == 0, k == kt - 1)
                last.then_inc(chunk_used, 1)
                for name, k in a["ex"]:
                    extra(name, k, l, a)

            def extra(name, k, l, a):
                pt = slots_mem * l + k + (XH if name[0] == "d" else 0)
                mix = mixes * l + k + {"m": XH if name[:2] == "ml" else 0, "d": XH + MH}.get(name[0], 0)
                if name == "memA":
                    eng.wait_ge(unit_act, evac(l, "qx"))
                    if k >= 2:
                        eng.wait_ge(p_mem, XH * l + k - 1)
                    for t in range(TT):
                        last = mm(ps[:, 2 + k % 2, t * NM:(t + 1) * NM], [(qx[:, k, t * P:(t + 1) * P], kmT[:, k, :])])
                    last.then_inc(s_mem, 1)
                elif name == "memC":
                    eng.wait_ge(p_mem, XH * l + k + 1)
                    if pt:
                        eng.wait_ge(pt_ready, pt)
                    pv = probs[:, k % 2, 0:2, :].rearrange("p a b -> p (a b)")
                    for i in range(4):
                        last = eng.transpose(ps[:, 5, i * P:(i + 1) * P], pv[:, i * P:(i + 1) * P], ident[:, :])
                    last.then_inc(pt_psum, 1)
                elif name == "memE":
                    eng.wait_ge(pt_ready, pt + 1)
                    if mix:
                        eng.wait_ge(mix_read, mix)
                    tv = probsT[:, :, :].rearrange("p a b -> p (a b)")
                    for t in range(TT):
                        last = mm(ps[:, 4, t * P:(t + 1) * P],
                                  [(tv[:, (2 * t + m) * P:(2 * t + m + 1) * P], vm[:, m, k * XD:(k + 1) * XD])
                                   for m in range(2)])
                    last.then_inc(mix_psum, 1)
                elif name == "cum":
                    eng.wait_ge(logf, l + 1)
                    mm(ps[:, 7, 0:MH], [(upper[:, :], lf[:, 0, :])])
                    mm(ps[:, 7, MH:2 * MH], [(ones[:, :], lf[:, 0, :]), (upper[:, :], lf[:, 1, :])]).then_inc(cum_psum, 1)
                elif name in ("brow", "mrow"):
                    n_ = 2 * l + (name == "mrow")
                    eng.wait_ge(diag_ready, n_ + 1)
                    eng.wait_ge(pt_ready, slots_mem * l + XH)
                    if n_:
                        eng.wait_ge(rows_read, n_)
                    for t in range(TT):
                        last = mm(ps[:, 5 + t, :], [(ones[:, :], diag[:, t, :, :].rearrange("p h j -> p (h j)"))])
                    last.then_inc(rows_psum, 1)
                elif name == "mlA":
                    eng.wait_ge(conv_done, 4 * (l + 1))
                    if k >= 2:
                        eng.wait_ge(sw_ml, MH * l + k - 1)
                    mm(ps[:, 2 + k % 2, 0:S], [(qk[:, MH + k, 0:P], qk[:, k, :])])
                    mm(ps[:, 2 + k % 2, S:S + P], [(qk[:, MH + k, P:S], qk[:, k, P:S])]).then_inc(s_ml, 1)
                elif name == "mlE":
                    eng.wait_ge(sw_ml, MH * l + k + 1)
                    eng.wait_ge(unit_act, evac(l, "vml"))
                    eng.wait_ge(mix_read, mix)
                    sw = probs[:, k % 2, 0, :]
                    mm(ps[:, 4, 0:VA], [(sw[:, 0:P], vaug[:, 0, k, :])])
                    mm(ps[:, 4, VA:2 * VA], [(sw[:, P:S], vaug[:, 0, k, :]), (sw[:, S:S + P], vaug[:, 1, k, :])])\
                        .then_inc(mix_psum, 1)
                elif name in ("dS", "dR"):
                    o, tile = (k % 2) * DD, k // 2
                    if name == "dS":
                        eng.wait_ge(unit_act, evac(l, "kd"))
                        eng.wait_ge(sw_ml, MH * (l + 1))
                        if k:
                            eng.wait_ge(d_masked, DG * (DHG * l + k))
                    else:
                        eng.wait_ge(d_masked, DG * (DHG * l + k) + 1)
                    for g in ((0, 1) if name == "dS" else (2,)):
                        q_, k_ = qd[o:o + DD, 2 * g + tile, :], kd[o:o + DD, 2 * g + tile, :]
                        mm(ps[:, 2 + g % 2, 0:P], [(q_[:, 0:P], k_[:, 0:P])])
                        mm(ps[:, 2 + g % 2, P:3 * P], [(q_[:, P:S], k_)]).then_inc(s_d, 1)
                elif name == "dT":
                    eng.wait_ge(p_d, DHG * l + k + 1)
                    eng.wait_ge(pt_ready, pt)
                    if not k:
                        eng.wait_ge(rows_read, 2 * l + 2)
                    for b in range(3):
                        for g in range(DG):
                            last = eng.transpose(ps[:, 5 + b, g * P:(g + 1) * P],
                                                 probs[:, k % 2, g, b * P:(b + 1) * P], ident[:, :])
                    last.then_inc(pt_psum, 1)
                elif name == "dE":
                    eng.wait_ge(pt_ready, pt + 1)
                    eng.wait_ge(mix_read, mix)
                    v_ = [[vd[:, t, g * DHG * DD + k * DD:g * DHG * DD + (k + 1) * DD] for g in range(DG)] for t in range(TT)]
                    pT = [[probsT[:, b, g * P:(g + 1) * P] for g in range(DG)] for b in range(3)]
                    mm(ps[:, 4, 0:DD], [(pT[0][g], v_[0][g]) for g in range(DG)])
                    mm(ps[:, 4, DD:2 * DD], [(pT[1 + t][g], v_[t][g]) for t in range(TT) for g in range(DG)])\
                        .then_inc(mix_psum, 1)
                elif name == "ht":
                    src, ks, _, _ = ht_src(k)
                    if k == HT_ORDER[0]:
                        eng.wait_ge(pt_ready, slots_mem * (l + 1))
                    if k < 2:
                        eng.wait_ge(mix_read, mixes * l + XH)
                    elif k < 4:
                        eng.wait_ge(hm_ready, l + 1)
                    else:
                        eng.wait_ge(mix_read, mixes * (l + 1))
                    if HT_ORDER.index(k) >= 2:
                        eng.wait_ge(tr_lo, a["tr"][k] - 1)
                    transposes(ht_bank(k), src, ks)

            def keep_warm(n_, bank=3):
                for _ in range(n_):
                    eng.matmul(ps[:, bank, 0:P], ones[:, :], ones[:, :], start=True, stop=True)

            def normed_transposes(a):
                src, rd = (mem, rdm) if a["src"] == "mem" else (x, rdx)
                if a["n"] % 3 == 2:
                    keep_warm(16)
                eng.wait_ge(rstd_ready, a["rstd"])
                if a["src"] == "mem":
                    if a["n"]:
                        eng.wait_ge(mem_reloaded, 16 * (a["n"] // 3))
                    else:
                        for t in range(TT):
                            eng.wait_ge(mem_loaded[t], 16)
                if a["tr"]:
                    eng.wait_ge(tr_lo, a["tr"])
                if a["n"] == 4:
                    eng.wait_ge(y_read, 4)
                for q in range(KT // 2):
                    for i in range(2):
                        for t in range(TT):
                            last = eng.matmul(ps[:, 4 + q, (i * TT + t) * P:(i * TT + t + 1) * P],
                                              src[:, t, (2 * q + i) * P:(2 * q + i + 1) * P], rd[:, t, :],
                                              start=True, stop=True)
                    last.then_inc(tr_psum, 1)

            eng.wait_ge(ident_made, 1)
            keep_warm(8)
            eng.wait_ge(consts_loaded, 64)
            eng.transpose(ps[:, 3, 0:NROWS], cwn[:, :], ident[0:NROWS, 0:NROWS]).then_inc(cw_psum, 1)
            for kind, a in plan:
                l = a.get("l")
                if kind == "xt":
                    normed_transposes(a)
                elif kind == "merged":
                    eng.wait_ge(tr_lo, a["tr"])
                    for q in range(KT // 2):
                        eng.wait_ge(merged_ready, 4 * a["l"] + 2 * (q // 2 + 1))
                        transposes(4 + q, merged, (2 * q, 2 * q + 1))
                if "c" not in a:
                    continue
                c = a["c"]
                eng.wait_ge(lo_done, c + 1)
                w = weights(c)
                if kind == "unit":
                    unit(a)
                elif kind == "branch":
                    hT = (hmT, hdT, hxT)[a["b"]]
                    eng.wait_ge(tr_lo, tr_ht[l][HT_LAST[a["b"]]] + 1)
                    for i, h in enumerate(a["halves"]):
                        for t in range(TT):
                            u = a["u"] + TT * i + t
                            wait_bank(eng, u)
                            for k in range(a["kt"]):
                                last = mm3(ps[:, u % 2, :], parts(hT, slice(None), k, slice(t * P, (t + 1) * P)),
                                           parts(w, slice(None), k, slice(i * HC, (i + 1) * HC)), k == 0, k == a["kt"] - 1)
                            last.then_inc(chunk_used if product[u][0] is chunk_used else unit_done, 1)
                elif kind == "outproj":
                    for t in range(TT):
                        u = a["u"] + t
                        if a["q"] == 0:
                            wait_bank(eng, u)
                        for k in range(4):
                            if a["h"] == 0 and t == 0 and k % 2 == 0:
                                eng.wait_ge(tr_lo, tr_merged[l] + 2 * a["q"] + k // 2 + 1)
                            last = mm3(ps[:, u % 2, :], parts(XT, slice(None), 4 * a["q"] + k, slice(t * P, (t + 1) * P)),
                                       parts(w, slice(None), k), a["q"] == 0 and k == 0, a["q"] == 1 and k == 3)
                        if a["q"] == 1 and t == 0:
                            last.then_inc(unit_done, 1)
                    last.then_inc(chunk_used, 1)
                elif kind in ("gate", "up"):
                    p = a["p"]
                    if p >= 2:
                        eng.wait_ge(silu_done if kind == "gate" else hid_done, p - 1)
                    b = (2 * p + (kind == "up")) % 4
                    for f in range(2):
                        for k in range(KT):
                            xt_part(a, f == 0, k)
                            last = mm3(ps[:, b, f * S:(f + 1) * S], parts(w, slice(None), k, slice(f * P, (f + 1) * P)),
                                       parts(XT, slice(None), k), k == 0, k == KT - 1)
                    last.then_inc(chunk_used, 1)
                elif kind == "down":
                    p = a["p"]
                    eng.wait_ge(hid_lo, p + 1)
                    if p == 0:
                        eng.wait_ge(tr_lo, tr_norm[3] + KT // 2)
                    for f in range(2):
                        for t in range(TT):
                            hT = parts((hThi, hTlo), slice(None), p % 2, slice(f * S + t * P, f * S + (t + 1) * P))
                            for h in range(2):
                                last = mm3(ps[:, 4 + 2 * t + h, :], hT, parts(w, slice(None), f, slice(h * HC, (h + 1) * HC)),
                                           p == 0 and f == 0, p == NP_ - 1 and f == 1)
                    last.then_inc(chunk_used, 1)

            keep_warm(16)
            eng.wait_ge(route_sel, 1)
            mm(ps[:, 7, 0:E], [(upper_s[:, :], sel[:, 0, :])])
            mm(ps[:, 7, E:2 * E], [(ones[:, :], sel[:, 0, :]), (upper_s[:, :], sel[:, 1, :])])
            mm(ps[:, 7, 2 * E:3 * E], [(ones[:, :], sel[:, 0, :]), (ones[:, :], sel[:, 1, :])]).then_inc(route_pos, 1)

            def gather(r, e, first=False):
                if first:
                    keep_warm(12)
                eng.wait_ge(m_pick, e + (r * E + 1))
                if first:
                    eng.wait_ge(xn_lo, TT)
                for k in range(KT):
                    last = mm(ps[:, 2 + k // 4, (k % 4) * P:(k % 4 + 1) * P],
                              [(v[:, k * P:(k + 1) * P], pick[:, t, :]) for t in range(TT) for v in (xnhi[t], xnlo[:, t, :])])
                last.then_inc(m_gath, 1)

            def scatter(r, e):
                eng.wait_ge(m_put, e + (r * (E + 1) + 1))
                for i in range(4):
                    h, t = i // 2, i % 2
                    if t == 0:
                        eng.wait_ge(m_y, e * 2 + (r * (E + 1) * 2 + h + 1))
                    if i >= 2:
                        eng.wait_ge(m_added, e * 4 + (r * (E + 1) * 4 + i - 1))
                    mm(ps[:, 4 + i % 2, :], [(put[:, t, :], v[:, h * HC:(h + 1) * HC]) for v in (yhi, ylo)])\
                        .then_inc(m_scat, 1)

            def hidden_T(r, e, j):
                eng.wait_ge(m_hid, e * NJ + (r * E * NJ + j + 1))
                for i in range(4):
                    last = eng.transpose(ps[:, 4 + j % 2, i * P:(i + 1) * P], hh[:, j % 2, i * P:(i + 1) * P], ident[:, :])
                last.then_inc(m_tp, 1)

            def experts_all(r):
                gather(r, 0, first=True)
                keep_warm(10, bank=1)
                with eng.Fori(0, E) as e:
                    eng.wait_ge(m_xelo, e + (r * E + 1))
                    for k in range(EC):
                        expert_chunk(r, e, k)
                        if k == EC - 4:
                            eng.wait_ge(m_tlo, e * NJ + (r * E * NJ + NJ - 2))
                            hidden_T(r, e, NJ - 1)
                        if k == EC - 3:
                            with eng.If(e < E - 1):
                                gather(r, e + 1)
                scatter(r, E)

            def expert_chunk(r, e, k):
                kind, j, part = moe_chunks[k]
                eng.wait_ge(lo_done, e * EC + (NDC + r * E * EC + k + 1))
                if kind == "d":
                    w = view(hi_moe[k % MHI], D, 2), view(lo_moe[k % MRAW], D, 2)
                    if part == 0:
                        eng.wait_ge(m_tlo, e * NJ + (r * E * NJ + j + 1))
                    for i in range(2):
                        kk = 2 * part + i
                        hT = parts((hThi, hTlo), slice(None), j % 2, slice(kk * P, (kk + 1) * P))
                        for h in range(2):
                            last = mm3(ps[:, 6 + h, :], hT, parts(w, slice(None), i, slice(h * HC, (h + 1) * HC)),
                                       j == 0 and kk == 0, j == NJ - 1 and kk == 3)
                    last.then_inc(chunk_used, 1)
                    return
                w = view(hi_moe[k % MHI], HC, 4), view(lo_moe[k % MRAW], HC, 4)
                if part == 0 and j >= 2:
                    eng.wait_ge(m_silu if kind == "g" else m_hid, e * NJ + (r * E * NJ + j - 1))
                b = 2 * (j % 2) + (kind == "u")
                for i in range(4):
                    kk = 4 * part + i
                    last = mm3(ps[:, b, :], (xehi[:, kk, :], xelo[:, kk, :]), parts(w, slice(None), i), kk == 0, kk == KT - 1)
                last.then_inc(chunk_used, 1)
                if part == 0:
                    return
                if kind == "g" and j == 0:
                    scatter(r, e)
                elif kind == "g":
                    if j == 1:
                        eng.wait_ge(m_added, e * 4 + (r * (E + 1) * 4 + 3))
                    elif j == 2:
                        eng.wait_ge(m_put, e + (r * (E + 1) + 2))
                        eng.wait_ge(m_gs, e + (r * E + 1))
                    else:
                        eng.wait_ge(m_tlo, e * NJ + (r * E * NJ + j - 2))
                    hidden_T(r, e, j - 1)
                elif j == 1:
                    eng.wait_ge(m_added, e * 4 + (r * (E + 1) * 4 + 4))
                    for t in range(TT):
                        mm(ps[:, 5, t * P:(t + 1) * P], [(pick[:, t, :], identr[:, :])])
                    mm(ps[:, 5, TT * P:TT * P + 2], [(pick[:, t, :], curg[:, t, :]) for t in range(TT)]).then_inc(m_putp, 1)

            eng.wait_ge(flag_ready, 1)
            over = eng.value_load(flag[0:1, 0:1], min_val=0, max_val=1)
            experts_all(0)
            with eng.If(over > 0):
                experts_all(1)

        @block.vector
        def _(eng):
            n = [0]

            def link(ins):
                n[0] += 1
                ins.then_inc(dve_seq, 1)
                eng.wait_ge(dve_seq, n[0])

            tt, ts, stt = eng.tensor_tensor, eng.tensor_scalar, eng.scalar_tensor_tensor

            def split_lo(c):
                if c >= NDC:
                    split_lo_moe(0, 0, c - NDC)
                    return
                kt, n_ = chunks[c][1:]
                eng.wait_ge(hi_done, c + 1)
                if n_ <= 2 * MH:
                    tt(narrow(c)[:, :, 1, :], view(raw[c % RAW], n_, kt), narrow(c)[:, :, 0, :].bitcast(f32),
                       ALU.subtract).then_inc(lo_done, 1)
                    return
                tt(lo[c % RAW][:, 0:kt * n_], raw[c % RAW][:, 0:kt * n_], hi[c % HI][:, 0:kt * n_].bitcast(f32),
                   ALU.subtract).then_inc(lo_done, 1)

            def split_lo_moe(r, e, m):
                eng.wait_ge(hi_done, e * EC + (NDC + r * E * EC + m + 1))
                tt(lo_moe[m % MRAW][:, :], raw_moe[m % MRAW][:, :], hi_moe[m % MHI][:, :].bitcast(f32), ALU.subtract)\
                    .then_inc(lo_done, 1)

            def transposed_lo(tr, bank, dst, hi_):
                eng.wait_ge(tr_hi, tr + 1)
                tt(dst, ps[:, bank, :], hi_.bitcast(f32), ALU.subtract).then_inc(tr_lo, 1)

            def rsqrt(r, v, t, ti):
                link(ts(ti, v.bitcast(i32), 1, None, ALU.logical_shift_right))
                link(ts(r.bitcast(i32), ti, -1.0, float(0x5F3759DF), ALU.mult, ALU.add))
                for _ in range(3):
                    link(tt(t, r, r, ALU.mult))
                    link(stt(t, t, -0.5, v, ALU.mult, ALU.mult))
                    link(stt(r, t, 1.5, r, ALU.add, ALU.mult))

            def mean_square(src, t, h):
                cols = slice(h * HC, (h + 1) * HC)
                return eng.tensor_tensor_reduce(xn[:, t, cols], src[:, t, cols], src[:, t, cols], 1.0 / D, 0.0,
                                                ALU.mult, ALU.add, ss[:, t, h:h + 1])

            def row_scale():
                link(stt(var[:, :], ss[:, :, 0], EPS, ss[:, :, 1], ALU.add, ALU.add))
                rsqrt(rstd[:, :], var[:, :], nt[:, :], nti[:, :])

            def stats(n_):
                src, rd = (mem, rdm) if n_ == 0 else (x, rdx)
                if n_ % 3 != 2:
                    for t in range(TT):
                        if n_ < 2:
                            eng.wait_ge((x_loaded if n_ else mem_loaded)[t], 16)
                        for h in range(2):
                            last = mean_square(src, t, h)
                    link(last)
                else:
                    eng.wait_ge(squares, 4 * (n_ // 3 + 1))
                row_scale()
                if n_ == 0:
                    eng.wait_ge(ident_made, 1)
                for t in range(TT):
                    last = ts(rd[:, t, :], ident[:, :], rstd[:, t:t + 1], None, ALU.mult)
                last.then_inc(rstd_ready, 1)

            def xt(a):
                hi_, lo_ = (mthi, mtlo) if a["src"] == "mem" else (xthi, xtlo)
                for q in range(KT // 2):
                    eng.wait_ge(tr_hi, a["tr"] + q + 1)
                    for i in range(2):
                        k = 2 * q + i
                        last = stt(lo_[:, k, :], ps[:, 4 + q, i * S:(i + 1) * S], gain_col(a["n"], k), hi_[:, k, :].bitcast(f32),
                                   ALU.mult, ALU.subtract)
                    last.then_inc(tr_lo, 1)

            def normed_rows(loaded, gain_):
                eng.wait_ge(loaded, 16)
                for t in range(TT):
                    for cols in (slice(0, HC), slice(HC, D)):
                        stt(xn[:, t, cols], x[:, t, cols], rstd[:, t:t + 1], gain_[:, cols], ALU.mult, ALU.mult)\
                            .then_inc(normed, 1)

            def conv(l, ci, u):
                eng.wait_ge(unit_act, read_count(u))
                for j in (3, 2, 1, 0):
                    for f in range(2):
                        y = convy[:, ci % 2, f * S:(f + 1) * S]
                        xx = convx[:, ci % 2, f, j:j + S]
                        row = (l * 4 + j) * 8 + 2 * ci + f
                        if j == 3:
                            last = ts(y, xx, cw[:, row:row + 1], None, ALU.mult)
                        else:
                            last = stt(y, xx, cw[:, row:row + 1], y, ALU.mult, ALU.add)
                    if j:
                        link(last)
                last.then_inc(conv_acc, 1)

            def diags(src):
                for t in range(TT):
                    for h in range(MH):
                        last = ts(diag[:, t, h, :], ident[:, :], src[:, t, h:h + 1], None, ALU.mult)
                last.then_inc(diag_ready, 1)

            def unit(a):
                (kind, i), l, u = a["to"], a["l"], a["u"]
                cols = slice(i * UC, (i + 1) * UC)
                if kind == "om":
                    eng.wait_ge(unit_act, read_count(u))
                    link(ts(so[:, :, cols], so[:, :, cols], 0.5, 0.5, ALU.mult, ALU.add))
                elif kind == "g":
                    eng.wait_ge(unit_act, read_count(u))
                    v = gates[:, i // 4, :, (i % 4) * UC:(i % 4 + 1) * UC]
                    ts(v, v, 0.5, 0.5, ALU.mult, ALU.add).then_inc(gate_done, 1)
                elif kind == "if":
                    eng.wait_ge(unit_act, read_count(u))
                    link(eng.memset(convx[:, :, :, 0:3], 0.0))
                    if l == 0:
                        eng.wait_ge(bif_loaded, 16)
                    link(tt(ifr[:, :, :], two[:, :, 0:E], two[:, :, E:2 * E], ALU.add))
                    link(tt(ifb[:, :, :], ifr[:, :, :], bif[:, l:l + 1, :].broadcast_to([P, TT, 2 * MH]), ALU.add))
                    f_ = ifb[:, :, MH:2 * MH]
                    stt(nab[:, :, :], f_, -1.0, f_, ALU.mult, ALU.min).then_inc(if_neg, 1)
                    eng.wait_ge(if_ln, l + 1)
                    stt(lf[:, :, :], f_, 0.0, ef[:, :, :], ALU.min, ALU.subtract).then_inc(logf, 1)
                elif kind == "route":
                    route(u)
                for name, k in a["ex"]:
                    extra(name, k, l, a)

            def extra(name, k, l, a):
                mix = mixes * l + k + {"m": XH if name[:2] == "ml" else 0, "d": XH + MH}.get(name[0], 0)
                if name == "cacc":
                    conv(l, k, a["u"])
                elif name == "memA":
                    eng.wait_ge(s_mem, XH * l + k + 1)
                    link(eng.tensor_reduce(mx[:, k % 2, :], ps[:, 2 + k % 2, :].rearrange("p (t n) -> p t n", t=TT), AX.X, ALU.max))
                    ts(nb[:, k % 2, :], mx[:, k % 2, :], -(XD ** -0.5), None, ALU.mult).then_inc(max_mem, 1)
                elif name in ("memE", "dE"):
                    eng.wait_ge(mix_psum, mix + 1)
                    link(eng.reciprocal(rec[:, :], den[:, k % 2, :]))
                    dst, w_ = (hx, XD) if name == "memE" else (hd, DD)
                    for t in range(TT):
                        last = ts(dst[:, t, k * w_:(k + 1) * w_], ps[:, 4, t * w_:(t + 1) * w_], rec[:, t:t + 1], None, ALU.mult)
                    last.then_inc(mix_read, 1)
                elif name == "conv":
                    eng.wait_ge(conv_tanh, 4 * l + k + 1)
                    link(ts(convt[:, k % 2, :], convt[:, k % 2, :], 0.5, 0.5, ALU.mult, ALU.add))
                    tt(qk[:, 2 * k:2 * k + 2, :].rearrange("p f s -> p (f s)"), convy[:, k % 2, :], convt[:, k % 2, :],
                       ALU.mult).then_inc(conv_done, 1)
                elif name == "cum":
                    eng.wait_ge(cum_psum, l + 1)
                    link(eng.tensor_copy(cumf[:, :, :].rearrange("p t h -> p (t h)"), ps[:, 7, 0:TT * MH]))
                    link(tt(bb[:, :, :], ifb[:, :, 0:MH], cumf[:, :, :], ALU.subtract))
                    diags(bb)
                elif name == "brow":
                    eng.wait_ge(rows_psum, 2 * l + 1)
                    heads = [ps[:, 5 + t, :].rearrange("p (h j) -> p h j", h=MH) for t in range(TT)]
                    cm = dmask[:, 0:1, 0:P].broadcast_to([P, MH, P])
                    tt(wml[:, :, 0:P], heads[0], cm, ALU.add)
                    link(tt(wml[:, :, P:2 * P], heads[1], cm, ALU.add))
                    eng.tensor_reduce(m2[:, 1, :], heads[0], AX.X, ALU.max).then_inc(rows_read, 1)
                    eng.tensor_reduce(mm_[:, 0, :], wml[:, :, 0:P], AX.X, ALU.max)
                    link(eng.tensor_reduce(m2[:, 0, :], wml[:, :, P:2 * P], AX.X, ALU.max))
                    link(tt(mm_[:, 1, :], m2[:, 0, :], m2[:, 1, :], ALU.max))
                    tt(fm[:, :, :], cumf[:, :, :], mm_[:, :, :], ALU.add).then_inc(em_in, 1)
                    link(ts(ngm[:, :, :], mm_[:, :, :], -1.0, None, ALU.mult))
                    diags(ngm)
                elif name == "mrow":
                    eng.wait_ge(rows_psum, 2 * l + 2)
                    heads = [ps[:, 5 + t, :].rearrange("p (h j) -> p h j", h=MH) for t in range(TT)]
                    cm = maskT[:, :].unsqueeze(1).broadcast_to([P, MH, P])
                    tt(wml[:, :, 0:P], heads[0], cm, ALU.add)
                    eng.tensor_copy(wml[:, :, P:2 * P], heads[1])
                    tt(wml[:, :, 2 * P:3 * P], heads[1], cm, ALU.add).then_inc(rows_read, 1)
                elif name == "mlA":
                    eng.wait_ge(s_ml, MH * l + k + 1)
                    eng.wait_ge(wml_ready, l + 1)
                    stt(probs[:, k % 2, 0, :], ps[:, 2 + k % 2, 0:3 * P], MD ** -0.5, wml[:, k, :], ALU.mult, ALU.mult)\
                        .then_inc(sw_ml, 1)
                elif name == "mlE":
                    eng.wait_ge(mix_psum, mix + 1)
                    eng.wait_ge(em_ready, l + 1)
                    link(eng.tensor_copy(dn[:, :], ps[:, 4, MD:2 * VA:VA]))
                    link(stt(dn[:, :], dn[:, :], -1.0, dn[:, :], ALU.mult, ALU.max))
                    link(tt(dn[:, :], dn[:, :], em[:, :, k], ALU.max))
                    link(eng.reciprocal(rec[:, :], dn[:, :]))
                    for t in range(TT):
                        last = ts(hraw[:, t, k, :], ps[:, 4, t * VA:t * VA + MD], rec[:, t:t + 1], None, ALU.mult)
                    last.then_inc(mix_read, 1)
                    eng.wait_ge(mix_read, mix + 1)
                    for t in range(TT):
                        link(eng.bn_stats(st[:, :], hraw[:, t, k, :]))
                        link(eng.bn_aggr(mv[:, t * MH + k, :], st[:, :]))
                elif name == "mlF":
                    link(ts(v8[:, :], mv[:, :, 1], EPS, None, ALU.add))
                    rsqrt(r8[:, :], v8[:, :], n8[:, :], ni8[:, :])
                    eng.wait_ge(mln_loaded, 16 * (l + 1))
                    for t in range(TT):
                        for h in range(MH):
                            i = t * MH + h
                            last = ts(hm[:, t, h * MD:(h + 1) * MD], hraw[:, t, h, :], mv[:, i, 0:1], r8[:, i:i + 1],
                                      ALU.subtract, ALU.mult)
                    link(last)
                    link(tt(hm[:, :, :], hm[:, :, :], mln[:, :].unsqueeze(1).broadcast_to([P, TT, MW]), ALU.mult))
                    tt(hm[:, :, :], hm[:, :, :], so[:, :, :], ALU.mult).then_inc(hm_ready, 1)
                elif name in ("dS", "dR"):
                    eng.wait_ge(consts_made, 2)
                    for g in ((0, 1) if name == "dS" else (2,)):
                        eng.wait_ge(s_d, DG * (DHG * l + k) + g + 1)
                        tt(probs[:, k % 2, g, :], ps[:, 2 + g % 2, 0:3 * P], dmask[:, g, :], ALU.add).then_inc(d_masked, 1)
                    if name == "dR":
                        eng.wait_ge(d_masked, DG * (DHG * l + k + 1))
                        eng.tensor_reduce(mx[:, k % 2, 0:1], probs[:, k % 2, :, 0:P], AX.XY, ALU.max)
                        link(eng.tensor_reduce(mx[:, k % 2, 1:2], probs[:, k % 2, :, P:3 * P], AX.XY, ALU.max))
                        ts(nb[:, k % 2, :], mx[:, k % 2, :], -(DD ** -0.5), None, ALU.mult).then_inc(max_d, 1)
                elif name == "ht":
                    _, _, dst, k0 = ht_src(k)
                    transposed_lo(a["tr"][k], ht_bank(k), *(dst[i][:, k0:k0 + 2, :].rearrange("p k s -> p (k s)") for i in (1, 0)))

            def route(u):
                for t in range(TT):
                    eng.wait_ge(xn_hi, t + 1)
                    tt(xnlo[:, t, :], xn[:, t, :], xnhi[t][:, :].bitcast(f32), ALU.subtract).then_inc(xn_lo, 1)
                eng.wait_ge(unit_act, read_count(u))
                link(tt(lg[:, :, :], two[:, :, 0:E], two[:, :, E:2 * E], ALU.add))
                others = lg[:, :, :].unsqueeze(2).broadcast_to([P, TT, E, E])
                own = lg[:, :, :].unsqueeze(3).broadcast_to([P, TT, E, E])
                eng.tensor_reduce(m1[:, :], lg[:, :, :], AX.X, ALU.max)
                tt(gt[:, :, :, :], others, own, ALU.is_gt)
                link(tt(eq[:, :, :, :], others, own, ALU.is_equal))
                link(tt(eq[:, :, :, :], eq[:, :, :, :], lt[:, :, :].unsqueeze(1).broadcast_to([P, TT, E, E]), ALU.mult))
                tt(eg[:, :, :], lg[:, :, :], m1[:, :].unsqueeze(2).broadcast_to([P, TT, E]), ALU.subtract)
                link(tt(gt[:, :, :, :], gt[:, :, :, :], eq[:, :, :, :], ALU.add))
                link(eng.tensor_reduce(cnt[:, :, :], gt[:, :, :, :], AX.X, ALU.add))
                ts(sel[:, :, :], cnt[:, :, :], 1.5, None, ALU.is_lt).then_inc(route_sel, 1)
                eng.wait_ge(route_sel, 1)
                eng.wait_ge(route_exp, 1)
                link(tt(eg[:, :, :], eg[:, :, :], sel[:, :, :], ALU.mult))
                link(eng.tensor_reduce(dg[:, :], eg[:, :, :], AX.X, ALU.add))
                link(eng.reciprocal(dg[:, :], dg[:, :]))
                tt(geg[:, :, :], eg[:, :, :], dg[:, :].unsqueeze(2).broadcast_to([P, TT, E]), ALU.mult)
                link(ts(cnt[:, :, :], sel[:, :, :], -1e6, 1e6, ALU.mult, ALU.add))
                eng.wait_ge(route_pos, 1)
                link(tt(posm[:, :, :], ps[:, 7, 0:TT * E].rearrange("p (t e) -> p t e", t=TT), cnt[:, :, :], ALU.add))
                by_e = [v[:, :, :].rearrange("p t e -> p e t") for v in (posm, geg)]
                eng.tensor_copy(tab[:, 0:E, :], by_e[0])
                link(eng.tensor_copy(gtab[:, 0:E, :, 0], by_e[1]))
                link(tt(gtab[:, 0:E, :, 1], by_e[1], gtab[:, 0:E, :, 0].bitcast(f32), ALU.subtract))
                link(eng.tensor_reduce(tmx[:, :], ps[:, 7, 2 * E:3 * E], AX.X, ALU.max))
                ts(flag[:, :], tmx[:, :], float(P) + 0.5, None, ALU.is_gt).then_inc(flag_ready, 1)

            for kind, a in plan:
                l = a.get("l")
                if "c" in a and a.get("pos") != 0:
                    split_lo(a["c"] + AHEAD)
                if kind == "split":
                    split_lo(a["m"])
                elif kind == "stats":
                    stats(a["n"])
                    if a["n"] == 0:
                        eng.wait_ge(cw_psum, 1)
                        eng.tensor_copy(cw[:, :], ps[:, 3, 0:NROWS]).then_inc(cw_ready, 1)
                        eng.wait_ge(cw_ready, 1)
                    if a["n"] == 1:
                        link(eng.tensor_copy(identr[:, :], ident[:, :]))
                        eng.wait_ge(consts_made, 1)
                        for g, dil in enumerate((4, 16)):
                            link(ts(diffm[:, g, :], diff[:, :], dil - 1, None, ALU.bitwise_and))
                            link(eng.tensor_copy(resid[:, g, :], diffm[:, g, :]))
                            link(ts(resid[:, g, :], resid[:, g, :], 0.5, NEG, ALU.is_gt, ALU.mult))
                        eng.memset(mx[:, :, :], 0.0).then_inc(masks_made, 1)
                elif kind == "xt":
                    xt(a)
                    if a["n"] == 3 * L - 1:
                        normed_rows(gain_loaded, gain)
                elif kind == "merged":
                    for q in range(KT // 2):
                        transposed_lo(a["tr"] + q, 4 + q, *(t[:, 2 * q:2 * q + 2, :].rearrange("p k s -> p (k s)")
                                                            for t in (xtlo, xthi)))
                elif kind == "unit":
                    unit(a)
                elif kind == "branch":
                    b = a["b"]
                    if a["pos"] == 0:
                        eng.wait_ge(gate_done, 12 * (l + 1))
                        eng.wait_ge(tr_psum, tr_merged[l])
                    for i, h in enumerate(a["halves"]):
                        for t in range(TT):
                            u = a["u"] + TT * i + t
                            cols = slice(h * HC, (h + 1) * HC)
                            g_ = gates[:, b, t, cols]
                            eng.wait_ge(*product[u])
                            dst = merged[:, t, cols] if a["pos"] == 0 else g_
                            tt(dst, ps[:, u % 2, :], g_, ALU.mult).then_inc(unit_dve, 1)
                            eng.wait_ge(unit_dve, read_count(u))
                            if a["pos"]:
                                last = tt(merged[:, t, cols], merged[:, t, cols], g_, ALU.add)
                                if a["pos"] == 2:
                                    last.then_inc(merged_ready, 1)
                                else:
                                    link(last)
                            if a["pos"] == 0 and i == 0 and t == TT - 1:
                                split_lo(a["c"] + AHEAD)
                elif kind == "outproj" and a["q"] == 1:
                    for t in range(TT):
                        u = a["u"] + t
                        eng.wait_ge(*product[u])
                        cols = slice(a["h"] * HC, (a["h"] + 1) * HC)
                        tt(x[:, t, cols], ps[:, u % 2, :], x[:, t, cols], ALU.add).then_inc(unit_dve, 1)
                        eng.wait_ge(unit_dve, read_count(u))
                elif kind == "up":
                    p = a["p"]
                    eng.wait_ge(chunk_used, a["c"] + 1)
                    eng.wait_ge(silu_done, p + 1)
                    tt(hh[:, p % 2, :], ps[:, (2 * p + 1) % 4, :], sg[:, p % 2, :], ALU.mult).then_inc(hid_done, 1)
                    eng.wait_ge(hid_done, p + 1)
                    eng.wait_ge(hid_hi, p + 1)
                    tt(hTlo[:, p % 2, :], hh[:, p % 2, :], hThi[:, p % 2, :].bitcast(f32), ALU.subtract).then_inc(hid_lo, 1)
                elif kind == "ffn_end":
                    eng.wait_ge(chunk_used, chunk_of["down", NP_ - 1] + 1)
                    for t in range(TT):
                        for h in range(2):
                            cols = slice(h * HC, (h + 1) * HC)
                            tt(x[:, t, cols], ps[:, 4 + 2 * t + h, :], x[:, t, cols], ALU.add).then_inc(y_read, 1)
                    eng.wait_ge(y_read, 4)

            def picks(r, e):
                eng.tensor_copy(curg[:, :, :].unsqueeze(1), gtab[:, bass.ds(e, 1), :, :])
                eng.tensor_copy(cur[:, :].unsqueeze(1), tab[:, bass.ds(e, 1), :]).then_inc(m_cur, 1)
                eng.wait_ge(m_cur, e + (r * E + 1))
                for t in range(TT):
                    last = ts(pick[:, t, :], slots[:, r, :], cur[:, t:t + 1], None, ALU.is_equal)
                last.then_inc(m_pick, 1)

            def gathered_lo(r, e):
                eng.wait_ge(m_xehi, e + (r * E + 1))
                tt(xelo[:, :, :].rearrange("p k s -> p (k s)"), ps[:, 2:4, :].rearrange("p a b -> p (a b)"),
                   xehi[:, :, :].rearrange("p k s -> p (k s)").bitcast(f32), ALU.subtract).then_inc(m_xelo, 1)

            def hidden_lo(r, e, j):
                eng.wait_ge(m_thi, e * NJ + (r * E * NJ + j + 1))
                tt(hTlo[:, j % 2, :], ps[:, 4 + j % 2, :], hThi[:, j % 2, :].bitcast(f32), ALU.subtract).then_inc(m_tlo, 1)

            def scattered(r, e):
                for i in range(4):
                    h, t = i // 2, i % 2
                    eng.wait_ge(m_scat, e * 4 + (r * (E + 1) * 4 + i + 1))
                    cols = slice(h * HC, (h + 1) * HC)
                    tt(x[:, t, cols], ps[:, 4 + i % 2, :], x[:, t, cols], ALU.add).then_inc(m_added, 1)

            def experts(r):
                if r:
                    eng.memset(ylo[:, :].bitcast(f32), 0.0).then_inc(m_y, 2)
                    eng.memset(put[:, :, :].bitcast(f32), 0.0).then_inc(m_put, 1)
                picks(r, 0)
                for m in range(0 if r else AHEAD, MAHEAD):
                    split_lo_moe(r, 0, m)
                gathered_lo(r, 0)
                with eng.Fori(0, E) as e:
                    for k, (kind, j, part) in enumerate(moe_chunks):
                        if kind == "g" and part == 1:
                            if j == 0:
                                scattered(r, e)
                            else:
                                hidden_lo(r, e, j - 1)
                            if j == 3:
                                with eng.If(e < E - 1):
                                    picks(r, e + 1)
                        if kind == "u" and part == 1:
                            eng.wait_ge(chunk_used, e * EC + (NDC + r * E * EC + k + 1))
                            eng.wait_ge(m_silu, e * NJ + (r * E * NJ + j + 1))
                            tt(hh[:, j % 2, :], ps[:, 2 * (j % 2) + 1, :], sg[:, j % 2, :], ALU.mult).then_inc(m_hid, 1)
                        if kind == "d" and part == 0 and j == 0:
                            eng.wait_ge(m_putp, e + (r * E + 1))
                            eng.tensor_copy(gs2[:, :], ps[:, 5, TT * P:TT * P + 2]).then_inc(m_gsp, 1)
                            eng.wait_ge(m_gsp, e + (r * E + 1))
                            tt(gs[:, :], gs2[:, 0:1], gs2[:, 1:2], ALU.add).then_inc(m_gs, 1)
                        if k == EC - 4:
                            hidden_lo(r, e, NJ - 1)
                        if k == EC - 3:
                            with eng.If(e < E - 1):
                                gathered_lo(r, e + 1)
                        if k + MAHEAD < EC:
                            split_lo_moe(r, e, k + MAHEAD)
                        else:
                            with eng.If(e < E - 1):
                                split_lo_moe(r, e, k + MAHEAD)
                    for h in range(2):
                        cols = slice(h * HC, (h + 1) * HC)
                        eng.wait_ge(m_yhi, e * 2 + (r * E * 2 + h + 1))
                        stt(ylo[:, cols], ps[:, 6 + h, :], gs[:, 0:1], yhi[:, cols].bitcast(f32),
                            ALU.mult, ALU.subtract).then_inc(m_y, 1)
                scattered(r, E)
                eng.wait_ge(m_squares, 4 * (r + 1))

            eng.wait_ge(flag_ready, 1)
            over = eng.value_load(flag[0:1, 0:1], min_val=0, max_val=1)
            experts(0)
            with eng.If(over > 0):
                experts(1)
            row_scale()
            normed_rows(gain_f_loaded, gain_f)


_INS = ['x', 'mem', 'norm_mix', 'w_in', 'conv_qk', 'b_gate_if', 'mlstm_norm', 'norm_mem', 'w_mem_kv', 'w_br_m', 'w_br_d',
        'w_br_x', 'w_out', 'norm_ffn', 'ffn_w_gate', 'ffn_w_up', 'ffn_w_down', 'moe_router', 'moe_w_gate', 'moe_w_up',
        'moe_w_down', 'norm_final']


def kernel(**inputs):
    import numpy as _np
    import concourse.bacc as _bacc
    from concourse import mybir as _mybir
    from concourse.bass_utils import run_bass_kernel_spmd as _run

    nc = _bacc.Bacc("TRN2", target_bir_lowering=False, num_devices=1)
    arrays, args = {}, []
    for name in _INS:
        a = _np.ascontiguousarray(inputs[name])
        arrays[f"in_{name}_dram"] = a
        args.append(nc.dram_tensor(f"in_{name}_dram", a.shape, _mybir.dt.from_np(a.dtype), kind="ExternalInput").ap())
    shape = arrays["in_x_dram"].shape
    args.append(nc.dram_tensor("out_0_dram", shape, _mybir.dt.float32, kind="ExternalOutput").ap())
    hybrid_trunk(nc, *args)
    r = _run(nc, [arrays], core_ids=[0])
    return r.results[0]["out_0_dram"]
```
